# Optimizing a Trainium2 kernel written in Bass

```python
import jax, jax.numpy as jnp
from jax import lax
import numpy as np

D_MODEL = 1024
BATCH = 1
SEQ = 512
DEPTH = 2

HEAD_DIM = 64
D_RNN = D_MODEL // 2
H_RNN = D_RNN // HEAD_DIM
RNN_BLOCK = D_RNN // H_RNN
CONV_W = 4
RG_C = 8.0
H_FOX = (D_MODEL // 2) // HEAD_DIM
FOX_W = H_FOX * HEAD_DIM
H_SB = D_MODEL // HEAD_DIM
SB_W = H_SB * HEAD_DIM
D_FF = 11 * D_MODEL // 4
Q_BLOCK = 128
RMS_EPS = 1e-6
N_EVEN = (DEPTH + 1) // 2
N_ODD = DEPTH // 2
HY_IN = 2 * D_RNN + 3 * FOX_W + H_FOX
HY_MIX = D_RNN + FOX_W


def _rmsnorm(x, g):
    x32 = x.astype(jnp.float32)
    y = x32 * lax.rsqrt(jnp.mean(x32 * x32, axis=-1, keepdims=True) + RMS_EPS)
    return (y * g.astype(jnp.float32)).astype(x.dtype)

def _swiglu(h, w_in, w_out):
    a, b = jnp.split(h @ w_in, 2, axis=-1)
    return (jax.nn.silu(a) * b) @ w_out

def _lin_combine(left, right):
    a1, b1 = left
    a2, b2 = right
    return a1 * a2, a2 * b1 + b2

def _rglru_branch(u, gate, conv_w, conv_b, gate_w, gate_b, lam):
    B, S, _ = u.shape
    up = jnp.pad(u, ((0, 0), (CONV_W - 1, 0), (0, 0)))
    xc = conv_b + sum(conv_w[j] * up[:, j:j + S] for j in range(CONV_W))
    xh = xc.reshape(B, S, H_RNN, RNN_BLOCK)
    g = jnp.einsum('bshi,ghij->gbshj', xh, gate_w).reshape(2, B, S, D_RNN) + gate_b[:, None, None, :]
    r = jax.nn.sigmoid(g[0].astype(jnp.float32))
    i = jax.nn.sigmoid(g[1].astype(jnp.float32))
    log_a = -RG_C * r * jax.nn.softplus(-lam.astype(jnp.float32))
    a = jnp.exp(log_a)
    b = jnp.sqrt(-jnp.expm1(2.0 * log_a)) * (i * xc.astype(jnp.float32))
    _, h = lax.associative_scan(_lin_combine, (a, b), axis=1)
    return h.astype(u.dtype) * jax.nn.gelu(gate)

def _to_query_blocks(q):
    B, H, S, d = q.shape
    return q.reshape(B, H, S // Q_BLOCK, Q_BLOCK, d).transpose(2, 0, 1, 3, 4)

def _from_query_blocks(o):
    nb, B, H, QB, d = o.shape
    return o.transpose(1, 0, 3, 2, 4).reshape(B, nb * QB, H * d)

def _fox_attention(q, k, v, logf):
    B, H, S, d = q.shape
    c = jnp.cumsum(logf, axis=-1)
    nb = S // Q_BLOCK
    qb = _to_query_blocks(q)
    cb = c.reshape(B, H, nb, Q_BLOCK).transpose(2, 0, 1, 3)
    kpos = jnp.arange(S)
    scale = d ** -0.5

    def block(args):
        qi, ci, bi = args
        qpos = bi * Q_BLOCK + jnp.arange(Q_BLOCK)
        s = jnp.einsum('bhqd,bhkd->bhqk', qi, k).astype(jnp.float32) * scale
        s = s + ci[..., None] - c[:, :, None, :]
        s = jnp.where(kpos[None, :] <= qpos[:, None], s, -jnp.inf)
        p = jax.nn.softmax(s, axis=-1)
        return jnp.einsum('bhqk,bhkd->bhqd', p.astype(v.dtype), v)

    return _from_query_blocks(lax.map(block, (qb, cb, jnp.arange(nb))))

def _stick_breaking_attention(q, k, v):
    B, H, S, d = q.shape
    nb = S // Q_BLOCK
    qb = _to_query_blocks(q)
    kpos = jnp.arange(S)
    scale = d ** -0.5

    def block(args):
        qi, bi = args
        qpos = bi * Q_BLOCK + jnp.arange(Q_BLOCK)
        mask = kpos[None, :] < qpos[:, None]
        z = jnp.einsum('bhqd,bhkd->bhqk', qi, k).astype(jnp.float32) * scale
        log_nb = jnp.where(mask, jax.nn.log_sigmoid(-z), 0.0)
        after = lax.cumsum(log_nb, axis=3, reverse=True) - log_nb
        w = jnp.where(mask, jnp.exp(jax.nn.log_sigmoid(z) + after), 0.0)
        return jnp.einsum('bhqk,bhkd->bhqd', w.astype(v.dtype), v)

    return _from_query_blocks(lax.map(block, (qb, jnp.arange(nb))))

def _heads(t, n):
    B, S, _ = t.shape
    return t.reshape(B, S, n, HEAD_DIM)

def _hybrid_mixer(h, w_in, conv_w, conv_b, gate_w, gate_b, lam, f_b, qk_g, w_out):
    proj = h @ w_in
    o = 2 * D_RNN
    u, gate, q, k, v, f = jnp.split(proj, [D_RNN, o, o + FOX_W, o + 2 * FOX_W, o + 3 * FOX_W], axis=-1)
    y_rnn = _rglru_branch(u, gate, conv_w, conv_b, gate_w, gate_b, lam)
    qh = _rmsnorm(_heads(q, H_FOX), qk_g[0]).transpose(0, 2, 1, 3)
    kh = _rmsnorm(_heads(k, H_FOX), qk_g[1]).transpose(0, 2, 1, 3)
    vh = _heads(v, H_FOX).transpose(0, 2, 1, 3)
    logf = jax.nn.log_sigmoid((f + f_b).astype(jnp.float32)).transpose(0, 2, 1)
    y_fox = _fox_attention(qh, kh, vh, logf)
    return jnp.concatenate([y_rnn, y_fox], axis=-1) @ w_out

def _sb_mixer(h, w_qkv, w_out):
    q, k, v = jnp.split(h @ w_qkv, 3, axis=-1)
    qh, kh, vh = (_heads(t, H_SB).transpose(0, 2, 1, 3) for t in (q, k, v))
    return _stick_breaking_attention(qh, kh, vh) @ w_out

def first_inputs(seed: int = 0) -> dict:
    key = jax.random.key(seed)
    ks = jax.random.split(key, 20)
    f32 = jnp.float32

    def nrm(k, shape, fan_in):
        return jax.random.normal(k, shape, f32) * (fan_in ** -0.5)

    a0 = jax.random.uniform(ks[9], (N_EVEN, D_RNN), f32, 0.9, 0.999)
    return {
        "x": jax.random.normal(ks[0], (BATCH, SEQ, D_MODEL), f32),
        "ffn_norm": 1.0 + 0.05 * jax.random.normal(ks[1], (DEPTH, 2, D_MODEL), f32),
        "ffn_w_in": nrm(ks[2], (DEPTH, 2, D_MODEL, 2 * D_FF), D_MODEL),
        "ffn_w_out": nrm(ks[3], (DEPTH, 2, D_FF, D_MODEL), D_FF),
        "mix_norm": 1.0 + 0.05 * jax.random.normal(ks[4], (DEPTH, D_MODEL), f32),
        "hy_w_in": nrm(ks[5], (N_EVEN, D_MODEL, HY_IN), D_MODEL),
        "rg_conv_w": nrm(ks[6], (N_EVEN, CONV_W, D_RNN), CONV_W),
        "rg_conv_b": 0.02 * jax.random.normal(ks[7], (N_EVEN, D_RNN), f32),
        "rg_gate_w": nrm(ks[8], (N_EVEN, 2, H_RNN, RNN_BLOCK, RNN_BLOCK), RNN_BLOCK),
        "rg_gate_b": 0.02 * jax.random.normal(ks[10], (N_EVEN, 2, D_RNN), f32),
        "rg_lambda": jnp.log(a0) - jnp.log1p(-a0),
        "fox_fgate_b": jax.random.uniform(ks[11], (N_EVEN, H_FOX), f32, 1.0, 4.0),
        "fox_qk_norm": 1.0 + 0.05 * jax.random.normal(ks[12], (N_EVEN, 2, HEAD_DIM), f32),
        "hy_w_out": nrm(ks[13], (N_EVEN, HY_MIX, D_MODEL), HY_MIX),
        "sb_w_qkv": nrm(ks[14], (N_ODD, D_MODEL, 3 * SB_W), D_MODEL),
        "sb_w_out": nrm(ks[15], (N_ODD, SB_W, D_MODEL), SB_W),
    }

def first_block(x, ffn_norm, ffn_w_in, ffn_w_out, mix_norm, hy_w_in, rg_conv_w, rg_conv_b,
              rg_gate_w, rg_gate_b, rg_lambda, fox_fgate_b, fox_qk_norm, hy_w_out,
              sb_w_qkv, sb_w_out):
    for layer in range(DEPTH):
        x = x + 0.5 * _swiglu(_rmsnorm(x, ffn_norm[layer, 0]), ffn_w_in[layer, 0], ffn_w_out[layer, 0])
        h = _rmsnorm(x, mix_norm[layer])
        if layer % 2 == 0:
            e = layer // 2
            y = _hybrid_mixer(h, hy_w_in[e], rg_conv_w[e], rg_conv_b[e], rg_gate_w[e], rg_gate_b[e],
                              rg_lambda[e], fox_fgate_b[e], fox_qk_norm[e], hy_w_out[e])
        else:
            o = layer // 2
            y = _sb_mixer(h, sb_w_qkv[o], sb_w_out[o])
        x = x + y
        x = x + 0.5 * _swiglu(_rmsnorm(x, ffn_norm[layer, 1]), ffn_w_in[layer, 1], ffn_w_out[layer, 1])
    return x


DEPTH_2 = 1

GRID_W = 64
CTX_LEN = 256
CHUNK = 128
RET_HEADS = 4
RET_DK = 128
RET_DV = 128
ML_HEADS = 4
ML_DH = 128
RET_W = RET_HEADS * RET_DK
RET_VW = RET_HEADS * RET_DV
ML_W = ML_HEADS * ML_DH
N_ML_GATES = 4 * ML_HEADS
FFN_HIDDEN = -((-8 * D_MODEL) // (3 * 256)) * 256
ROPE_BASE = 10000.0
EPS = 1e-6
IN_WIDTHS = (RET_W, RET_W, RET_VW, RET_VW, ML_W, ML_W, ML_W, ML_W, N_ML_GATES, D_MODEL, D_MODEL)
IN_COLS = sum(IN_WIDTHS)


def rms_norm(x, gain):
    xf = x.astype(jnp.float32)
    y = xf * lax.rsqrt(jnp.mean(xf * xf, axis=-1, keepdims=True) + EPS)
    return (y * gain.astype(jnp.float32)).astype(x.dtype)

def head_norm(t):
    tf = t.astype(jnp.float32)
    return tf * lax.rsqrt(jnp.mean(tf * tf, axis=-1, keepdims=True) + EPS)

def modulate(h, shift, scale):
    return h * (1 + scale) + shift

def to_heads(t, n_heads):
    b, n, _ = t.shape
    return t.reshape(b, n, n_heads, -1).transpose(0, 2, 1, 3)

def from_heads(t):
    b, h, n, d = t.shape
    return t.transpose(0, 2, 1, 3).reshape(b, n, h * d)

def rope_2d(n):
    n_rows = n // GRID_W
    rows = jnp.broadcast_to(jnp.arange(n_rows, dtype=jnp.float32)[:, None], (n_rows, GRID_W)).reshape(n)
    cols = jnp.broadcast_to(jnp.arange(GRID_W, dtype=jnp.float32)[None, :], (n_rows, GRID_W)).reshape(n)
    n_freq = RET_DK // 4
    inv = ROPE_BASE ** (-jnp.arange(n_freq, dtype=jnp.float32) / n_freq)
    ang = jnp.concatenate([rows[:, None] * inv, cols[:, None] * inv], axis=-1)
    return jnp.cos(ang), jnp.sin(ang)

def apply_rope(t, cos, sin):
    half = t.shape[-1] // 2
    t1, t2 = t[..., :half], t[..., half:]
    cos = cos.astype(t.dtype)
    sin = sin.astype(t.dtype)
    return jnp.concatenate([t1 * cos - t2 * sin, t2 * cos + t1 * sin], axis=-1)

def to_chunks(t):
    b, h, n = t.shape[:3]
    t = t.reshape(b, h, n // CHUNK, CHUNK, *t.shape[3:])
    return jnp.moveaxis(t, 2, 0)

def from_chunks(t):
    t = jnp.moveaxis(t, 0, 2)
    b, h, nc, l = t.shape[:4]
    return t.reshape(b, h, nc * l, *t.shape[4:])

def retention_scan(q, k, v, log_gamma, state):
    q, k, v = (t.astype(jnp.float32) for t in (q, k, v))
    lg = log_gamma.astype(jnp.float32)
    pos = jnp.arange(CHUNK, dtype=jnp.float32)
    rel = pos[:, None] - pos[None, :]
    intra = jnp.where(rel >= 0, jnp.exp(lg[:, None, None] * jnp.maximum(rel, 0.0)), 0.0)
    inter = jnp.exp(lg[:, None] * (pos + 1.0))
    to_end = jnp.exp(lg[:, None] * (CHUNK - 1.0 - pos))
    chunk_decay = jnp.exp(lg * CHUNK)

    def step(s, inp):
        qc, kc, vc = inp
        scores = jnp.einsum("bhld,bhsd->bhls", qc, kc) * intra
        out = jnp.einsum("bhls,bhsv->bhlv", scores, vc) + inter[..., None] * jnp.einsum("bhld,bhdv->bhlv", qc, s)
        s_new = chunk_decay[:, None, None] * s + jnp.einsum("bhsd,bhsv->bhdv", kc * to_end[..., None], vc)
        return s_new, out

    final, outs = lax.scan(step, state, (to_chunks(q), to_chunks(k), to_chunks(v)))
    return from_chunks(outs), final

def mlstm_scan(q, k, v, i_pre, log_f, state):
    q, k, v, i_pre, log_f = (t.astype(jnp.float32) for t in (q, k, v, i_pre, log_f))
    causal = jnp.tril(jnp.ones((CHUNK, CHUNK), dtype=bool))

    def step(carry, inp):
        c_mat, n_vec, m = carry
        qc, kc, vc, ic, fc = inp
        b_cum = jnp.cumsum(fc, axis=-1)
        log_inter = b_cum + m[..., None]
        log_intra = jnp.where(causal, b_cum[..., :, None] - b_cum[..., None, :] + ic[..., None, :], -jnp.inf)
        m_t = jnp.maximum(log_inter, jnp.max(log_intra, axis=-1))
        w_inter = jnp.exp(log_inter - m_t)
        w_intra = jnp.exp(log_intra - m_t[..., None])
        s = jnp.einsum("bhld,bhsd->bhls", qc, kc) * w_intra
        num = jnp.einsum("bhls,bhsv->bhlv", s, vc) + w_inter[..., None] * jnp.einsum("bhvd,bhld->bhlv", c_mat, qc)
        den = jnp.sum(s, axis=-1) + w_inter * jnp.einsum("bhd,bhld->bhl", n_vec, qc)
        h = num / jnp.maximum(jnp.abs(den), jnp.exp(-m_t))[..., None]
        b_last = b_cum[..., -1]
        log_src = b_last[..., None] - b_cum + ic
        m_new = jnp.maximum(b_last + m, jnp.max(log_src, axis=-1))
        w_old = jnp.exp(b_last + m - m_new)
        w_src = jnp.exp(log_src - m_new[..., None])
        c_new = w_old[..., None, None] * c_mat + jnp.einsum("bhs,bhsv,bhsd->bhvd", w_src, vc, kc)
        n_new = w_old[..., None] * n_vec + jnp.einsum("bhs,bhsd->bhd", w_src, kc)
        return (c_new, n_new, m_new), h

    final, outs = lax.scan(step, state, tuple(to_chunks(t) for t in (q, k, v, i_pre, log_f)))
    return from_chunks(outs), final

def zero_states(b):
    ret = jnp.zeros((b, RET_HEADS, RET_DK, RET_DV), jnp.float32)
    ml = (jnp.zeros((b, ML_HEADS, ML_DH, ML_DH), jnp.float32),
          jnp.zeros((b, ML_HEADS, ML_DH), jnp.float32),
          jnp.zeros((b, ML_HEADS), jnp.float32))
    return (ret, ml)

def mixer_inputs(h, w_in, gate_bias, rope):
    offsets = np.cumsum(IN_WIDTHS)[:-1].tolist()
    rq, rk, rv, rg, mq, mk, mv, mo, mg, bg_ret, bg_ml = (h @ w for w in jnp.split(w_in, offsets, axis=-1))
    rq = to_heads(rq, RET_HEADS)
    rk = to_heads(rk, RET_HEADS) * (RET_DK ** -0.5)
    if rope is not None:
        rq = apply_rope(rq, *rope)
        rk = apply_rope(rk, *rope)
    rv = to_heads(rv, RET_HEADS)
    mq = to_heads(mq, ML_HEADS)
    mk = to_heads(mk, ML_HEADS) * (ML_DH ** -0.5)
    mv = to_heads(mv, ML_HEADS)
    b, n, _ = mg.shape
    mg = (mg + gate_bias.reshape(-1)).reshape(b, n, 4, ML_HEADS).transpose(2, 0, 3, 1)
    i_f, lf_f, i_b, lf_b = mg[0], jax.nn.log_sigmoid(mg[1]), mg[2], jax.nn.log_sigmoid(mg[3])
    feats = (rq, rk, rv, mq, mk, mv, i_f, lf_f, i_b, lf_b)
    post = (rg, mo, bg_ret, bg_ml)
    return feats, post

def bidirectional_scans(feats, log_gamma, st_f, st_b):
    rq, rk, rv, mq, mk, mv, i_f, lf_f, i_b, lf_b = feats
    flip = lambda t: jnp.flip(t, axis=2)
    ret_f, r_state_f = retention_scan(rq, rk, rv, log_gamma[0], st_f[0])
    ml_f, m_state_f = mlstm_scan(mq, mk, mv, i_f, lf_f, st_f[1])
    ret_b, r_state_b = retention_scan(flip(rq), flip(rk), flip(rv), log_gamma[1], st_b[0])
    ml_b, m_state_b = mlstm_scan(flip(mq), flip(mk), flip(mv), flip(i_b), flip(lf_b), st_b[1])
    return ret_f + flip(ret_b), ml_f + flip(ml_b), (r_state_f, m_state_f), (r_state_b, m_state_b)

def mixer_output(ret, ml, rg, mo, bg_ret, bg_ml, w_ret_up, w_ml_up, w_out):
    dtype = rg.dtype
    y_ret = from_heads(head_norm(ret)).astype(dtype) * jax.nn.silu(rg)
    y_ml = from_heads(head_norm(jax.nn.sigmoid(to_heads(mo, ML_HEADS)) * ml)).astype(dtype)
    merged = jax.nn.sigmoid(bg_ret) * (y_ret @ w_ret_up) + jax.nn.sigmoid(bg_ml) * (y_ml @ w_ml_up)
    return merged @ w_out

def swiglu(h, w_ffn_in, w_ffn_out):
    gate, up = jnp.split(h @ w_ffn_in, 2, axis=-1)
    return (jax.nn.silu(gate) * up) @ w_ffn_out

def second_inputs(seed: int = 0) -> dict:
    key = jax.random.key(seed)
    ks = jax.random.split(key, 20)
    f32 = jnp.float32

    def nrm(k, shape, scale):
        return jax.random.normal(k, shape, f32) * scale

    x = nrm(ks[0], (BATCH, SEQ, D_MODEL), 1.0)
    c = nrm(ks[1], (BATCH, D_MODEL), 1.0)
    ctx = nrm(ks[2], (BATCH, CTX_LEN, D_MODEL), 1.0)
    c_ctx = nrm(ks[3], (D_MODEL,), 1.0)
    w_ada = nrm(ks[4], (DEPTH_2, D_MODEL, 6 * D_MODEL), 0.5 * D_MODEL ** -0.5)
    b_ada = nrm(ks[5], (DEPTH_2, 6 * D_MODEL), 0.02)
    norm1_gain = 1.0 + nrm(ks[6], (DEPTH_2, D_MODEL), 0.02)
    norm2_gain = 1.0 + nrm(ks[7], (DEPTH_2, D_MODEL), 0.02)
    w_in = nrm(ks[8], (DEPTH_2, D_MODEL, IN_COLS), D_MODEL ** -0.5)
    i_bias = nrm(ks[9], (DEPTH_2, 2, ML_HEADS), 0.1)
    f_bias = jnp.linspace(3.0, 6.0, ML_HEADS, dtype=f32) + nrm(ks[10], (DEPTH_2, 2, ML_HEADS), 0.1)
    mlstm_gate_bias = jnp.stack([i_bias[:, 0], f_bias[:, 0], i_bias[:, 1], f_bias[:, 1]], axis=1)
    gamma = 1.0 - 2.0 ** (-5.0 - jnp.arange(RET_HEADS, dtype=f32))
    ret_decay_logit = jnp.log(gamma / (1.0 - gamma)) + nrm(ks[11], (DEPTH_2, 2, RET_HEADS), 0.1)
    w_ret_up = nrm(ks[12], (DEPTH_2, RET_VW, D_MODEL), RET_VW ** -0.5)
    w_ml_up = nrm(ks[13], (DEPTH_2, ML_W, D_MODEL), ML_W ** -0.5)
    w_out = nrm(ks[14], (DEPTH_2, D_MODEL, D_MODEL), D_MODEL ** -0.5)
    w_ffn_in = nrm(ks[15], (DEPTH_2, D_MODEL, 2 * FFN_HIDDEN), D_MODEL ** -0.5)
    w_ffn_out = nrm(ks[16], (DEPTH_2, FFN_HIDDEN, D_MODEL), FFN_HIDDEN ** -0.5)
    final_gain = 1.0 + nrm(ks[17], (D_MODEL,), 0.02)
    return {"x": x, "c": c, "ctx": ctx, "c_ctx": c_ctx, "w_ada": w_ada, "b_ada": b_ada,
            "norm1_gain": norm1_gain, "norm2_gain": norm2_gain, "w_in": w_in,
            "mlstm_gate_bias": mlstm_gate_bias, "ret_decay_logit": ret_decay_logit,
            "w_ret_up": w_ret_up, "w_ml_up": w_ml_up, "w_out": w_out,
            "w_ffn_in": w_ffn_in, "w_ffn_out": w_ffn_out, "final_gain": final_gain}

def second_block(x, c, ctx, c_ctx, w_ada, b_ada, norm1_gain, norm2_gain, w_in, mlstm_gate_bias,
              ret_decay_logit, w_ret_up, w_ml_up, w_out, w_ffn_in, w_ffn_out, final_gain):
    b, n, _ = x.shape
    rope = rope_2d(n)
    log_gamma = jax.nn.log_sigmoid(ret_decay_logit.astype(jnp.float32))
    for layer in range(DEPTH_2):
        mod = jax.nn.silu(c) @ w_ada[layer] + b_ada[layer]
        sh1, sc1, g1, sh2, sc2, g2 = jnp.split(mod[:, None, :], 6, axis=-1)
        mod_c = jax.nn.silu(c_ctx) @ w_ada[layer] + b_ada[layer]
        csh1, csc1, cg1, csh2, csc2, cg2 = jnp.split(mod_c, 6)

        hc = modulate(rms_norm(ctx, norm1_gain[layer]), csh1, csc1)
        feats_c, post_c = mixer_inputs(hc, w_in[layer], mlstm_gate_bias[layer], None)
        zero = zero_states(b)
        ret_c, ml_c, st_f, st_b = bidirectional_scans(feats_c, log_gamma[layer], zero, zero)

        hx = modulate(rms_norm(x, norm1_gain[layer]), sh1, sc1)
        feats_x, post_x = mixer_inputs(hx, w_in[layer], mlstm_gate_bias[layer], rope)
        ret_x, ml_x, _, _ = bidirectional_scans(feats_x, log_gamma[layer], st_f, st_b)
        x = x + g1 * mixer_output(ret_x, ml_x, *post_x, w_ret_up[layer], w_ml_up[layer], w_out[layer])
        x = x + g2 * swiglu(modulate(rms_norm(x, norm2_gain[layer]), sh2, sc2), w_ffn_in[layer], w_ffn_out[layer])

        if layer + 1 < DEPTH_2:
            ctx = ctx + cg1 * mixer_output(ret_c, ml_c, *post_c, w_ret_up[layer], w_ml_up[layer], w_out[layer])
            ctx = ctx + cg2 * swiglu(modulate(rms_norm(ctx, norm2_gain[layer]), csh2, csc2),
                                     w_ffn_in[layer], w_ffn_out[layer])
    return rms_norm(x, final_gain)


def setup_inputs(seed=0):
    out = dict(first_inputs(seed))
    for name, value in second_inputs(seed + 1).items():
        if name != "x":
            out[name + "_2"] = value
    return out


def reference(
    x, ffn_norm, ffn_w_in, ffn_w_out, mix_norm, hy_w_in, rg_conv_w, rg_conv_b, rg_gate_w,
    rg_gate_b, rg_lambda, fox_fgate_b, fox_qk_norm, hy_w_out, sb_w_qkv, sb_w_out, c_2, ctx_2,
    c_ctx_2, w_ada_2, b_ada_2, norm1_gain_2, norm2_gain_2, w_in_2, mlstm_gate_bias_2,
    ret_decay_logit_2, w_ret_up_2, w_ml_up_2, w_out_2, w_ffn_in_2, w_ffn_out_2, final_gain_2,
):
    x = first_block(
        x, ffn_norm, ffn_w_in, ffn_w_out, mix_norm, hy_w_in, rg_conv_w, rg_conv_b, rg_gate_w,
        rg_gate_b, rg_lambda, fox_fgate_b, fox_qk_norm, hy_w_out, sb_w_qkv, sb_w_out,
    )
    return second_block(
        x, c_2, ctx_2, c_ctx_2, w_ada_2, b_ada_2, norm1_gain_2, norm2_gain_2, w_in_2,
        mlstm_gate_bias_2, ret_decay_logit_2, w_ret_up_2, w_ml_up_2, w_out_2, w_ffn_in_2,
        w_ffn_out_2, final_gain_2,
    )


_drawn_inputs = setup_inputs


def setup_inputs(seed=0):
    import zlib

    import numpy as np

    out = dict(_drawn_inputs(seed))
    spreads = {}
    factors = {'rg_gate_b': 8.0,
     'fox_qk_norm': 4.487,
     'b_ada_2': 2.796,
     'norm1_gain_2': 7.507,
     'norm2_gain_2': 8.0,
     'final_gain_2': 2.834}
    for name, (base, spread) in spreads.items():
        noise = np.random.default_rng([zlib.crc32(name.encode()), seed]).standard_normal(out[name].shape)
        drawn = base * np.exp(spread * noise) if base else spread * noise
        out[name] = __import__('jax').numpy.asarray(drawn.astype(out[name].dtype))
    for name, factor in factors.items():
        out[name] = (out[name] * factor).astype(out[name].dtype)
    return out
```

```python
from contextlib import ExitStack

import numpy as np
import concourse.bass as bass
from concourse import mybir

P = 128
D, S, SC = 1024, 512, 256
KT = D // P
FF = 2816
FT = FF // P
UNIT = 2048
UC = 256
FOXH, SBH, HD = 8, 16, 64
NH = 4
TB = S // P
EPS = 1e-6
NEG = -1e30
F32, F32R = mybir.dt.float32, mybir.dt.float32r
ALU, ACT, AX = mybir.AluOpType, mybir.ActivationFunctionType, mybir.AxisListType.X

VCOLS = {}
_n = 0
for _name, _k in (("ffn0", 8), ("ffn1", 8), ("ffn2", 8), ("ffn3", 8), ("mix0", 8), ("mix1", 8), ("norm1", 8),
                  ("norm2", 8), ("final", 8), ("b_ada", 48), ("conv_w", 16), ("conv_b", 4), ("gate_b", 8),
                  ("soft", 12), ("qk", 2), ("fox_b", 1), ("ml_b", 2), ("cond", 16)):
    VCOLS[_name] = (_n, _k)
    _n += _k
NVEC = _n

N_ADA = 24
FFN_IN, FFN_OUT = 22, 12
FFN_UNITS = FFN_IN + FFN_OUT
FFN_CHUNKS = (8, 8, 6)
U_FFN = [0, 49, 83, 133, 200]
U_HY, U_HYO, U_SB, U_SBO, U_B2, U_POST, U_UP, U_B2O = 34, 45, 117, 129, 167, 180, 192, 196
N_UNITS = 234


class Tally:

    def __init__(self, sem):
        self.sem, self.n = sem, 0

    def up(self, k=1):
        self.n += k
        return self.sem, k

    def now(self):
        return self.sem, self.n


HY_VISITS = ([(U_HY + i, "feat", ("u", i)) for i in range(2)] + [(U_HY + 2 + i, "feat", ("gate", i)) for i in range(2)]
             + [(U_HY + 4 + i, "feat", ("q", i)) for i in range(2)] + [(U_HY + 6 + i, "feat", ("k", i)) for i in range(2)]
             + [(U_HY + 8 + i, "tok", ("v", i)) for i in range(2)] + [(U_HY + 10, "gates1", ("f", 0))])
SB_VISITS = ([(U_SB + i, "feat", ("q", i)) for i in range(4)] + [(U_SB + 4 + i, "feat", ("k", i)) for i in range(4)]
             + [(U_SB + 8 + i, "tok", ("v", i)) for i in range(4)])
B2_VISITS = ([x for i in range(2) for x in ((U_B2 + i, "ctok", ("crk", i)), (U_B2 + i, "feat", ("rk", i)))]
             + [x for i in range(2) for x in ((U_B2 + 2 + i, "ctok", ("crv", i)), (U_B2 + 2 + i, "tok", ("rv", i)))]
             + [x for i in range(2) for x in ((U_B2 + 4 + i, "ctok", ("cmk", i)), (U_B2 + 4 + i, "feat", ("mk", i)))]
             + [x for i in range(2) for x in ((U_B2 + 6 + i, "ctok", ("cmv", i)), (U_B2 + 6 + i, "tok", ("mv", i)))]
             + [(U_B2 + 8, "cgates", ("cmg", 0)), (U_B2 + 8, "gates", ("mg", 0))]
             + [(U_B2 + 9 + i, "feat", ("rq", i)) for i in range(2)] + [(U_B2 + 11 + i, "feat", ("mq", i)) for i in range(2)])
POST_VISITS = ([(U_POST + i, "feat", ("rg", i)) for i in range(2)] + [(U_POST + 2 + i, "feat", ("mo", i)) for i in range(2)]
               + [(U_POST + 4 + i, "feat", ("bg", i)) for i in range(8)])
N_EXTRA = len(B2_VISITS) - 13


def visit_base(u):
    return u + (N_EXTRA if u >= U_POST else 0)


VLAST = {}
for _u in range(N_UNITS):
    VLAST[_u] = visit_base(_u)
for _v, (_u, _k, _w) in enumerate(B2_VISITS):
    VLAST[_u] = U_B2 + _v

N_NORM = {"ffn0": 0, "mix0": 1, "ffn1": 2, "ffn2": 3, "mix1": 4, "ffn3": 5, "norm1": 6, "norm2": 7, "final": 8}


def build(nc, A):
    ctx = ExitStack()
    with ctx:
        def sb(name, shape, dt=F32):
            return ctx.enter_context(nc.sbuf_tensor("sb_" + name, shape, dt))

        def layout(tag, items):
            with ExitStack() as phase:
                return {n: phase.enter_context(nc.sbuf_tensor(f"{tag}_{n}", s, dt)) for n, s, dt in items}

        def sem(name):
            return ctx.enter_context(nc.semaphore(name))

        PS = ctx.enter_context(nc.psum_tensor("PS", [P, 8, 512], F32))
        XT = sb("XT", [P, KT, S])
        HH, HL = sb("HH", [P, KT, S], F32R), sb("HL", [P, KT, S], F32R)
        RAW = [sb(f"RAW{s}", [P, UNIT]) for s in range(2)]
        WH = [sb(f"WH{s}", [P, UNIT], F32R) for s in range(2)]
        WL = [sb(f"WL{s}", [P, UNIT], F32R) for s in range(2)]
        VEC = sb("VEC", [P, NVEC])
        IDENT, ONES = sb("IDENT", [P, P]), sb("ONES", [P, P])
        EPSC = sb("EPSC", [P, 1])
        SQT, SSACC, RINV = sb("SQT", [P, 2, S]), sb("SSACC", [P, S]), sb("RINV", [P, S])
        HT = sb("HT", [P, 2, S])
        SPT = sb("SPT", [P, 8, 12])
        MOD = sb("MOD", [P, 48, 2])
        CSC = sb("CSC", [P, 3, KT])
        QKG = sb("QKG", [P, 2])
        CS = sb("CS", [P, 16])
        LGS = sb("LGS", [P, 20])
        NGC, GCP, WS = sb("NGC", [P, 8]), sb("GCP", [P, 8]), sb("WS", [P, 8, 2])
        CEX, TE = sb("CEX", [P, 4]), sb("TE", [P, 4])
        SIL, G = HT, SQT

        ff = layout("ff", [("GH", [P, FT, S], F32R), ("GL", [P, FT, S], F32R)])
        GH, GL = ff["GH"], ff["GL"]
        hy = layout("hy", [("UP", [P, 4, S + 4], F32), ("GT", [P, 4, S], F32), ("Q", [P, 4, S], F32), ("K", [P, 4, S], F32),
                           ("V", [P, TB, 512], F32), ("F", [P, 2, S], F32), ("XC", [P, 4, S], F32), ("R", [P, 4, S], F32),
                           ("I", [P, 4, S], F32), ("PT", [P, 2, TB, S], F32), ("BD", [P, 8, P], F32), ("B64", [P, P], F32),
                           ("MASK", [P, P], F32), ("SEL", [P, 8, P], F32), ("ST", [P, 2, 2 * TB], F32)])
        sbm = layout("sbm", [("Q", [P, 8, S], F32), ("K", [P, 8, S], F32), ("V", [P, TB, D], F32), ("E", [P, 2, 1536], F32),
                             ("SP", [P, 2, 1536], F32), ("W", [P, 2, 1536], F32), ("TRI", [P, P], F32),
                             ("NONE", [P, P], F32), ("M01", [P, 3, P], F32)])
        lead = [("RQ", [P, 4, S], F32), ("MQ", [P, 4, S], F32), ("RK", [P, 4, S], F32), ("MK", [P, 4, S], F32),
                ("RV", [P, TB, 512], F32), ("MV", [P, TB, 512], F32), ("CRK", [P, 2, 512], F32),
                ("CRV", [P, 2, 512], F32), ("CMK", [P, 2, 512], F32), ("CMV", [P, 2, 512], F32)]
        b2 = layout("b2", lead + [("CT", [P, KT, SC], F32), ("HCH", [P, KT, SC], F32R), ("HCL", [P, KT, SC], F32R),
                                  ("ROPE", [P, 2, S], F32), ("SW", [P, 2, S], F32)])
        gr = layout("gr", lead + [("IG", [P, S + SC], F32), ("FG", [P, S + SC], F32)])
        rw = layout("rw", lead + [("CT", [P, KT, SC], F32), ("REL", [P, 896], F32), ("MX", [P, 896], F32), ("POS", [P, S], F32),
                                  ("QF", [P, 2, S], F32), ("SM", [P, TB, S], F32), ("KS", [P, 4, P], F32), ("ST", [P, 2, P], F32)])
        mw = layout("mw", lead + [("CT", [P, KT, SC], F32), ("F", [P, S + SC], F32), ("GM", [P, S + SC], F32),
                                  ("AB", [P, S + SC], F32), ("SEL", [P, 8, P], F32), ("MSK", [P, 2, P], F32),
                                  ("GCOL", [P, 6, 36], F32), ("ONE", [P, S], F32), ("KS", [P, 2, P], F32), ("QW", [P, S], F32)])
        po = layout("po", lead[:2] + [("BG", [P, 16, S], F32), ("RG", [P, 4, S], F32), ("MO", [P, 4, S], F32),
                                      ("MH", [P, KT, S], F32R), ("ML", [P, KT, S], F32R)])

        def col(name, i=0, n=1, rows=P):
            c = VCOLS[name][0] + i
            return VEC[0:rows, c:c + n]

        def f32(ap):
            return ap.bitcast(F32)

        raw_loaded = [sem(f"raw_loaded{s}") for s in range(2)]
        T = {n: Tally(sem(n)) for n in (
            "vec_in", "x_upd", "const_in", "ada_done", "mod_ready", "small", "act_step", "dve_step", "pool_step",
            "w_hi", "w_lo", "visit_done", "evac", "sq_ready", "ss_acc", "ss_sum", "rms_ready", "ht_ready", "hh_ready",
            "h_ready", "silu_ready", "g_mul", "gh_ready", "g_ready", "out_stored",
            "xc_ready", "rg_mm", "rg_sig", "rg_at", "rg_b2", "rg_sq", "y_f32", "y_hi", "y_ready", "up_clear",
            "qk_sq", "qk_ss", "qk_rms", "qk_norm", "f_abs", "f_ln", "c_ready",
            "fx_s", "fx_max", "fx_exp", "fx_p", "fx_t", "fx_pt", "fx_o",
            "sb_z", "sb_ln", "sb_sp", "sb_tri", "sb_exp", "sb_w", "sb_o",
            "csq", "css_acc", "css_sum", "crms", "cht", "chh", "ch_ready", "rope_sw", "rope_done",
            "rt_e", "rt_x", "rt_m", "rt_qx", "rt_q", "rt_ce", "rt_ks", "rt_st", "rt_stc", "rt_s", "rt_sm", "rt_o", "rt_out",
            "ml_abs", "ml_ln", "ml_rows", "ml_gt", "ml_gc", "ml_gcp", "ml_ws", "ml_ks", "ml_c0", "ml_c0c", "ml_s", "ml_g",
            "ml_w", "ml_sm", "ml_nd", "ml_h", "hn_in", "hn_sq", "hn_ss", "hn_rms",
            "up_mm", "up_m", "up_hi", "m_ready", "rot_in")}
        X0 = 16

        T["cond_ready"] = Tally(sem("cond_ready"))
        block = ctx.enter_context(nc.Block())
        B2U, HYV, SBV, B2V, POV, UPV = U_B2, U_HY, U_SB, U_B2, visit_base(U_POST), visit_base(U_UP)
        EV = {"hy": 0, "sb": len(HY_VISITS)}
        EV["b2"] = EV["sb"] + len(SB_VISITS)
        EV["po"] = EV["b2"] + len(B2_VISITS)
        RES = {"ffn0": 0, "hy": 1, "ffn1": 2, "ffn2": 3, "sb": 4, "ffn3": 5, "b2": 6, "ffn4": 7}
        Y0 = {"hy": 0, "sb": 8, "b2": 16}
        OFF = {0: 0, 1: 512, 3: 896, 2: 1024}

        def zs(h):
            return PS[:, 3 * (h % 2):3 * (h % 2) + 3, :].rearrange("p b c -> p (b c)")

        def diagonals(t, h):
            return ((t[:, h % 2, :].rearrange("p (a c) -> p a c", a=3)[:, :, 0:P], 3), (t[:, h % 2, 896:1024], 1))

        def PX(h):
            return hy["R"] if h % 2 == 0 else hy["I"]

        def LA(m):
            return SPT[:, 6, m:m + 1]

        def LAN(m):
            return SPT[:, 6, 4 + m:5 + m]

        def SQC(t):
            return SQT[:, t % 2, 0:SC]

        SSC, RINC = HT[:, 0, 0:SC], HT[:, 1, 0:SC]

        def WM(d):
            return [b2["RK"][:, j, :] if d == 0 else b2["CRK" if j < 2 else "CRV"][:, j % 2, :] for j in range(TB)]

        def C0N(k):
            return b2["RV"][:, k // 2, 256 * (k % 2):256 * (k % 2) + 256]

        def span(d, j):
            return (P * j, S) if d == 0 else (0, P * (j + 1))

        @block.sync
        def _(sp):
            def load(slot, unit):
                sp.dma_start(RAW[slot][:, :], A["weights"][unit]).then_inc(raw_loaded[slot], 16)

            load(0, 0)
            load(1, 1)
            sp.dma_start(XT[:, :, :], A["x"]).then_inc(*T["x_upd"].up(16))
            with sp.Fori(0, N_ADA // 2) as i:
                for s in range(2):
                    sp.wait_ge(T["ada_done"].sem, 2 * i + s + 1)
                    load(s, 2 * i + s + 2)
            with sp.Fori(0, (N_UNITS - 2) // 2) as i:
                for s in range(2):
                    sp.wait_ge(T["w_lo"].sem, 2 * i + s + 1)
                    load(s, 2 * i + s + N_ADA + 2)
            sp.wait_ge(T["ht_ready"].sem, 8 * 8 + 8)
            sp.dma_start(A["out"], XT[:, :, :]).then_inc(*T["out_stored"].up(16))
            sp.wait_ge(*T["out_stored"].now())

        @block.gpsimd
        def _(pool):
            def const(dst, src):
                pool.dma_start(dst, src).then_inc(*T["const_in"].up(16))

            pool.wait_ge(T["visit_done"].sem, visit_base(U_HY))
            pool.memset(hy["UP"][:, :, 0:4], 0.0).then_inc(*T["up_clear"].up())
            const(hy["BD"][:, :, :], A["c_gates"])
            const(hy["B64"][:, :], A["c_b64"])
            const(hy["MASK"][:, :], A["c_causal"])
            const(hy["SEL"][:, :, :], A["c_sel_fox"])
            pool.wait_ge(T["visit_done"].sem, visit_base(U_SB))
            const(sbm["TRI"][:, :], A["c_tri"])
            const(sbm["NONE"][:, :], A["c_negones"])
            const(sbm["M01"][:, :, :], A["c_m01"])
            for h in range(SBH):
                pool.wait_ge(T["sb_exp"].sem, h + 1)
                for ap, k in diagonals(sbm["W"], h):
                    last = pool.affine_select(out=ap, in_=ap, pattern=[[0, k], [1, P]] if k > 1 else [[1, P]],
                                              compare_op=ALU.is_gt, fill=0.0, base=0, channel_multiplier=-1)
                last.then_inc(*T["sb_w"].up())
            pool.wait_ge(T["visit_done"].sem, visit_base(U_B2))
            const(b2["CT"][:, :, :], A["ctx"])
            const(b2["ROPE"][:, :, :], A["c_rope"])
            pool.wait_ge(T["rope_done"].sem, 8)
            pool.wait_ge(T["visit_done"].sem, POV)
            const(rw["REL"][:, :], A["c_rel"])
            const(rw["POS"][:, :], A["c_pos"])
            pool.wait_ge(T["rt_out"].sem, 4)
            const(mw["SEL"][:, :, :], A["c_sel_ml"])
            const(mw["MSK"][:, :, :], A["c_msk_ml"])

        @block.scalar
        def _(act):
            st, sm = T["act_step"], T["small"]

            def split_hi(slot, free):
                if free is not None:
                    act.wait_ge(T["visit_done"].sem, free)
                act.activation(WH[slot][:, :], RAW[slot][:, :], ACT.Copy).then_inc(*T["w_hi"].up())

            def split(u):
                if u < N_UNITS:
                    act.wait_ge(raw_loaded[u % 2], 16 * ((N_ADA + u) // 2 + 1))
                    split_hi(u % 2, VLAST[u - 2] + 1 if u >= 2 else None)

            def split_at(base, per, i, off):
                u = base + off
                free = per * i + (visit_base(base) + off - 1)
                act.wait_ge(raw_loaded[u % 2], per * 8 * i + 16 * ((N_ADA + u) // 2 + 1))
                split_hi(u % 2, free if not isinstance(free, int) or free > 0 else None)

            def norm(m, shift=None):
                act.wait_ge(T["ss_sum"].sem, m + 1)
                act.activation(RINV[:, :], PS[:, 4, :], ACT.Sqrt, scale=1.0 / D, bias=EPSC[:, 0:1]).then_inc(*T["rms_ready"].up())
                if m == N_NORM["final"]:
                    return
                for kt in range(KT):
                    act.wait_ge(T["ht_ready"].sem, 8 * m + kt + 1)
                    if shift is None:
                        ins = act.activation(HH[:, kt, :], HT[:, kt % 2, :], ACT.Copy)
                    else:
                        ins = act.activation(HH[:, kt, :], HT[:, kt % 2, :], ACT.Identity, bias=shift(kt))
                    ins.then_inc(*T["hh_ready"].up())

            def ffn(n, shift=None):
                u0, v0 = U_FFN[n], visit_base(U_FFN[n])
                norm(N_NORM[("ffn0", "ffn1", "ffn2", "ffn3", "norm2")[n]], shift)

                def high_g(i):
                    act.wait_ge(T["g_mul"].sem, 22 * n + 2 * i + 2)
                    for m in range(2):
                        last = act.activation(GH[:, 2 * i + m, :], G[:, m, :], ACT.Copy)
                    last.then_inc(*T["gh_ready"].up())

                def pair(i, first):
                    split_at(u0, 2, i, 1)
                    if not first:
                        high_g(i - 1)
                    split_at(u0, 2, i, 2)
                    act.wait_ge(T["visit_done"].sem, 2 * i + v0 + 1)
                    for m in range(2):
                        act.activation(SIL[:, m, :], PS[:, m, :], ACT.Silu).then_inc(*T["silu_ready"].up())

                pair(0, True)
                with act.Fori(1, FFN_IN // 2) as i:
                    pair(i, False)
                high_g(FFN_IN // 2 - 1)
                residual(RES[f"ffn{n}"], u0 + FFN_IN, 3, n < 4)

            def residual(r, u0, chunks, loop):
                def group(i, j):
                    for c in range(chunks):
                        if not (isinstance(i, int) and u0 + chunks * (2 * i + j) + c + 1 >= N_UNITS):
                            split_at(u0, 2 * chunks, i, chunks * j + c + 1)
                    for m in range(2):
                        act.wait_ge(T["x_upd"].sem, 4 * i + X0 + 8 * r + 2 * j + m + 1)
                        act.wait_ge(T["ss_acc"].sem, 4 * i + 8 * (r + 1) + 2 * j + m - 1)
                        act.activation(SQT[:, m, :], XT[:, 4 * i + 2 * j + m, :], ACT.Square).then_inc(*T["sq_ready"].up())

                if loop:
                    with act.Fori(0, 2) as i:
                        group(i, 0)
                        group(i, 1)
                else:
                    for i in range(2):
                        group(i, 0)
                        group(i, 1)

            def visits(name, vis, evacuate):
                ev0, v0 = EV[name], {"hy": HYV, "sb": SBV, "b2": B2V, "po": POV}[name]
                seen = set()
                for k, (u, kind, what) in enumerate(vis):
                    if u not in seen:
                        seen.add(u)
                        split(u + 1)
                    act.wait_ge(T["visit_done"].sem, v0 + k + 1)
                    b = 2 * (k % 4)
                    evacuate(kind, what, b).then_inc(*T["evac"].up())

            def feat(dst, i, b, func=ACT.Copy, scale=1.0):
                for m in range(2):
                    last = act.activation(dst[:, 2 * i + m, :], PS[:, b + m, :], func, scale=scale)
                return last

            def tok(dst, i, b, blocks=TB, scale=1.0):
                for t in range(0, blocks, 2):
                    last = act.activation(dst[:, t:t + 2, UC * i:UC * i + UC],
                                          PS[:, b + t // 2, :].rearrange("p (t c) -> p t c", t=2), ACT.Copy, scale=scale)
                return last

            act.dma_start(VEC[:, :], A["vec"]).then_inc(*T["vec_in"].up(16))
            act.dma_start(IDENT[:, :], A["c_ident"]).then_inc(*T["vec_in"].up(16))
            act.dma_start(ONES[:, :], A["c_ones"]).then_inc(*T["vec_in"].up(16))
            act.dma_start(CEX[:, :], A["c_cex"]).then_inc(*T["vec_in"].up(16))
            act.wait_ge(*T["vec_in"].now())
            act.activation(CS[:, :], col("cond", 0, 16), ACT.Silu).then_inc(*T["cond_ready"].up())
            act.wait_ge(sm.sem, 1)
            act.activation(SPT[:, 1, :], SPT[:, 0, :], ACT.Exp, scale=-1.0).then_inc(*sm.up())
            act.wait_ge(sm.sem, 3)
            act.activation(SPT[:, 3, :], SPT[:, 2, :], ACT.Ln).then_inc(*sm.up())
            act.wait_ge(T["x_upd"].sem, X0)
            for t in range(KT):
                if t >= 2:
                    act.wait_ge(T["ss_acc"].sem, t - 1)
                act.activation(SQT[:, t % 2, :], XT[:, t, :], ACT.Square).then_inc(*T["sq_ready"].up())
            split(0)
            ffn(0)

            norm(N_NORM["mix0"])
            act.wait_ge(T["up_clear"].sem, 1)

            def evac_hy(kind, what, b):
                name, i = what
                if name == "u":
                    for m in range(2):
                        last = act.activation(hy["UP"][:, 2 * i + m, 4:S + 4], PS[:, b + m, :], ACT.Copy)
                    return last
                if name == "gate":
                    return feat(hy["GT"], i, b, ACT.Gelu_apprx_tanh)
                if name == "v":
                    return tok(hy["V"], i, b)
                if name == "f":
                    return act.activation(hy["F"][0:8, 0, :], PS[0:8, b, :], ACT.Identity, bias=col("fox_b", rows=8))
                return feat(hy[name.upper()], i, b)

            visits("hy", HY_VISITS, evac_hy)

            for g, dst in enumerate((hy["R"], hy["I"])):
                for m in range(4):
                    act.wait_ge(T["rg_mm"].sem, 4 * g + m + 1)
                    act.activation(dst[:, m, :], PS[:, 4 * g + m, :], ACT.Sigmoid, bias=col("gate_b", 4 * g + m)).then_inc(*T["rg_sig"].up())
            act.wait_ge(*T["rg_sig"].now())
            act.wait_ge(T["xc_ready"].sem, 4)
            for m in range(4):
                act.activation(hy["UP"][:, m, 0:S], hy["R"][:, m, :], ACT.Exp, scale=LA(m)).then_inc(*st.up())
                act.wait_ge(*st.now())
                act.activation(hy["R"][:, m, :], hy["R"][:, m, :], ACT.Tanh, scale=LAN(m)).then_inc(*T["rg_at"].up())
            for m in range(4):
                act.wait_ge(T["rg_b2"].sem, m + 1)
                act.activation(hy["R"][:, m, :], hy["R"][:, m, :], ACT.Sqrt).then_inc(*T["rg_sq"].up())
            for m in range(4):
                act.wait_ge(T["y_f32"].sem, m + 1)
                act.activation(HH[:, m, :], hy["XC"][:, m, :], ACT.Copy).then_inc(*T["y_hi"].up())

            for t in range(8):
                src = (hy["Q"] if t < 4 else hy["K"])[:, t % 4, :]
                if t >= 2:
                    act.wait_ge(T["qk_ss"].sem, t - 1)
                act.activation(SQT[:, t % 2, :], src, ACT.Square).then_inc(*T["qk_sq"].up())
                act.wait_ge(T["qk_ss"].sem, t + 1)
                if t >= 2:
                    act.wait_ge(T["qk_norm"].sem, t - 1)
                act.activation(HT[:, t % 2, :], PS[:, t % 2, :], ACT.Sqrt, scale=1.0 / HD, bias=EPSC[:, 0:1]).then_inc(*T["qk_rms"].up())
            act.wait_ge(T["f_abs"].sem, 1)
            fa = hy["PT"][0:8, 0, 0, :]
            act.activation(fa, fa, ACT.Exp, scale=-1.0).then_inc(*st.up())
            act.wait_ge(*st.now())
            act.activation(fa, fa, ACT.Ln, bias=1.0).then_inc(*T["f_ln"].up())

            def fox_exp(h):
                for i in range(TB):
                    act.wait_ge(T["fx_max"].sem, TB * h + i + 1)
                    w = P * (i + 1)
                    act.activation(PX(h)[:, i, 0:w], PS[:, i, 0:w], ACT.Exp, bias=hy["ST"][:, h % 2, i:i + 1],
                                   accum_out=hy["ST"][:, h % 2, TB + i:TB + i + 1]).then_inc(*T["fx_exp"].up())

            def fox_pt(h):
                for j in range(TB):
                    act.wait_ge(T["fx_t"].sem, TB * h + j + 1)
                    if h >= 2:
                        act.wait_ge(T["fx_o"].sem, h - 1)
                    w = S - P * j
                    act.activation(hy["PT"][:, h % 2, j, 0:w], PS[:, 4 + j % 2, 0:w], ACT.Copy).then_inc(*T["fx_pt"].up())
                if h % 2:
                    act.wait_ge(T["fx_o"].sem, h + 1)
                    act.activation(HH[:, 4 + h // 2, :], PS[:, 6 + h // 2 % 2, :], ACT.Copy).then_inc(*T["y_hi"].up())

            for h in range(FOXH):
                fox_exp(h)
                fox_pt(h)
            residual(RES["hy"], U_HYO, 1, True)
            ffn(1)
            ffn(2)

            norm(N_NORM["mix1"])
            visits("sb", SB_VISITS, lambda kind, what, b: tok(sbm["V"], what[1], b) if what[0] == "v" else
                   feat(sbm[what[0].upper()], what[1], b, scale=HD ** -0.5 if what[0] == "q" else 1.0))

            def sb_logs(h):
                E = sbm["E"][:, h % 2, 0:1280]
                act.wait_ge(T["sb_z"].sem, h + 1)
                if h >= 2:
                    act.wait_ge(T["sb_sp"].sem, h - 1)
                act.activation(E, zs(h)[:, 0:1280], ACT.Abs).then_inc(*st.up())
                act.wait_ge(*st.now())
                act.activation(E, E, ACT.Exp, scale=-1.0).then_inc(*st.up())
                act.wait_ge(*st.now())
                act.activation(E, E, ACT.Ln, bias=1.0).then_inc(*T["sb_ln"].up())

            def sb_weights(h):
                act.wait_ge(T["sb_tri"].sem, h + 1)
                if h >= 2:
                    act.wait_ge(T["sb_o"].sem, h - 1)
                act.activation(sbm["W"][:, h % 2, 0:1280], zs(h)[:, 0:1280], ACT.Exp).then_inc(*T["sb_exp"].up())

            def sb_out(h):
                if h % 2:
                    act.wait_ge(T["sb_o"].sem, h + 1)
                    act.activation(HH[:, h // 2, :], PS[:, 6 + h // 2 % 2, :], ACT.Copy).then_inc(*T["y_hi"].up())

            sb_logs(0)
            for h in range(SBH):
                if h + 1 < SBH:
                    sb_logs(h + 1)
                sb_weights(h)
                if h >= 1:
                    sb_out(h - 1)
            sb_out(SBH - 1)
            residual(RES["sb"], U_SBO, 1, True)
            ffn(3)

            act.wait_ge(T["const_in"].sem, 16 * 9)
            act.wait_ge(T["ss_acc"].sem, 8 * (N_NORM["norm1"] + 1))
            for t in range(KT):
                if t >= 2:
                    act.wait_ge(T["css_acc"].sem, t - 1)
                act.activation(SQC(t), b2["CT"][:, t, :], ACT.Square).then_inc(*T["csq"].up())
            act.wait_ge(T["css_sum"].sem, 1)
            act.activation(RINC, PS[:, 5, 0:SC], ACT.Sqrt, scale=1.0 / D, bias=EPSC[:, 0:1]).then_inc(*T["crms"].up())
            for t in range(KT):
                act.wait_ge(T["cht"].sem, t + 1)
                act.activation(b2["HCH"][:, t, :], SQC(t), ACT.Identity, bias=MOD[:, t, 1:2]).then_inc(*T["chh"].up())
            norm(N_NORM["norm1"], lambda kt: MOD[:, kt, 0:1])
            rots = [0]

            def evac_b2(kind, what, b):
                name, i = what
                if name in ("rq", "rk"):
                    scale = P ** -0.5 if name == "rk" else 1.0
                    for m in range(2):
                        if rots[0]:
                            act.wait_ge(T["rope_done"].sem, rots[0])
                        act.activation(b2[name.upper()][:, 2 * i + m, :], PS[:, b + m, :], ACT.Copy, scale=scale)
                        act.activation(b2["SW"][0:64, 0, :], PS[64:128, b + m, :], ACT.Copy, scale=scale)
                        last = act.activation(b2["SW"][64:128, 0, :], PS[0:64, b + m, :], ACT.Copy, scale=scale)
                        rots[0] += 1
                        if m == 0:
                            last.then_inc(*T["rope_sw"].up())
                    return last
                if name in ("cmg", "mg"):
                    lo, w = (0, SC) if name == "cmg" else (SC, S)
                    act.activation(gr["IG"][0:36, lo:lo + w], PS[0:36, b, 0:w], ACT.Identity, bias=col("ml_b", 0, rows=36))
                    return act.activation(gr["FG"][0:36, lo:lo + w], PS[0:36, b + 1, 0:w], ACT.Identity, bias=col("ml_b", 1, rows=36))
                scale = P ** -0.5 if name in ("crk", "mk", "cmk") else 1.0
                if kind == "feat":
                    return feat(b2[name.upper()], i, b, scale=scale)
                return tok(b2[name.upper()], i, b, TB if kind == "tok" else 2, scale)

            visits("b2", B2_VISITS, evac_b2)

            for h in range(NH):
                act.wait_ge(T["rt_e"].sem, h + 1)
                act.activation(rw["MX"][:, :], rw["MX"][:, :], ACT.Exp).then_inc(*T["rt_x"].up())
                if h:
                    act.wait_ge(T["rt_o"].sem, h)
                act.activation(rw["QF"][:, 0, :], rw["POS"][:, :], ACT.Exp, scale=LGS[:, h:h + 1]).then_inc(*T["rt_qx"].up())
                act.activation(rw["QF"][:, 1, :], rw["POS"][:, :], ACT.Exp, scale=LGS[:, 12 + h:13 + h],
                               bias=LGS[:, 16 + h:17 + h]).then_inc(*T["rt_qx"].up())
                if h:
                    act.wait_ge(T["rt_ks"].sem, h)
                act.activation(TE[:, 0:2], CEX[:, 0:2], ACT.Exp, scale=LGS[:, h:h + 1])
                act.activation(TE[:, 2:4], CEX[:, 2:4], ACT.Exp, scale=LGS[:, 4 + h:5 + h]).then_inc(*T["rt_ce"].up())
                act.wait_ge(T["rt_st"].sem, h + 1)
                act.activation(rw["ST"][:, 0, :], PS[:, 4, 0:P], ACT.Copy)
                act.activation(rw["ST"][:, 1, :], PS[:, 5, 0:P], ACT.Copy).then_inc(*T["rt_stc"].up())
                act.wait_ge(T["rt_o"].sem, h + 1)
                act.activation(b2["RQ"][:, h, :], PS[:, 6 + h % 2, :], ACT.Copy).then_inc(*T["rt_out"].up())

            act.wait_ge(T["ml_abs"].sem, 1)
            act.activation(mw["AB"][0:36, :], mw["AB"][0:36, :], ACT.Exp, scale=-1.0).then_inc(*st.up())
            act.wait_ge(*st.now())
            act.activation(mw["AB"][0:36, :], mw["AB"][0:36, :], ACT.Ln, bias=1.0).then_inc(*T["ml_ln"].up())
            act.wait_ge(T["ml_gt"].sem, 1)
            act.activation(mw["GCOL"][:, :, :].rearrange("p a b -> p (a b)"), PS[:, 0, 0:216], ACT.Copy)
            act.activation(NGC[:, :], PS[:, 1, 0:8], ACT.Copy)
            act.activation(GCP[:, :], PS[:, 1, 0:8], ACT.Copy, scale=-1.0).then_inc(*T["ml_gc"].up())
            act.wait_ge(*T["ml_gc"].now())
            for k in range(2 * NH):
                r = 32 * (k % 2) + k // 2
                act.activation(WS[:, k, :], mw["GCOL"][:, 0:2, r], ACT.Exp, bias=NGC[:, k:k + 1]).then_inc(*T["ml_ws"].up())
            for k in range(2 * NH):
                act.wait_ge(T["ml_c0"].sem, k + 1)
                act.activation(C0N(k), PS[:, 2 + k % 2, 0:256], ACT.Copy).then_inc(*T["ml_c0c"].up())
            for k in range(2 * NH):
                h, d = k // 2, k % 2
                r = 32 * d + h
                act.wait_ge(T["ml_g"].sem, k + 1)
                if k >= 2:
                    act.wait_ge(T["ml_h"].sem, k - 1)
                for j in range(TB):
                    lo, hi = span(d, j)
                    dg = P * j
                    g = mw["GCOL"][:, 2 + j, r:r + 1]
                    act.activation(WM(d)[j][:, dg:dg + P], PS[:, 5, dg:dg + P], ACT.Exp, bias=g)
                    lo, hi = (dg + P, hi) if d == 0 else (lo, dg)
                    if hi > lo:
                        act.activation(WM(d)[j][:, lo:hi], PS[:, 4, lo:hi], ACT.Exp, bias=g)
                act.activation(SQT[:, k % 2, :], PS[:, 4, :], ACT.Exp, bias=GCP[:, k:k + 1])
                act.activation(HT[:, k % 2, :], PS[:, 6, :], ACT.Exp).then_inc(*T["ml_w"].up())

            act.wait_ge(T["ml_h"].sem, 2 * NH)

            def evac_po(kind, what, b):
                name, i = what
                return feat(po[name.upper()], i, b, ACT.Silu if name == "rg" else ACT.Sigmoid)

            visits("po", POST_VISITS, evac_po)
            for t in range(8):
                src = b2["RQ" if t < 4 else "MQ"][:, t % 4, :]
                if t >= 4:
                    act.wait_ge(T["hn_in"].sem, t - 3)
                if t >= 2:
                    act.wait_ge(T["hn_ss"].sem, t - 1)
                act.activation(SQT[:, t % 2, :], src, ACT.Square).then_inc(*T["hn_sq"].up())
                act.wait_ge(T["hn_ss"].sem, t + 1)
                if t >= 2:
                    act.wait_ge(T["y_f32"].sem, 4 + t - 1)
                act.activation(HT[:, t % 2, :], PS[:, t % 2, :], ACT.Sqrt, scale=1.0 / P, bias=EPSC[:, 0:1]).then_inc(*T["hn_rms"].up())
                act.wait_ge(T["y_f32"].sem, 4 + t + 1)
                act.activation(HH[:, t, :], src, ACT.Copy).then_inc(*T["y_hi"].up())
            for i in range(2):
                split(U_UP + 2 * i + 1)
                split(U_UP + 2 * i + 2)
                for m in range(4):
                    act.wait_ge(T["up_m"].sem, 4 * i + m + 1)
                    act.activation(po["MH"][:, 4 * i + m, :], SQT[:, m % 2, :], ACT.Copy).then_inc(*T["up_hi"].up())
            residual(RES["b2"], U_B2O, 1, False)
            ffn(4, lambda kt: MOD[:, 24 + kt, 0:1])
            norm(N_NORM["final"])

        @block.vector
        def _(dve):
            st, sm = T["dve_step"], T["small"]

            def split_lo(slot, u):
                dve.wait_ge(T["w_hi"].sem, u + 1)
                dve.tensor_tensor(WL[slot][:, :], RAW[slot][:, :], f32(WH[slot][:, :]), ALU.subtract).then_inc(*T["w_lo"].up())

            def split(u):
                if u < N_UNITS:
                    split_lo(u % 2, u)

            def split_at(base, per, i, off):
                split_lo((base + off) % 2, per * i + (base + off))

            def step(ins):
                ins.then_inc(*st.up())
                dve.wait_ge(*st.now())

            def norm(m, gain, shift=None):
                dve.wait_ge(T["rms_ready"].sem, m + 1)
                step(dve.reciprocal(RINV[:, :], RINV[:, :]))
                final = m == N_NORM["final"]

                def scaled(kt):
                    dst = XT[:, kt, :] if final else HT[:, kt % 2, :]
                    if kt >= 2 and not final:
                        dve.wait_ge(T["h_ready"].sem, 8 * m + kt - 1)
                    dve.scalar_tensor_tensor(dst, XT[:, kt, :], gain(kt), RINV[:, :], ALU.mult, ALU.mult).then_inc(*T["ht_ready"].up())

                def low(kt):
                    dve.wait_ge(T["hh_ready"].sem, 8 * m + kt + 1)
                    if shift is None:
                        ins = dve.tensor_tensor(HL[:, kt, :], HT[:, kt % 2, :], f32(HH[:, kt, :]), ALU.subtract)
                    else:
                        ins = dve.scalar_tensor_tensor(HL[:, kt, :], HT[:, kt % 2, :], shift(kt), f32(HH[:, kt, :]), ALU.add, ALU.subtract)
                    ins.then_inc(*T["h_ready"].up())

                scaled(0)
                for kt in range(KT):
                    if kt + 1 < KT:
                        scaled(kt + 1)
                    if not final:
                        low(kt)

            def sum_square(count, slot):
                dve.wait_ge(T["sq_ready"].sem, count + 1)
                dve.wait_ge(T["ss_acc"].sem, count)
                dve.tensor_tensor(SSACC[:, :], SSACC[:, :], SQT[:, slot, :], ALU.add).then_inc(*T["ss_acc"].up())

            def ffn(n, gain, shift=None, scale=0.5):
                u0 = U_FFN[n]
                norm(N_NORM[("ffn0", "ffn1", "ffn2", "ffn3", "norm2")[n]], gain, shift)

                def gated(i):
                    if not isinstance(i, int) or 22 * n + 2 * i > 0:
                        dve.wait_ge(T["g_ready"].sem, 2 * i + 22 * n)
                    for m in range(2):
                        dve.wait_ge(T["silu_ready"].sem, 2 * i + 22 * n + m + 1)
                        if m == 0:
                            dve.wait_ge(T["visit_done"].sem, 2 * i + visit_base(u0) + 2)
                        dve.tensor_tensor(G[:, m, :], PS[:, 2 + m, :], SIL[:, m, :], ALU.mult).then_inc(*T["g_mul"].up())
                    dve.wait_ge(T["gh_ready"].sem, i + 11 * n + 1)
                    for m in range(2):
                        dve.tensor_tensor(GL[:, 2 * i + m, :], G[:, m, :], f32(GH[:, 2 * i + m, :]), ALU.subtract).then_inc(*T["g_ready"].up())

                def pair(i, first):
                    split_at(u0, 2, i, 1)
                    if not first:
                        gated(i - 1)
                    split_at(u0, 2, i, 2)

                pair(0, True)
                with dve.Fori(1, FFN_IN // 2) as i:
                    pair(i, False)
                gated(FFN_IN // 2 - 1)
                residual(RES[f"ffn{n}"], u0 + FFN_IN, 3, n < 4, scale)

            def residual(r, u0, chunks, loop, scale):
                dve.memset(SSACC[:, :], 0.0).then_inc(*st.up())
                cleared = st.n

                def group(i, j):
                    for c in range(chunks):
                        if not (isinstance(i, int) and u0 + chunks * (2 * i + j) + c + 1 >= N_UNITS):
                            split_at(u0, 2 * chunks, i, chunks * j + c + 1)
                    dve.wait_ge(T["visit_done"].sem, 2 * chunks * i + (visit_base(u0) + chunks * (j + 1)))
                    for m in range(2):
                        t = 4 * i + 2 * j + m
                        dve.scalar_tensor_tensor(XT[:, t, :], PS[:, 4 + 2 * j + m, :], scale if isinstance(scale, float) else scale(t),
                                                 XT[:, t, :], ALU.mult, ALU.add).then_inc(*T["x_upd"].up())
                    dve.wait_ge(st.sem, cleared)
                    for m in range(2):
                        sum_square(4 * i + (8 * (r + 1) + 2 * j + m), m)

                if loop:
                    with dve.Fori(0, 2) as i:
                        group(i, 0)
                        group(i, 1)
                else:
                    for i in range(2):
                        group(i, 0)
                        group(i, 1)

            step(dve.memset(EPSC[:, :], EPS))
            step(dve.memset(SSACC[:, :], 0.0))
            dve.wait_ge(T["vec_in"].sem, 64)
            Z = col("soft", 0, 12)
            a, e, u, l, d, t, la, sp = (SPT[:, k, :] for k in range(8))
            dve.scalar_tensor_tensor(a, Z, -1.0, Z, ALU.mult, ALU.max).then_inc(*sm.up())
            dve.wait_ge(sm.sem, 2)
            sm.n = 2
            dve.tensor_scalar(u, e, 1.0, None, ALU.add).then_inc(*sm.up())
            dve.wait_ge(sm.sem, 4)
            step(dve.tensor_scalar(d, u, -1.0, 1e-7, ALU.add, ALU.max))
            step(dve.reciprocal(d, d))
            step(dve.tensor_tensor(l, l, e, ALU.mult))
            step(dve.tensor_tensor(l, l, d, ALU.mult))
            step(dve.scalar_tensor_tensor(t, u, 1.0, e, ALU.is_equal, ALU.mult))
            step(dve.tensor_tensor(l, l, t, ALU.add))
            step(dve.tensor_scalar(t, Z, -1.0, 0.0, ALU.mult, ALU.max))
            step(dve.tensor_tensor(sp, t, l, ALU.add))
            step(dve.tensor_scalar(SPT[:, 6, 0:4], SPT[:, 7, 0:4], -8.0, None, ALU.mult))
            step(dve.tensor_scalar(SPT[:, 6, 4:8], SPT[:, 7, 0:4], 8.0, None, ALU.mult))
            step(dve.tensor_scalar(LGS[:, 0:8], SPT[:, 7, 4:12], -1.0, None, ALU.mult))
            step(dve.tensor_copy(LGS[:, 8:16], SPT[:, 7, 4:12]))
            step(dve.tensor_scalar(LGS[:, 16:20], SPT[:, 7, 8:12], -(S + 1.0), None, ALU.mult))
            step(dve.tensor_scalar(QKG[:, 0:1], col("qk", 0), HD ** -0.5, None, ALU.mult))
            step(dve.tensor_copy(QKG[:, 1:2], col("qk", 1)))
            for t_ in range(KT):
                sum_square(t_, t_ % 2)
            dve.wait_ge(T["ada_done"].sem, N_ADA)
            for j in range(2):
                step(dve.tensor_tensor(MOD[:, :, j], PS[:, 0, 0:96].rearrange("p (m j) -> p m j", j=2)[:, :, j], col("b_ada", 0, 48), ALU.add))
            for k, (g, lo, j) in enumerate((("norm1", 8, 0), ("norm1", 8, 1), ("norm2", 32, 0))):
                ins = dve.scalar_tensor_tensor(CSC[:, k, :], MOD[:, lo:lo + 8, j], 1.0, col(g, 0, 8), ALU.add, ALU.mult)
                if k < 2:
                    step(ins)
            ins.then_inc(*T["mod_ready"].up())
            dve.wait_ge(*T["mod_ready"].now())
            split(0)
            ffn(0, lambda kt: col("ffn0", kt))

            norm(N_NORM["mix0"], lambda kt: col("mix0", kt))
            for u_ in range(U_HY + 1, U_HYO + 1):
                split(u_)
            XC, R, I, UP = hy["XC"], hy["R"], hy["I"], hy["UP"]
            dve.wait_ge(T["evac"].sem, 2)
            for m in range(4):
                taps = [UP[:, m, 1 + j:1 + j + S] for j in range(4)]
                step(dve.tensor_scalar(XC[:, m, :], taps[0], col("conv_w", m), col("conv_b", m), ALU.mult, ALU.add))
                for j in range(1, 4):
                    ins = dve.scalar_tensor_tensor(XC[:, m, :], taps[j], col("conv_w", 4 * j + m), XC[:, m, :], ALU.mult, ALU.add)
                    if j < 3:
                        step(ins)
                ins.then_inc(*T["xc_ready"].up())
            for m in range(4):
                dve.wait_ge(T["rg_sig"].sem, 8)
                dve.wait_ge(T["xc_ready"].sem, 4)
                step(dve.tensor_tensor(I[:, m, :], I[:, m, :], XC[:, m, :], ALU.mult))
                dve.wait_ge(T["rg_at"].sem, m + 1)
                if m:
                    dve.wait_ge(*T["rg_b2"].now())
                step(dve.tensor_scalar(HT[:, 0, :], R[:, m, :], 1.0, None, ALU.add))
                step(dve.reciprocal(HT[:, 0, :], HT[:, 0, :]))
                dve.scalar_tensor_tensor(R[:, m, :], R[:, m, :], 2.0, HT[:, 0, :], ALU.mult, ALU.mult).then_inc(*T["rg_b2"].up())
            dve.wait_ge(T["evac"].sem, 4)
            dve.wait_ge(T["rg_mm"].sem, 8)
            for m in range(4):
                dve.wait_ge(T["rg_sq"].sem, m + 1)
                step(dve.tensor_tensor(I[:, m, :], I[:, m, :], R[:, m, :], ALU.mult))
                step(dve.tensor_tensor_scan(XC[:, m, :], UP[:, m, 0:S], I[:, m, :], 0.0, ALU.mult, ALU.add))
                dve.tensor_tensor(XC[:, m, :], XC[:, m, :], hy["GT"][:, m, :], ALU.mult).then_inc(*T["y_f32"].up())
            for m in range(4):
                dve.wait_ge(T["y_hi"].sem, m + 1)
                dve.tensor_tensor(HL[:, m, :], XC[:, m, :], f32(HH[:, m, :]), ALU.subtract).then_inc(*T["y_ready"].up())
            for t_ in range(8):
                dst = (hy["Q"] if t_ < 4 else hy["K"])[:, t_ % 4, :]
                dve.wait_ge(T["qk_rms"].sem, t_ + 1)
                step(dve.reciprocal(HT[:, t_ % 2, :], HT[:, t_ % 2, :]))
                dve.scalar_tensor_tensor(dst, dst, QKG[:, t_ // 4:t_ // 4 + 1], HT[:, t_ % 2, :], ALU.mult, ALU.mult).then_inc(*T["qk_norm"].up())
            F0, F1, F2 = hy["F"][0:8, 0, :], hy["PT"][0:8, 0, 0, :], hy["PT"][0:8, 0, 1, :]
            dve.wait_ge(T["evac"].sem, len(HY_VISITS))
            dve.scalar_tensor_tensor(F1, F0, -1.0, F0, ALU.mult, ALU.max).then_inc(*T["f_abs"].up())
            step(dve.memset(F2, 1.0))
            step(dve.memset(hy["F"][:, 1, :], 0.0))
            dve.wait_ge(T["f_ln"].sem, 1)
            step(dve.scalar_tensor_tensor(F0, F0, 0.0, F1, ALU.min, ALU.subtract))
            dve.tensor_tensor_scan(hy["F"][0:8, 1, :], F2, F0, 0.0, ALU.mult, ALU.add).then_inc(*T["c_ready"].up())

            def fox_max(h):
                if h >= 2:
                    dve.wait_ge(T["fx_p"].sem, TB * (h - 1))
                for i in range(TB):
                    dve.wait_ge(T["fx_s"].sem, TB * h + i + 1)
                    dve.tensor_reduce(hy["ST"][:, h % 2, i:i + 1], PS[:, i, 0:P * (i + 1)], AX, ALU.max, negate=True).then_inc(*T["fx_max"].up())

            def fox_norm(h):
                dve.wait_ge(T["fx_exp"].sem, TB * (h + 1))
                sums = hy["ST"][:, h % 2, TB:2 * TB]
                step(dve.reciprocal(sums, sums))
                for i in range(TB):
                    p = PX(h)[:, i, 0:P * (i + 1)]
                    dve.tensor_scalar(p, p, hy["ST"][:, h % 2, TB + i:TB + i + 1], None, ALU.mult).then_inc(*T["fx_p"].up())

            def out_low(y0, p, tile):
                dve.wait_ge(T["y_hi"].sem, y0 + 1)
                dve.tensor_tensor(HL[:, tile, :], PS[:, 6 + p % 2, :], f32(HH[:, tile, :]), ALU.subtract).then_inc(*T["y_ready"].up())

            for h in range(FOXH):
                fox_max(h)
                fox_norm(h)
                if h % 2:
                    out_low(4 + h // 2, h // 2, 4 + h // 2)
            split_ready = None
            residual(RES["hy"], U_HYO, 1, True, 1.0)
            ffn(1, lambda kt: col("ffn1", kt))
            ffn(2, lambda kt: col("ffn2", kt))

            norm(N_NORM["mix1"], lambda kt: col("mix1", kt))
            for u_ in range(U_SB + 1, U_SBO + 1):
                split(u_)
            dve.wait_ge(T["const_in"].sem, 16 * 7)

            def sb_soft(h):
                dve.wait_ge(T["sb_ln"].sem, h + 1)
                if h >= 2:
                    dve.wait_ge(T["sb_tri"].sem, h - 1)
                step(dve.scalar_tensor_tensor(sbm["SP"][:, h % 2, 0:1280], zs(h)[:, 0:1280], 0.0, sbm["E"][:, h % 2, 0:1280], ALU.max, ALU.add))
                (d3, _), (d1, _) = diagonals(sbm["SP"], h)
                dve.tensor_tensor(d3, d3, sbm["M01"][:, :, :], ALU.mult)
                dve.tensor_tensor(d1, d1, sbm["M01"][:, 0, :], ALU.mult).then_inc(*T["sb_sp"].up())

            def sb_low(h):
                if h % 2:
                    out_low(8 + h // 2, h // 2, h // 2)

            for h in range(SBH):
                sb_soft(h)
                if h >= 1:
                    sb_low(h - 1)
            sb_low(SBH - 1)
            residual(RES["sb"], U_SBO, 1, True, 1.0)
            ffn(3, lambda kt: col("ffn3", kt))

            step(dve.memset(SSC, 0.0))
            for t_ in range(KT):
                dve.wait_ge(T["csq"].sem, t_ + 1)
                dve.tensor_tensor(SSC, SSC, SQC(t_), ALU.add).then_inc(*T["css_acc"].up())
                dve.wait_ge(*T["css_acc"].now())
            dve.wait_ge(T["crms"].sem, 1)
            step(dve.reciprocal(RINC, RINC))
            for t_ in range(KT):
                if t_ >= 2:
                    dve.wait_ge(T["ch_ready"].sem, t_ - 1)
                dve.scalar_tensor_tensor(SQC(t_), b2["CT"][:, t_, :], CSC[:, 1, t_:t_ + 1], RINC, ALU.mult, ALU.mult).then_inc(*T["cht"].up())
                dve.wait_ge(T["chh"].sem, t_ + 1)
                dve.scalar_tensor_tensor(b2["HCL"][:, t_, :], SQC(t_), MOD[:, t_, 1:2], f32(b2["HCH"][:, t_, :]), ALU.add,
                                         ALU.subtract).then_inc(*T["ch_ready"].up())
            norm(N_NORM["norm1"], lambda kt: CSC[:, 0, kt:kt + 1], lambda kt: MOD[:, kt, 0:1])
            seen = set()
            for k, (u_, kind, (name, i)) in enumerate(B2_VISITS):
                if u_ not in seen:
                    seen.add(u_)
                    split(u_ + 1)
                if name in ("rq", "rk"):
                    dve.wait_ge(T["const_in"].sem, 16 * 9)
                    for m in range(2):
                        q = b2[name.upper()][:, 2 * i + m, :]
                        if m == 0:
                            dve.wait_ge(T["rope_sw"].sem, T["rot_in"].n + 1)
                            T["rot_in"].n += 1
                        else:
                            dve.wait_ge(T["evac"].sem, EV["b2"] + k + 1)
                        step(dve.tensor_tensor(b2["SW"][:, 0, :], b2["SW"][:, 0, :], b2["ROPE"][:, 1, :], ALU.mult))
                        step(dve.tensor_tensor(q, q, b2["ROPE"][:, 0, :], ALU.mult))
                        dve.tensor_tensor(q, q, b2["SW"][:, 0, :], ALU.add).then_inc(*T["rope_done"].up())

            dve.wait_ge(T["const_in"].sem, 16 * 11)
            dve.wait_ge(T["evac"].sem, EV["po"])
            MX, SM, KS = rw["MX"], rw["SM"], rw["KS"]
            for h in range(NH):
                if h:
                    dve.wait_ge(T["rt_sm"].sem, TB * h)
                step(dve.tensor_scalar(MX[:, :], rw["REL"][:, :], LGS[:, 12 + h:13 + h], None, ALU.mult))
                dve.scalar_tensor_tensor(MX[:, :], rw["REL"][:, :], LGS[:, h:h + 1], MX[:, :], ALU.mult, ALU.min).then_inc(*T["rt_e"].up())
                dve.wait_ge(T["rt_x"].sem, h + 1)
                step(dve.tensor_tensor(MX[:, 384:512], MX[:, 384:512], IDENT[:, :], ALU.add))
                for d_ in range(2):
                    dve.wait_ge(T["rt_qx"].sem, 2 * h + d_ + 1)
                    dve.tensor_tensor(rw["QF"][:, d_, :], rw["QF"][:, d_, :], b2["RQ"][:, h, :], ALU.mult).then_inc(*T["rt_q"].up())
                dve.wait_ge(T["rt_ce"].sem, h + 1)
                if h:
                    dve.wait_ge(T["rt_st"].sem, h)
                for k in range(4):
                    last = dve.tensor_scalar(KS[:, k, :], b2["CRK"][:, k % 2, P * h:P * h + P], TE[:, k:k + 1], None, ALU.mult)
                last.then_inc(*T["rt_ks"].up())
                if h:
                    dve.wait_ge(T["rt_o"].sem, h)
                for j in range(TB):
                    dve.wait_ge(T["rt_s"].sem, TB * h + j + 1)
                    dve.tensor_tensor(SM[:, j, :], PS[:, j, :], MX[:, 384 - P * j:896 - P * j], ALU.mult).then_inc(*T["rt_sm"].up())

            IG, FG, F, GM, ONE = gr["IG"], gr["FG"], mw["F"], mw["GM"], mw["ONE"]
            dve.wait_ge(T["rt_out"].sem, NH)
            dve.scalar_tensor_tensor(mw["AB"][0:36, :], FG[0:36, :], -1.0, FG[0:36, :], ALU.mult, ALU.max).then_inc(*T["ml_abs"].up())
            step(dve.memset(F[0:36, :], 0.0))
            step(dve.memset(GM[0:36, :], 0.0))
            step(dve.memset(ONE[0:36, :], 1.0))
            dve.wait_ge(T["ml_ln"].sem, 1)
            step(dve.scalar_tensor_tensor(FG[0:36, :], FG[0:36, :], 0.0, mw["AB"][0:36, :], ALU.min, ALU.subtract))

            def both_scans(dst, src, op):
                for rows, c, x, end in ((slice(0, 4), (lambda t: t[0:4, 0:SC]), (lambda t: t[0:4, SC:SC + S]), dst[0:4, SC - 1:SC]),
                                        (slice(32, 36), (lambda t: t[32:36, 0:SC][:, ::-1]), (lambda t: t[32:36, SC:SC + S][:, ::-1]), dst[32:36, 0:1])):
                    step(dve.tensor_tensor_scan(c(dst), ONE[rows, 0:SC], c(src), 0.0, ALU.mult, op))
                    step(dve.tensor_tensor_scan(x(dst), ONE[rows, 0:S], x(src), end, ALU.mult, op))

            both_scans(F, FG, ALU.add)
            step(dve.tensor_tensor(IG[0:36, :], IG[0:36, :], F[0:36, :], ALU.subtract))
            both_scans(GM, IG, ALU.max)
            dve.tensor_tensor(F[0:36, :], F[0:36, :], GM[0:36, :], ALU.add).then_inc(*T["ml_rows"].up())
            for k in range(2 * NH):
                dve.wait_ge(T["ml_ws"].sem, k + 1)
                if k:
                    dve.wait_ge(T["ml_c0"].sem, k)
                for c in range(2):
                    last = dve.tensor_scalar(mw["KS"][:, c, :], b2["CMK"][:, c, P * (k // 2):P * (k // 2) + P], WS[:, k, c:c + 1], None, ALU.mult)
                last.then_inc(*T["ml_ks"].up())
            for k in range(2 * NH):
                h, d_ = k // 2, k % 2
                dve.wait_ge(T["ml_w"].sem, k + 1)
                dve.wait_ge(T["ml_s"].sem, h + 1)
                if k:
                    dve.wait_ge(T["ml_nd"].sem, k)
                for j in range(TB):
                    lo, hi = span(d_, j)
                    dve.tensor_tensor(WM(d_)[j][:, lo:hi], PS[:, j, lo:hi], WM(d_)[j][:, lo:hi], ALU.mult)
                dve.tensor_tensor(mw["QW"][:, :], b2["MQ"][:, h, :], SQT[:, k % 2, :], ALU.mult).then_inc(*T["ml_sm"].up())
                dve.wait_ge(T["ml_nd"].sem, k + 1)
                den = HT[:, k % 2, :]
                step(dve.scalar_tensor_tensor(den, PS[:, 7, :], -1.0, den, ALU.mult, ALU.max))
                step(dve.tensor_tensor(den, PS[:, 7, :], den, ALU.max))
                step(dve.reciprocal(den, den))
                if d_ == 0:
                    dve.tensor_tensor(SSACC[:, :], PS[:, 6, :], den, ALU.mult).then_inc(*T["ml_h"].up())
                else:
                    step(dve.tensor_tensor(den, PS[:, 6, :], den, ALU.mult))
                    dve.wait_ge(T["ml_h"].sem, k)
                    dve.tensor_tensor(b2["MQ"][:, h, :], SSACC[:, :], den, ALU.add).then_inc(*T["ml_h"].up())

            for u_ in range(U_POST + 1, U_UP + 1):
                split(u_)
            dve.wait_ge(T["evac"].sem, EV["po"] + 4)
            for m in range(4):
                dve.tensor_tensor(b2["MQ"][:, m, :], b2["MQ"][:, m, :], po["MO"][:, m, :], ALU.mult).then_inc(*T["hn_in"].up())
            for t_ in range(8):
                y = b2["RQ" if t_ < 4 else "MQ"][:, t_ % 4, :]
                dve.wait_ge(T["hn_rms"].sem, t_ + 1)
                dve.wait_ge(T["hn_in"].sem, 4)
                step(dve.reciprocal(HT[:, t_ % 2, :], HT[:, t_ % 2, :]))
                ins = dve.tensor_tensor(y, y, HT[:, t_ % 2, :], ALU.mult)
                if t_ < 4:
                    step(ins)
                    ins = dve.tensor_tensor(y, y, po["RG"][:, t_, :], ALU.mult)
                ins.then_inc(*T["y_f32"].up())
                dve.wait_ge(*T["y_f32"].now())
                dve.wait_ge(T["y_hi"].sem, 16 + t_ + 1)
                dve.tensor_tensor(HL[:, t_, :], y, f32(HH[:, t_, :]), ALU.subtract).then_inc(*T["y_ready"].up())
            for i in range(2):
                split(U_UP + 2 * i + 1)
                split(U_UP + 2 * i + 2)
                dve.wait_ge(T["evac"].sem, EV["po"] + len(POST_VISITS))
                dve.wait_ge(T["visit_done"].sem, UPV + 2 * i + 2)
                for m in range(4):
                    a, b = HT[:, m % 2, :], SQT[:, m % 2, :]
                    if 4 * i + m >= 2:
                        dve.wait_ge(T["m_ready"].sem, 4 * i + m - 1)
                    step(dve.tensor_tensor(a, PS[:, m, :], po["BG"][:, 4 * i + m, :], ALU.mult))
                    step(dve.tensor_tensor(b, PS[:, 4 + m, :], po["BG"][:, 8 + 4 * i + m, :], ALU.mult))
                    dve.tensor_tensor(b, a, b, ALU.add).then_inc(*T["up_m"].up())
                    dve.wait_ge(*T["up_m"].now())
                    dve.wait_ge(T["up_hi"].sem, 4 * i + m + 1)
                    dve.tensor_tensor(po["ML"][:, 4 * i + m, :], b, f32(po["MH"][:, 4 * i + m, :]), ALU.subtract).then_inc(*T["m_ready"].up())
            residual(RES["b2"], U_B2O, 1, False, lambda t: MOD[:, 16 + t, 0:1])
            ffn(4, lambda kt: CSC[:, 2, kt:kt + 1], lambda kt: MOD[:, 24 + kt, 0:1], lambda t: MOD[:, 40 + t, 0:1])
            norm(N_NORM["final"], lambda kt: col("final", kt))

        @block.tensor
        def _(pe):
            def three(out, wh, wl, xh, xl, start, stop):
                pe.matmul(out, wh, xh, start=start, stop=False)
                pe.matmul(out, wh, xl, start=False, stop=False)
                return pe.matmul(out, wl, xh, start=False, stop=stop)

            def feature_major(slot, xh, xl, banks, tokens=S, k0=0, n=KT, start=True, stop=True, width=UC, ready=None):
                wh, wl = (w[slot][:, :].rearrange("p (k c) -> p k c", c=width) for w in (WH, WL))
                for k in range(n):
                    if ready is not None:
                        pe.wait_ge(T["h_ready"].sem, ready + k + 1)
                    for m, b in enumerate(banks):
                        c = slice(P * m, P * m + P)
                        last = three(PS[:, b, 0:tokens], wh[:, k, c], wl[:, k, c], xh[:, k0 + k, 0:tokens], xl[:, k0 + k, 0:tokens],
                                     start and k == 0, stop and k == n - 1)
                return last

            def token_major(slot, xh, xl, b, blocks):
                wh, wl = (w[slot][:, :].rearrange("p (k c) -> p k c", c=UC) for w in (WH, WL))
                for t in range(blocks):
                    out = PS[:, b + t // 2, UC * (t % 2):UC * (t % 2) + UC]
                    c = slice(P * t, P * t + P)
                    for k in range(KT):
                        last = three(out, xh[:, k, c], xl[:, k, c], wh[:, k, :], wl[:, k, :], k == 0, k == KT - 1)
                return last

            def norm(m):
                pe.wait_ge(T["ss_acc"].sem, 8 * (m + 1))
                pe.matmul(PS[:, 4, :], ONES[:, :], SSACC[:, :], start=True, stop=True).then_inc(*T["ss_sum"].up())

            def ffn(n):
                m = N_NORM[("ffn0", "ffn1", "ffn2", "ffn3", "norm2")[n]]
                u0 = U_FFN[n]
                norm(m)

                def pair(i, first):
                    for s, banks in ((0, (0, 1)), (1, (2, 3))):
                        pe.wait_ge(T["w_lo"].sem, 2 * i + (u0 + s + 1))
                        if not first:
                            pe.wait_ge(T["g_mul" if s else "silu_ready"].sem, 2 * i + 22 * n)
                        feature_major((u0 + s) % 2, HH, HL, banks, ready=8 * m if first and s == 0 else None)\
                            .then_inc(*T["visit_done"].up())

                pair(0, True)
                with pe.Fori(1, FFN_IN // 2) as i:
                    pair(i, False)
                residual(RES[f"ffn{n}"], u0 + FFN_IN, FFN_CHUNKS, GH, GL, n < 4, 22 * n)

            def residual(r, u0, chunks, xh, xl, loop, g0=None):
                def group(i, j):
                    for c, n in enumerate(chunks):
                        u = u0 + len(chunks) * j + c
                        pe.wait_ge(T["w_lo"].sem, 2 * len(chunks) * i + (u + 1))
                        if g0 is not None:
                            pe.wait_ge(T["g_ready"].sem, g0 + sum(chunks[:c + 1]))
                        if c == 0:
                            pe.wait_ge(T["x_upd"].sem, 4 * i + (X0 + 8 * r + 2 * j - 2))
                        feature_major(u % 2, xh, xl, (4 + 2 * j, 5 + 2 * j), k0=sum(chunks[:c]), n=n, start=c == 0,
                                      stop=c == len(chunks) - 1).then_inc(*T["visit_done"].up())

                if loop:
                    with pe.Fori(0, 2) as i:
                        group(i, 0)
                        group(i, 1)
                else:
                    for i in range(2):
                        group(i, 0)
                        group(i, 1)

            def visits(name, vis, m=None):
                for k, (u, kind, what) in enumerate(vis):
                    pe.wait_ge(T["w_lo"].sem, u + 1)
                    if k >= 4:
                        pe.wait_ge(T["evac"].sem, EV[name] + k - 3)
                    b = 2 * (k % 4)
                    first = 8 * m if m is not None and k == (1 if name == "b2" else 0) else None
                    if kind == "feat":
                        last = feature_major(u % 2, HH, HL, (b, b + 1), ready=first)
                    elif kind in ("gates", "gates1"):
                        last = feature_major(u % 2, HH, HL, (b, b + 1) if kind == "gates" else (b,))
                    elif kind == "cgates":
                        last = feature_major(u % 2, b2["HCH"], b2["HCL"], (b, b + 1), tokens=SC)
                    elif kind == "tok":
                        last = token_major(u % 2, HH, HL, b, TB)
                    else:
                        last = token_major(u % 2, b2["HCH"], b2["HCL"], b, 2)
                    last.then_inc(*T["visit_done"].up())

            pe.wait_ge(*T["vec_in"].now())
            pe.wait_ge(T["cond_ready"].sem, 1)
            out = PS[:, 0, 0:96].rearrange("p (i m j) -> p i m j", m=4, j=2)
            with pe.Fori(0, N_ADA // 2) as i:
                for s in range(2):
                    pe.wait_ge(raw_loaded[s], 16 * i + 16)
                    w = RAW[s][:, :].rearrange("p (k c) -> p k c", c=UC)
                    for m in range(2):
                        for k in range(KT):
                            last = pe.matmul(out[:, i, 2 * s + m, :], w[:, k, P * m:P * m + P], CS[:, 2 * k:2 * k + 2], start=k == 0, stop=k == KT - 1)
                    last.then_inc(*T["ada_done"].up())
            ffn(0)

            norm(N_NORM["mix0"])
            visits("hy", HY_VISITS, N_NORM["mix0"])
            pe.wait_ge(T["evac"].sem, EV["sb"])
            pe.wait_ge(T["const_in"].sem, 16 * 4)
            for g in range(2):
                for m in range(4):
                    pe.wait_ge(T["xc_ready"].sem, m + 1)
                    pe.matmul(PS[:, 4 * g + m, :], hy["BD"][:, 4 * g + m, :], hy["XC"][:, m, :], start=True, stop=True)\
                        .then_inc(*T["rg_mm"].up())
            pe.wait_ge(T["rg_sig"].sem, 8)
            for t in range(8):
                pe.wait_ge(T["qk_sq"].sem, t + 1)
                if t >= 2:
                    pe.wait_ge(T["qk_rms"].sem, t - 1)
                pe.matmul(PS[:, t % 2, :], hy["B64"][:, :], SQT[:, t % 2, :], start=True, stop=True).then_inc(*T["qk_ss"].up())

            def fox_scores(h):
                r = slice(64 * (h % 2), 64 * (h % 2) + 64)
                for i in range(TB):
                    w = P * (i + 1)
                    if h:
                        pe.wait_ge(T["fx_exp"].sem, TB * (h - 1) + i + 1)
                    o = PS[:, i, 0:w]
                    pe.matmul(o, hy["Q"][r, h // 2, P * i:w], hy["K"][r, h // 2, 0:w], start=True, stop=False)
                    pe.matmul(PS[:, i, P * i:w], IDENT[:, :], hy["MASK"][:, :], start=False, stop=False, skip_group_check=True)
                    pe.matmul(o, hy["SEL"][:, h, :], hy["F"][:, 1, 0:w], start=False, stop=True)\
                        .then_inc(*T["fx_s"].up())

            def values(out_bank, h, v, probs, widths):
                r = slice(64 * (h % 2), 64 * (h % 2) + 64)
                for j in range(TB):
                    last = pe.matmul(PS[r, out_bank, P * j:S], v[:, j, HD * h:HD * h + HD], probs(j), start=j == 0, stop=True,
                                     skip_group_check=True)
                return last

            pe.wait_ge(T["qk_norm"].sem, 8)
            pe.wait_ge(T["c_ready"].sem, 1)
            fox_scores(0)
            for h in range(FOXH):
                if h + 1 < FOXH:
                    fox_scores(h + 1)
                for j in range(TB):
                    n = TB * h + j
                    if n >= 2:
                        pe.wait_ge(T["fx_pt"].sem, n - 1)
                    for i in range(j, TB):
                        pe.wait_ge(T["fx_p"].sem, TB * h + i + 1)
                        last = pe.transpose(PS[:, 4 + j % 2, P * (i - j):P * (i - j) + P], PX(h)[:, i, P * j:P * j + P], IDENT[:, :])
                    last.then_inc(*T["fx_t"].up())
                pe.wait_ge(T["fx_pt"].sem, TB * (h + 1))
                if h >= 4 and h % 2 == 0:
                    pe.wait_ge(T["y_ready"].sem, 4 + h // 2 - 1)
                values(6 + h // 2 % 2, h, hy["V"], lambda j: hy["PT"][:, h % 2, j, 0:S - P * j], None).then_inc(*T["fx_o"].up())
            pe.wait_ge(T["y_ready"].sem, 8)
            residual(RES["hy"], U_HYO, (8,), HH, HL, True)
            ffn(1)
            ffn(2)

            norm(N_NORM["mix1"])
            visits("sb", SB_VISITS, N_NORM["mix1"])
            pe.wait_ge(T["evac"].sem, EV["b2"])
            pe.wait_ge(T["const_in"].sem, 16 * 7)

            def sb_scores(h):
                r = slice(64 * (h % 2), 64 * (h % 2) + 64)
                if h >= 2:
                    pe.wait_ge(T["sb_exp"].sem, h - 1)
                for i in (0, 1, 3, 2):
                    last = pe.matmul(zs(h)[:, OFF[i]:OFF[i] + S - P * i], sbm["K"][r, h // 2, P * i:P * i + P], sbm["Q"][r, h // 2, P * i:S],
                                     start=i != 3, stop=True, skip_group_check=True)
                last.then_inc(*T["sb_z"].up())

            def sb_logs(h):
                pe.wait_ge(T["sb_sp"].sem, h + 1)
                sp_ = sbm["SP"][:, h % 2, :]
                for i in range(TB):
                    for j in range(i, TB):
                        w = S - P * j
                        o = OFF[i] + P * (j - i)
                        last = pe.matmul(zs(h)[:, o:o + w], (sbm["TRI"] if i == j else sbm["NONE"])[:, :], sp_[:, OFF[j]:OFF[j] + w],
                                         start=False, stop=True, skip_group_check=True)
                last.then_inc(*T["sb_tri"].up())

            def sb_values(h):
                pe.wait_ge(T["sb_w"].sem, h + 1)
                if h >= 4 and h % 2 == 0:
                    pe.wait_ge(T["y_ready"].sem, 8 + h // 2 - 1)
                values(6 + h // 2 % 2, h, sbm["V"], lambda j: sbm["W"][:, h % 2, OFF[j]:OFF[j] + S - P * j], None).then_inc(*T["sb_o"].up())

            sb_scores(0)
            for h in range(SBH):
                if h + 1 < SBH:
                    sb_scores(h + 1)
                sb_logs(h)
                if h >= 1:
                    sb_values(h - 1)
            sb_values(SBH - 1)
            pe.wait_ge(T["y_ready"].sem, 16)
            residual(RES["sb"], U_SBO, (8,), HH, HL, True)
            ffn(3)

            pe.wait_ge(T["css_acc"].sem, 8)
            pe.matmul(PS[:, 5, 0:SC], ONES[:, :], SSC, start=True, stop=True).then_inc(*T["css_sum"].up())
            norm(N_NORM["norm1"])
            pe.wait_ge(T["ch_ready"].sem, 8)
            visits("b2", B2_VISITS, N_NORM["norm1"])
            pe.wait_ge(T["evac"].sem, EV["po"])
            pe.wait_ge(T["rope_done"].sem, 8)

            for h in range(NH):
                c = slice(P * h, P * h + P)
                pe.wait_ge(T["rt_ks"].sem, h + 1)
                if h:
                    pe.wait_ge(T["rt_stc"].sem, h)
                for d in range(2):
                    for b in range(2):
                        last = pe.matmul(PS[:, 4 + d, 0:P], rw["KS"][:, 2 * d + b, :], b2["CRV"][:, b, c], start=b == 0, stop=b == 1)
                last.then_inc(*T["rt_st"].up())
                for j in range(TB):
                    if h:
                        pe.wait_ge(T["rt_sm"].sem, TB * (h - 1) + j + 1)
                    pe.matmul(PS[:, j, :], b2["RK"][:, h, P * j:P * j + P], b2["RQ"][:, h, :], start=True, stop=True).then_inc(*T["rt_s"].up())
                if h >= 2:
                    pe.wait_ge(T["rt_out"].sem, h - 1)
                for j in range(TB):
                    pe.wait_ge(T["rt_sm"].sem, TB * h + j + 1)
                    pe.matmul(PS[:, 6 + h % 2, :], b2["RV"][:, j, c], rw["SM"][:, j, :], start=j == 0, stop=False)
                pe.wait_ge(T["rt_q"].sem, 2 * h + 2)
                pe.wait_ge(T["rt_stc"].sem, h + 1)
                for d in range(2):
                    last = pe.matmul(PS[:, 6 + h % 2, :], rw["ST"][:, d, :], rw["QF"][:, d, :], start=False, stop=d == 1)
                last.then_inc(*T["rt_o"].up())

            pe.wait_ge(T["ml_rows"].sem, 1)
            pe.wait_ge(T["const_in"].sem, 16 * 13)
            for b in range(6):
                pe.transpose(PS[:, 0, 36 * b:36 * b + 36], gr["IG"][0:36, P * b:P * b + P], IDENT[0:36, 0:36])
            for k in range(2 * NH):
                e = 0 if k % 2 else SC - 1
                last = pe.matmul(PS[:, 1, k:k + 1], mw["SEL"][0:36, k, :], mw["GM"][0:36, e:e + 1], start=True, stop=True)
            last.then_inc(*T["ml_gt"].up())
            for k in range(2 * NH):
                pe.wait_ge(T["ml_ks"].sem, k + 1)
                if k >= 2:
                    pe.wait_ge(T["ml_c0c"].sem, k - 1)
                for part in range(2):
                    for b in range(2):
                        v = b2["CMV"][:, b, P * (k // 2):P * (k // 2) + P] if part == 0 else ONES[:, :]
                        last = pe.matmul(PS[:, 2 + k % 2, P * part:P * part + P], mw["KS"][:, b, :], v, start=b == 0, stop=b == 1)
                last.then_inc(*T["ml_c0"].up())
            pe.wait_ge(T["ml_c0c"].sem, 2 * NH)
            for k in range(2 * NH):
                h, d = k // 2, k % 2
                if d == 0:
                    if h:
                        pe.wait_ge(T["ml_sm"].sem, k)
                    for j in range(TB):
                        last = pe.matmul(PS[:, j, :], b2["MK"][:, h, P * j:P * j + P], b2["MQ"][:, h, :], start=True, stop=True)
                    last.then_inc(*T["ml_s"].up())
                if k:
                    pe.wait_ge(T["ml_w"].sem, k)
                    pe.wait_ge(T["ml_h"].sem, k)
                sel, gm = mw["SEL"][0:36, k, :], mw["GM"][0:36, SC:SC + S]
                pe.matmul(PS[:, 4, :], sel, gm, start=True, stop=True)
                pe.matmul(PS[:, 5, :], sel, gm, start=True, stop=True)
                for j in range(TB):
                    pe.matmul(PS[:, 5, P * j:P * j + P], IDENT[:, :], mw["MSK"][:, d, :], start=False, stop=True, skip_group_check=True)
                pe.matmul(PS[:, 6, :], sel, mw["F"][0:36, SC:SC + S], start=True, stop=True).then_inc(*T["ml_g"].up())
                pe.wait_ge(T["ml_sm"].sem, k + 1)
                for bank, v, inter in ((6, lambda j: b2["MV"][:, j, P * h:P * h + P], C0N(k)[:, 0:P]), (7, lambda j: ONES[:, :], C0N(k)[:, P:2 * P])):
                    order = range(TB) if d == 0 else range(TB - 1, -1, -1)
                    for n, j in enumerate(order):
                        lo, hi = span(d, j)
                        pe.matmul(PS[:, bank, lo:hi], v(j), WM(d)[j][:, lo:hi], start=n == 0, stop=True, skip_group_check=n > 0)
                    last = pe.matmul(PS[:, bank, :], inter, mw["QW"][:, :], start=False, stop=True, skip_group_check=True)
                last.then_inc(*T["ml_nd"].up())

            visits("po", POST_VISITS)
            pe.wait_ge(T["evac"].sem, EV["po"] + len(POST_VISITS))
            for t in range(8):
                pe.wait_ge(T["hn_sq"].sem, t + 1)
                if t >= 2:
                    pe.wait_ge(T["hn_rms"].sem, t - 1)
                pe.matmul(PS[:, t % 2, :], ONES[:, :], SQT[:, t % 2, :], start=True, stop=True).then_inc(*T["hn_ss"].up())
            pe.wait_ge(T["y_ready"].sem, 24)
            for i in range(2):
                if i:
                    pe.wait_ge(T["up_m"].sem, 4 * i)
                for s in range(2):
                    u = U_UP + 2 * i + s
                    pe.wait_ge(T["w_lo"].sem, u + 1)
                    feature_major(u % 2, HH, HL, range(4 * s, 4 * s + 4), k0=4 * s, n=4, width=512).then_inc(*T["visit_done"].up())
            pe.wait_ge(T["m_ready"].sem, 8)
            residual(RES["b2"], U_B2O, (8,), po["MH"], po["ML"], False)
            ffn(4)
            norm(N_NORM["final"])


def _tiles(w, cols):
    w = np.asarray(w)[:, cols]
    return w.reshape(w.shape[0] // P, P, w.shape[1]).transpose(1, 0, 2)


def _unit(w, cols):
    t = _tiles(w, cols)
    out = np.zeros((P, UNIT // UC, UC) if t.shape[2] <= UC else (P, UNIT // t.shape[2], t.shape[2]), np.float32)
    out[:, :t.shape[1], :t.shape[2]] = t
    return out.reshape(P, UNIT)


def _ffn_units(w_in, w_out):
    units = []
    for i in range(FT // 2):
        units += [_unit(w_in, slice(UC * i, UC * i + UC)), _unit(w_in, slice(FF + UC * i, FF + UC * i + UC))]
    for j in range(D // UC):
        at = 0
        for n in FFN_CHUNKS:
            units.append(_unit(w_out[at:at + P * n], slice(UC * j, UC * j + UC)))
            at += P * n
    return units


def _columns(w, lo, n):
    return [_unit(w, slice(lo + UC * i, lo + UC * i + UC)) for i in range(n // UC)]


def _placed(w, places):
    t = np.zeros((w.shape[0], UC), np.float32)
    for p, c in places:
        t[:, p] = w[:, c]
    return _unit(t, slice(0, UC))


def _col(v):
    return np.asarray(v).reshape(-1, P).T


def _constants():
    f = np.float32
    r = np.arange(P)
    t = np.arange(S)
    row, colm = (t // 64).astype(f), (t % 64).astype(f)
    inv = (10000.0 ** (-np.arange(32, dtype=np.float64) / 32)).astype(f)
    ang = np.concatenate([row[:, None] * inv, colm[:, None] * inv], -1).T.astype(np.float64)
    rope = np.stack([np.concatenate([np.cos(ang), np.cos(ang)]), np.concatenate([-np.sin(ang), np.sin(ang)])], 1)
    sel_fox = np.zeros((P, 8, P))
    for h in range(8):
        sel_fox[h, h] = -1
    sel_ml = np.zeros((P, 8, P))
    for k in range(8):
        sel_ml[32 * (k % 2) + k // 2, k] = -1
    s = np.arange(P)[:, None]
    cex = np.stack([255 - r, 127 - r, r, 128 + r], 1)
    return {k: np.ascontiguousarray(v, dtype=f) for k, v in {
        "c_ident": np.eye(P), "c_ones": np.ones((P, P)), "c_cex": cex,
        "c_b64": np.kron(np.eye(2), np.ones((64, 64))), "c_causal": np.where(r[None, :] <= s, 0.0, NEG), "c_sel_fox": sel_fox,
        "c_tri": np.where(s >= r[None, :], -1.0, 0.0), "c_negones": -np.ones((P, P)),
        "c_m01": np.repeat((s < r[None, :])[:, None, :], 3, 1), "c_rope": rope,
        "c_rel": (np.arange(896) - 384)[None, :] - s, "c_pos": np.broadcast_to(t + 1.0, (P, S)),
        "c_sel_ml": sel_ml, "c_msk_ml": np.stack([np.where(r[None, :] >= s, 0.0, NEG), np.where(r[None, :] <= s, 0.0, NEG)], 1),
    }.items()}


def _pack(a):
    g = {k: np.asarray(v) for k, v in a.items()}
    hy, b2, out = g["hy_w_in"][0], g["w_in_2"][0], {}
    units = _columns(g["w_ada_2"][0], 0, 6 * D)
    ffn = [_ffn_units(g["ffn_w_in"][l, k], g["ffn_w_out"][l, k]) for l in range(2) for k in range(2)]
    units += ffn[0] + _columns(hy, 0, 5 * 512) + [_placed(hy, [(h, 2560 + h) for h in range(8)])] + _columns(g["hy_w_out"][0], 0, D)
    units += ffn[1] + ffn[2] + _columns(g["sb_w_qkv"][0], 0, 3 * D) + _columns(g["sb_w_out"][0], 0, D) + ffn[3]
    part = lambda i: _columns(b2, 512 * i, 512)
    gates = [(32 * d + h, 4096 + 8 * d + h) for d in range(2) for h in range(4)]
    gates += [(P + 32 * d + h, 4096 + 8 * d + 4 + h) for d in range(2) for h in range(4)]
    units += part(1) + part(2) + part(5) + part(6) + [_placed(b2, gates)] + part(0) + part(4) + part(3) + part(7)
    units += _columns(b2, 4112, 2 * D)
    for i in range(2):
        units += [_unit(g[n][0], slice(512 * i, 512 * i + 512)) for n in ("w_ret_up_2", "w_ml_up_2")]
    units += _columns(g["w_out_2"][0], 0, D) + _ffn_units(g["w_ffn_in_2"][0], g["w_ffn_out_2"][0])
    assert len(units) == N_ADA + N_UNITS
    out["weights"] = np.stack(units)
    vec = np.zeros((P, NVEC), np.float32)

    def put(name, v):
        c, n = VCOLS[name]
        assert v.shape[1] == n
        vec[0:v.shape[0], c:c + n] = v

    for l in range(2):
        for k in range(2):
            put(f"ffn{2 * l + k}", _col(g["ffn_norm"][l, k]))
        put(f"mix{l}", _col(g["mix_norm"][l]))
    put("norm1", _col(g["norm1_gain_2"][0]))
    put("norm2", _col(g["norm2_gain_2"][0]))
    put("final", _col(g["final_gain_2"]))
    put("b_ada", _col(g["b_ada_2"][0]))
    put("conv_w", _col(g["rg_conv_w"][0]))
    put("conv_b", _col(g["rg_conv_b"][0]))
    put("gate_b", _col(g["rg_gate_b"][0]))
    put("soft", np.concatenate([_col(g["rg_lambda"][0]), np.broadcast_to(g["ret_decay_logit_2"][0].reshape(1, 8), (P, 8))], 1))
    put("qk", np.concatenate([g["fox_qk_norm"][0]] * 2, 1).T)
    put("fox_b", g["fox_fgate_b"][0][:, None])
    mb, b = g["mlstm_gate_bias_2"][0], np.zeros((36, 2), np.float32)
    for d in range(2):
        b[32 * d:32 * d + 4, 0], b[32 * d:32 * d + 4, 1] = mb[2 * d], mb[2 * d + 1]
    put("ml_b", b)
    put("cond", np.stack([_col(g["c_2"][0]), _col(g["c_ctx_2"])], 2).reshape(P, 16))
    out["vec"] = vec
    gw = g["rg_gate_w"][0]
    bd = np.zeros((P, 8, P), np.float32)
    for k in range(2):
        for m in range(4):
            for q in range(2):
                bd[64 * q:64 * q + 64, 4 * k + m, 64 * q:64 * q + 64] = gw[k, 2 * m + q]
    out["c_gates"] = bd
    out["x"] = _tiles(g["x"][0].T, slice(0, S))
    out["ctx"] = _tiles(g["ctx_2"][0].T, slice(0, SC))
    out.update(_constants())
    return {k: np.ascontiguousarray(v) for k, v in out.items()}


def kernel(**inputs):
    import concourse.bacc as _bacc
    from concourse.bass_utils import run_bass_kernel_spmd as _run

    nc = _bacc.Bacc("TRN2", target_bir_lowering=False, num_devices=1)
    arrays, A = {}, {}
    for name, a in _pack(inputs).items():
        arrays["in_" + name] = a
        A[name] = nc.dram_tensor("in_" + name, a.shape, F32, kind="ExternalInput").ap()
    A["out"] = nc.dram_tensor("out_t", (P, KT, S), F32, kind="ExternalOutput").ap()
    build(nc, A)
    got = _run(nc, [arrays], core_ids=[0]).results[0]["out_t"]
    return np.ascontiguousarray(got.transpose(2, 1, 0).reshape(1, S, D))
```

```python
from contextlib import ExitStack

import numpy as np
import concourse.bass as bass
from concourse import mybir

P = 128
D, S, SC = 1024, 512, 256
KT = D // P
FF = 2816
FT = FF // P
UNIT = 2048
UC = 256
FOXH, SBH, HD = 8, 16, 64
NH = 4
TB = S // P
EPS = 1e-6
NEG = -1e30
F32, F32R = mybir.dt.float32, mybir.dt.float32r
ALU, ACT, AX = mybir.AluOpType, mybir.ActivationFunctionType, mybir.AxisListType.X

VCOLS = {}
_n = 0
for _name, _k in (("ffn0", 8), ("ffn1", 8), ("ffn2", 8), ("ffn3", 8), ("mix0", 8), ("mix1", 8), ("norm1", 8),
                  ("norm2", 8), ("final", 8), ("b_ada", 48), ("conv_w", 16), ("conv_b", 4), ("gate_b", 8),
                  ("soft", 12), ("qk", 2), ("fox_b", 1), ("ml_b", 2), ("cond", 16)):
    VCOLS[_name] = (_n, _k)
    _n += _k
NVEC = _n

N_ADA, ADA_PER = 24, 12
FFN_IN, FFN_OUT = 22, 12
FFN_UNITS = FFN_IN + FFN_OUT
FFN_CHUNKS = (8, 8, 6)
U_FFN = [0, 49, 83, 133, 209]
U_HY, U_HYO, U_SB, U_SBO, U_B2, U_B2O = 34, 45, 117, 129, 167, 205
N_UNITS = 243


class Tally:

    def __init__(self, sem):
        self.sem, self.n = sem, 0

    def up(self, k=1):
        self.n += k
        return self.sem, k

    def now(self):
        return self.sem, self.n


HY_VISITS = ([("feat", (n, i)) for n in ("u", "q", "k", "gate") for i in range(2)] + [("gates1", ("f", 0))]
             + [("tok", ("v", i)) for i in range(2)])
SB_VISITS = [("feat", ("q", i)) for i in range(4)] + [("feat", ("k", i)) for i in range(4)] + [("tok", ("v", i)) for i in range(4)]
B2_VISITS = [(kind, (n, i)) for n, kind, k in (
    ("rk", "feat", 2), ("rv", "tok", 2), ("rq", "feat", 2), ("crk", "ctok", 2), ("crv", "ctok", 2), ("cmk", "ctok", 2),
    ("cmv", "ctok", 2), ("cmg", "cgates", 1), ("mg", "gates", 1), ("mk", "feat", 2), ("mv", "tok", 2), ("mq", "feat", 2),
    ("rg", "feat", 2), ("mo", "feat", 2)) for i in range(k)]
V_RET, V_PREP, V_ML = 15, 19, 22
UP_VISITS = [v for h in range(2) for v in [("feat", (n, i)) for n in ("br", "bm") for i in range(2)] + [("up", (n, h)) for n in ("ret", "ml")]]
V_UP = len(B2_VISITS)
B2_VISITS = B2_VISITS + UP_VISITS

N_NORM = {"ffn0": 0, "mix0": 1, "ffn1": 2, "ffn2": 3, "mix1": 4, "ffn3": 5, "norm1": 6, "norm2": 7, "final": 8}


def build(nc, A):
    ctx = ExitStack()
    with ctx:
        def sb(name, shape, dt=F32):
            return ctx.enter_context(nc.sbuf_tensor("sb_" + name, shape, dt))

        def layout(tag, items):
            with ExitStack() as phase:
                return {n: phase.enter_context(nc.sbuf_tensor(f"{tag}_{n}", s, dt)) for n, s, dt in items}

        def sem(name):
            return ctx.enter_context(nc.semaphore(name))

        PS = ctx.enter_context(nc.psum_tensor("PS", [P, 8, 512], F32))
        XT = sb("XT", [P, KT, S])
        HH, HL = sb("HH", [P, KT, S], F32R), sb("HL", [P, KT, S], F32R)
        RAW = [sb(f"RAW{s}", [P, UNIT]) for s in range(2)]
        WH = [sb(f"WH{s}", [P, UNIT], F32R) for s in range(2)]
        WL = [sb(f"WL{s}", [P, UNIT], F32R) for s in range(2)]
        VEC = sb("VEC", [P, NVEC])
        IDENT, ONES = sb("IDENT", [P, P]), sb("ONES", [P, P])
        EPSC = sb("EPSC", [P, 1])
        SQT, SSACC, RINV = sb("SQT", [P, 2, S]), sb("SSACC", [P, S]), sb("RINV", [P, S])
        HT = sb("HT", [P, 2, S])
        SPT = sb("SPT", [P, 8, 12])
        MOD = sb("MOD", [P, 48, 2])
        CSC = sb("CSC", [P, 3, KT])
        QKG = sb("QKG", [P, 2])
        CS = sb("CS", [P, 16])
        LGS = sb("LGS", [P, 20])
        NGC, GCP, WS = sb("NGC", [P, 8]), sb("GCP", [P, 8]), sb("WS", [P, 8, 2])
        CEX, TE = sb("CEX", [P, 4]), sb("TE", [P, 4])
        SIL, G = HT, SQT

        ff = layout("ff", [("GH", [P, FT, S], F32R), ("GL", [P, FT, S], F32R), ("ADAW", [P, 1024], F32), ("ACC", [P, 2, UC], F32)])
        GH, GL, ADAW, ACC = ff["GH"], ff["GL"], ff["ADAW"], ff["ACC"]
        hy = layout("hy", [("UP", [P, 4, S + 4], F32), ("GT", [P, 4, S], F32), ("Q", [P, 4, S], F32), ("K", [P, 4, S], F32),
                           ("V", [P, TB, 512], F32), ("CH", [P, 2, S], F32R), ("XC", [P, 4, S], F32), ("R", [P, 4, S], F32),
                           ("I", [P, 4, S], F32), ("PT", [P, 2, TB, S], F32), ("BD", [P, 8, P], F32), ("B64", [P, P], F32),
                           ("MASK", [P, P], F32R), ("SEL", [P, 8, P], F32R), ("EYE", [P, P], F32R), ("ST", [P, 2, 2 * TB], F32)])
        sbm = layout("sbm", [("Q", [P, 8, S], F32), ("K", [P, 8, S], F32), ("V", [P, TB, D], F32), ("E", [P, 2, 1280], F32),
                             ("SH", [P, 2, 1280], F32R), ("SL", [P, 2, 1280], F32R), ("W", [P, 2, 1280], F32), ("TRI", [P, P], F32R),
                             ("NONE", [P, P], F32R), ("MASK", [P, P], F32R), ("EYE", [P, P], F32R)])
        lead = [("RQ", [P, 4, S], F32), ("MQ", [P, 4, S], F32), ("RK", [P, 4, S], F32), ("RV", [P, TB, 512], F32),
                ("MK", [P, 4, S], F32), ("MV", [P, TB, 512], F32), ("CRK", [P, 2, 512], F32),
                ("CRV", [P, 2, 512], F32), ("CMK", [P, 2, 512], F32), ("CMV", [P, 2, 512], F32)]
        b2 = layout("b2", lead + [("CT", [P, KT, SC], F32), ("HCH", [P, KT, SC], F32R), ("HCL", [P, KT, SC], F32R),
                                  ("ROPE", [P, 2, S], F32), ("SW", [P, 2, S], F32)])
        gr = layout("gr", lead + [("IG", [P, S + SC], F32), ("FG", [P, S + SC], F32)])
        rw = layout("rw", lead + [("CT", [P, KT, SC], F32), ("REL", [P, 896], F32), ("MX", [P, 896], F32), ("POS", [P, S], F32),
                                  ("QF", [P, 2, S], F32), ("SM", [P, TB, S], F32), ("KS", [P, 4, P], F32), ("ST", [P, 2, P], F32)])
        mw = layout("mw", lead + [("MO", [P, 4, S], F32), ("F", [P, S + SC], F32), ("GM", [P, S + SC], F32),
                                  ("AB", [P, S + SC], F32), ("SEL", [P, 8, P], F32), ("GCOL", [P, 6, 36], F32), ("ONE", [P, S], F32),
                                  ("MSK", [P, 2, P], F32), ("KS", [P, 2, 2, P], F32), ("QW", [P, 2, S], F32)])
        ml = layout("ml", lead[:2] + [("W0", [P, TB, S], F32), ("C0", [P, 4, S], F32)] + lead[4:6] + [("W1", [P, TB, S], F32), ("RG", [P, 4, S], F32)])
        po = layout("po", [("MH", [P, KT, S], F32R), ("YH", [P, KT, S], F32R), ("YL", [P, KT, S], F32R), ("ML", [P, KT, S], F32R),
                           ("CT", [P, KT, SC], F32), ("BG", [P, 8, S], F32)])

        def col(name, i=0, n=1, rows=P):
            c = VCOLS[name][0] + i
            return VEC[0:rows, c:c + n]

        def f32(ap):
            return ap.bitcast(F32)

        raw_loaded = [sem(f"raw_loaded{s}") for s in range(2)]
        T = {n: Tally(sem(n)) for n in (
            "vec_in", "x_upd", "const_in", "ada_in", "ada_step", "ada_mm", "ada_mod", "mod_ready", "small", "act_step", "dve_step", "pool_step",
            "w_hi", "w_lo", "visit_done", "evac", "sq_ready", "ss_acc", "ss_sum", "rms_ready", "ht_ready", "hh_ready",
            "h_ready", "silu_ready", "g_mul", "gh_ready", "g_ready", "out_stored",
            "xc_ready", "rg_mm", "rg_sig", "rg_at", "rg_b2", "rg_sq", "y_f32", "y_hi", "y_ready", "up_clear",
            "qk_sq", "qk_ss", "qk_rms", "qk_norm", "f_abs", "f_ln", "c_ready", "c_hi", "c_lo", "fx_const", "sb_const", "sb_sl",
            "fx_s", "fx_max", "fx_exp", "fx_p", "fx_t", "fx_pt", "fx_o",
            "sb_z", "sb_ln", "sb_tri", "sb_exp", "sb_o",
            "csq", "css_acc", "css_sum", "crms", "cht", "chh", "ch_ready", "rope_sw", "rope_done",
            "rt_e", "rt_x", "rt_m", "rt_qx", "rt_q", "rt_ce", "rt_ks", "rt_st", "rt_stc", "rt_s", "rt_sm", "rt_o", "rt_out",
            "ml_abs", "ml_ln", "ml_rows", "ml_gt", "ml_gc", "ml_gcp", "ml_ws", "ml_ks", "ml_c0", "ml_c0c", "ml_s", "ml_g",
            "ml_w", "ml_diag", "ml_qw", "ml_sm", "ml_nd", "ml_h", "hn_in", "hn_sq", "hn_ss", "hn_rms",
            "up_mm", "up_m", "up_hi", "m_ready", "rot_in")}
        X0 = 16

        T["cond_ready"] = Tally(sem("cond_ready"))
        block = ctx.enter_context(nc.Block())
        V0 = {"hy": U_HY, "sb": U_SB, "b2": U_B2}
        EV = {"hy": 0, "sb": len(HY_VISITS)}
        EV["b2"] = EV["sb"] + len(SB_VISITS)

        def ev(k):
            return EV["b2"] + 1 + k - sum(kind == "up" for kind, _ in B2_VISITS[:k])

        RES = {"ffn0": 0, "hy": 1, "ffn1": 2, "ffn2": 3, "sb": 4, "ffn3": 5, "b2": 6, "ffn4": 7}
        Y0 = {"hy": 0, "sb": 8, "b2": 16}
        OFF = {0: 0, 1: 512, 3: 896, 2: 1024}

        def zs(h):
            return PS[:, 3 * (h % 2):3 * (h % 2) + 3, :].rearrange("p b c -> p (b c)")

        def PX(h):
            return hy["R"] if h % 2 == 0 else hy["I"]

        def LA(m):
            return SPT[:, 6, m:m + 1]

        def LAN(m):
            return SPT[:, 6, 4 + m:5 + m]

        def SQC(t):
            return SQT[:, t % 2, 0:SC]

        SSC, RINC = HT[:, 0, 0:SC], HT[:, 1, 0:SC]

        WM = (ml["W0"], ml["W1"])

        def C0N(k):
            return ml["C0"][:, k // 2, 256 * (k % 2):256 * (k % 2) + 256]

        def hy_bank(k):
            return 2 * k if k < 4 else 4 + 2 * (k % 2)

        def bank(k):
            if k < V_RET:
                return 2 * (k % 4)
            if k < V_ML or V_UP <= k < V_UP + 4:
                return 4 + 2 * (k % 2)
            return 6 if k < V_UP else 2 * (k - V_UP - 6)

        def span(d, j):
            return (P * j, S) if d == 0 else (0, P * (j + 1))

        @block.sync
        def _(sp):
            def load(slot, unit):
                sp.dma_start(RAW[slot][:, :], A["weights"][unit]).then_inc(raw_loaded[slot], 16)

            sp.dma_start(XT[:, :, :], A["x"]).then_inc(*T["x_upd"].up(16))
            load(0, 0)
            load(1, 1)
            with sp.Fori(0, (N_UNITS - 2) // 2) as i:
                for s in range(2):
                    sp.wait_ge(T["w_lo"].sem, 2 * i + s + 1)
                    load(s, 2 * i + s + 2)
            sp.wait_ge(T["w_lo"].sem, N_UNITS - 2)
            load((N_UNITS - 1) % 2, N_UNITS - 1)
            sp.wait_ge(T["ht_ready"].sem, 8 * 8 + 8)
            sp.dma_start(A["out"], XT[:, :, :]).then_inc(*T["out_stored"].up(16))
            sp.wait_ge(*T["out_stored"].now())

        @block.gpsimd
        def _(pool):
            def const(dst, src):
                pool.dma_start(dst, src).then_inc(*T["const_in"].up(16))

            def conditioning(f):
                def half(u, h):
                    pool.dma_start(ADAW[:, :], A["w_ada"][u, :, 1024 * h:1024 * h + 1024]).then_inc(*T["ada_in"].up(16))

                half(ADA_PER * f, 0)
                with pool.Fori(0, ADA_PER - 1) as i:
                    pool.wait_ge(T["ada_step"].sem, 16 * i + (16 * ADA_PER * f + 8))
                    half(i + ADA_PER * f, 1)
                    pool.wait_ge(T["ada_step"].sem, 16 * i + (16 * ADA_PER * f + 16))
                    half(i + (ADA_PER * f + 1), 0)
                pool.wait_ge(T["ada_step"].sem, 16 * ADA_PER * (f + 1) - 8)
                half(ADA_PER * (f + 1) - 1, 1)

            conditioning(0)
            pool.wait_ge(T["ada_mod"].sem, ADA_PER)
            pool.wait_ge(T["visit_done"].sem, U_HY)
            pool.memset(hy["UP"][:, :, 0:4], 0.0).then_inc(*T["up_clear"].up())
            const(hy["BD"][:, :, :], A["c_gates"])
            const(hy["B64"][:, :], A["c_b64"])
            const(hy["PT"][:, 1, 2, 0:P], A["c_causal"])
            const(hy["PT"][:, 1, 0:2, :], A["c_sel_fox"])
            pool.wait_ge(T["visit_done"].sem, U_FFN[1])
            conditioning(1)
            pool.wait_ge(T["visit_done"].sem, U_SB)
            for n, (name, src) in enumerate((("TRI", "c_tri"), ("NONE", "c_negones"), ("MASK", "c_strict"))):
                const(sbm["W"][:, 0, P * n:P * n + P], A[src])
            pool.wait_ge(T["visit_done"].sem, U_B2)
            const(b2["CT"][:, :, :], A["ctx"])
            const(b2["ROPE"][:, :, :], A["c_rope"])
            pool.wait_ge(T["rope_done"].sem, 8)
            pool.wait_ge(T["visit_done"].sem, U_B2 + V_RET)
            const(rw["REL"][:, :], A["c_rel"])
            const(rw["POS"][:, :], A["c_pos"])
            pool.wait_ge(T["rt_out"].sem, 4)
            const(mw["SEL"][:, :, :], A["c_sel_ml"])
            const(mw["MSK"][:, :, :], A["c_msk_ml"])

        @block.scalar
        def _(act):
            st, sm = T["act_step"], T["small"]

            def split_hi(slot, free):
                if free is not None:
                    act.wait_ge(T["visit_done"].sem, free)
                act.activation(WH[slot][:, :], RAW[slot][:, :], ACT.Copy).then_inc(*T["w_hi"].up())

            def split(u):
                if u < N_UNITS:
                    act.wait_ge(raw_loaded[u % 2], 16 * (u // 2 + 1))
                    split_hi(u % 2, u - 1 if u >= 2 else None)

            def split_at(base, per, i, off):
                u = base + off
                free = per * i + (base + off - 1)
                act.wait_ge(raw_loaded[u % 2], per * 8 * i + 16 * (u // 2 + 1))
                split_hi(u % 2, free if not isinstance(free, int) or free > 0 else None)

            def logs_table():
                act.preload_act_table_set("natural_log_exp_and_others")

            def root_inverse(dst, src, width):
                act.activation(dst, src, ACT.Ln, scale=1.0 / width, bias=EPSC[:, 0:1]).then_inc(*st.up())
                act.wait_ge(*st.now())
                return act.activation(dst, dst, ACT.Exp, scale=-0.5)

            def norm(m, shift=None):
                logs_table()
                act.wait_ge(T["ss_sum"].sem, m + 1)
                root_inverse(RINV[:, :], PS[:, 4, :], D).then_inc(*T["rms_ready"].up())
                if m == N_NORM["final"]:
                    return
                for kt in range(KT):
                    act.wait_ge(T["ht_ready"].sem, 8 * m + kt + 1)
                    if shift is None:
                        ins = act.activation(HH[:, kt, :], HT[:, kt % 2, :], ACT.Copy)
                    else:
                        ins = act.activation(HH[:, kt, :], HT[:, kt % 2, :], ACT.Identity, bias=shift(kt))
                    ins.then_inc(*T["hh_ready"].up())

            def ffn(n, shift=None):
                u0, v0 = U_FFN[n], U_FFN[n]
                norm(N_NORM[("ffn0", "ffn1", "ffn2", "ffn3", "norm2")[n]], shift)

                def high_g(i):
                    act.wait_ge(T["g_mul"].sem, 22 * n + 2 * i + 2)
                    for m in range(2):
                        last = act.activation(GH[:, 2 * i + m, :], G[:, m, :], ACT.Copy)
                    last.then_inc(*T["gh_ready"].up())

                def pair(i, first):
                    split_at(u0, 2, i, 1)
                    if not first:
                        high_g(i - 1)
                    split_at(u0, 2, i, 2)
                    act.wait_ge(T["visit_done"].sem, 2 * i + v0 + 1)
                    for m in range(2):
                        act.activation(SIL[:, m, :], PS[:, m, :], ACT.Silu).then_inc(*T["silu_ready"].up())

                pair(0, True)
                with act.Fori(1, FFN_IN // 2) as i:
                    pair(i, False)
                high_g(FFN_IN // 2 - 1)
                residual(RES[f"ffn{n}"], u0 + FFN_IN, 3, n < 4)

            def residual(r, u0, chunks, loop):
                def group(i, j):
                    for c in range(chunks):
                        if not (isinstance(i, int) and u0 + chunks * (2 * i + j) + c + 1 >= N_UNITS):
                            split_at(u0, 2 * chunks, i, chunks * j + c + 1)
                    for m in range(2):
                        act.wait_ge(T["x_upd"].sem, 4 * i + X0 + 8 * r + 2 * j + m + 1)
                        act.wait_ge(T["ss_acc"].sem, 4 * i + 8 * (r + 1) + 2 * j + m - 1)
                        act.activation(SQT[:, m, :], XT[:, 4 * i + 2 * j + m, :], ACT.Square).then_inc(*T["sq_ready"].up())

                if loop:
                    with act.Fori(0, 2) as i:
                        group(i, 0)
                        group(i, 1)
                else:
                    for i in range(2):
                        group(i, 0)
                        group(i, 1)

            def visits(name, vis, evacuate):
                for k, (kind, what) in enumerate(vis):
                    split(V0[name] + k + 1)
                    act.wait_ge(T["visit_done"].sem, V0[name] + k + 1)
                    evacuate(kind, what, 2 * (k % 4)).then_inc(*T["evac"].up())

            def feat(dst, i, b, func=ACT.Copy, scale=1.0):
                for m in range(2):
                    last = act.activation(dst[:, 2 * i + m, :], PS[:, b + m, :], func, scale=scale)
                return last

            def tok(dst, i, b, blocks=TB, scale=1.0):
                for t in range(0, blocks, 2):
                    last = act.activation(dst[:, t:t + 2, UC * i:UC * i + UC],
                                          PS[:, b + t // 2, :].rearrange("p (t c) -> p t c", t=2), ACT.Copy, scale=scale)
                return last

            act.dma_start(VEC[:, :], A["vec"]).then_inc(*T["vec_in"].up(16))
            act.dma_start(IDENT[:, :], A["c_ident"]).then_inc(*T["vec_in"].up(16))
            act.dma_start(ONES[:, :], A["c_ones"]).then_inc(*T["vec_in"].up(16))
            act.dma_start(CEX[:, :], A["c_cex"]).then_inc(*T["vec_in"].up(16))
            act.wait_ge(*T["vec_in"].now())
            act.activation(CS[:, :], col("cond", 0, 16), ACT.Silu).then_inc(*T["cond_ready"].up())
            act.wait_ge(sm.sem, 1)
            act.activation(SPT[:, 1, :], SPT[:, 0, :], ACT.Exp, scale=-1.0).then_inc(*sm.up())
            act.wait_ge(sm.sem, 3)
            act.activation(SPT[:, 3, :], SPT[:, 2, :], ACT.Ln).then_inc(*sm.up())
            act.wait_ge(T["x_upd"].sem, X0)
            for t in range(KT):
                if t >= 2:
                    act.wait_ge(T["ss_acc"].sem, t - 1)
                act.activation(SQT[:, t % 2, :], XT[:, t, :], ACT.Square).then_inc(*T["sq_ready"].up())
            split(0)
            ffn(0)

            norm(N_NORM["mix0"])
            act.wait_ge(T["up_clear"].sem, 1)

            def take(k):
                (name, i), b = HY_VISITS[k][1], hy_bank(k)
                split(U_HY + k + 1)
                act.wait_ge(T["visit_done"].sem, U_HY + k + 1)
                if name == "u":
                    for m in range(2):
                        last = act.activation(hy["UP"][:, 2 * i + m, 4:S + 4], PS[:, b + m, :], ACT.Copy)
                elif name == "gate":
                    last = feat(hy["GT"], i, b, ACT.Gelu_apprx_tanh)
                elif name == "v":
                    last = tok(hy["V"], i, b)
                elif name == "f":
                    last = act.activation(hy["PT"][0:8, 0, 2, :], PS[0:8, b, :], ACT.Identity, bias=col("fox_b", rows=8))
                else:
                    last = feat(hy[name.upper()], i, b)
                last.then_inc(*T["evac"].up())

            def gate(g, dst):
                for m in range(4):
                    act.wait_ge(T["rg_mm"].sem, 4 * g + m + 1)
                    act.activation(dst[:, m, :], PS[:, m, :], ACT.Sigmoid, bias=col("gate_b", 4 * g + m)).then_inc(*T["rg_sig"].up())

            def squares(t0):
                for t in (t0, t0 + 1):
                    src = (hy["Q"] if t < 4 else hy["K"])[:, t % 4, :]
                    if t >= 2:
                        act.wait_ge(T["qk_ss"].sem, t - 1)
                    act.activation(SQT[:, t % 2, :], src, ACT.Square).then_inc(*T["qk_sq"].up())

            def roots(t0):
                logs_table()
                for t in (t0, t0 + 1):
                    act.wait_ge(T["qk_ss"].sem, t + 1)
                    if t >= 2:
                        act.wait_ge(T["qk_norm"].sem, t - 1)
                    else:
                        act.wait_ge(T["rg_b2"].sem, 4)
                    root_inverse(HT[:, t % 2, :], PS[:, t % 2, :], HD).then_inc(*T["qk_rms"].up())

            for k in range(5):
                take(k)
            gate(0, hy["R"])
            take(5)
            gate(1, hy["I"])
            act.wait_ge(*T["rg_sig"].now())
            act.wait_ge(T["xc_ready"].sem, 4)
            for m in range(4):
                act.activation(hy["UP"][:, m, 0:S], hy["R"][:, m, :], ACT.Exp, scale=LA(m)).then_inc(*st.up())
            act.wait_ge(*st.now())
            for m in range(4):
                act.activation(hy["R"][:, m, :], hy["R"][:, m, :], ACT.Tanh, scale=LAN(m)).then_inc(*T["rg_at"].up())
            squares(0)
            take(6)
            roots(0)
            squares(2)
            take(7)
            roots(2)
            squares(4)
            for m in range(4):
                act.wait_ge(T["rg_b2"].sem, m + 1)
                act.activation(hy["R"][:, m, :], hy["R"][:, m, :], ACT.Sqrt).then_inc(*T["rg_sq"].up())
            take(8)
            roots(4)
            squares(6)
            take(9)
            roots(6)
            act.wait_ge(T["f_abs"].sem, 1)
            fa = hy["PT"][0:8, 0, 0, :]
            act.activation(fa, fa, ACT.Exp, scale=-1.0).then_inc(*st.up())
            act.wait_ge(*st.now())
            act.activation(fa, fa, ACT.Ln, bias=1.0).then_inc(*T["f_ln"].up())
            act.wait_ge(T["const_in"].sem, 16 * 4)
            act.activation(hy["MASK"][:, :], hy["PT"][:, 1, 2, 0:P], ACT.Copy)
            act.activation(hy["EYE"][:, :], IDENT[:, :], ACT.Copy)
            act.activation(hy["SEL"][:, :, :].rearrange("p h q -> p (h q)"), hy["PT"][:, 1, 0:2, :].rearrange("p a c -> p (a c)"), ACT.Copy)\
                .then_inc(*T["fx_const"].up())
            take(10)
            act.wait_ge(T["c_ready"].sem, 1)
            act.activation(hy["CH"][:, 0, :], hy["PT"][:, 0, 3, :], ACT.Copy).then_inc(*T["c_hi"].up())
            for m in range(4):
                act.wait_ge(T["y_f32"].sem, m + 1)
                act.activation(HH[:, m, :], hy["XC"][:, m, :], ACT.Copy).then_inc(*T["y_hi"].up())

            def fox_exp(h):
                for i in range(TB):
                    act.wait_ge(T["fx_max"].sem, TB * h + i + 1)
                    w = P * (i + 1)
                    act.activation(PX(h)[:, i, 0:w], PS[:, i, 0:w], ACT.Exp, bias=hy["ST"][:, h % 2, i:i + 1],
                                   accum_out=hy["ST"][:, h % 2, TB + i:TB + i + 1]).then_inc(*T["fx_exp"].up())

            def fox_pt(h):
                for j in range(TB):
                    act.wait_ge(T["fx_t"].sem, TB * h + j + 1)
                    if h >= 2:
                        act.wait_ge(T["fx_o"].sem, h - 1)
                    w = S - P * j
                    act.activation(hy["PT"][:, h % 2, j, 0:w], PS[:, 4 + j % 2, 0:w], ACT.Copy).then_inc(*T["fx_pt"].up())
                if h % 2:
                    act.wait_ge(T["fx_o"].sem, h + 1)
                    act.activation(HH[:, 4 + h // 2, :], PS[:, 6 + h // 2 % 2, :], ACT.Copy).then_inc(*T["y_hi"].up())

            for h in range(FOXH):
                fox_exp(h)
                fox_pt(h)
            residual(RES["hy"], U_HYO, 1, True)
            ffn(1)
            ffn(2)

            norm(N_NORM["mix1"])
            visits("sb", SB_VISITS, lambda kind, what, b: tok(sbm["V"], what[1], b) if what[0] == "v" else
                   feat(sbm[what[0].upper()], what[1], b, scale=HD ** -0.5 if what[0] == "q" else 1.0))

            act.wait_ge(T["const_in"].sem, 16 * 7)
            for n, name in enumerate(("TRI", "NONE", "MASK")):
                act.activation(sbm[name][:, :], sbm["W"][:, 0, P * n:P * n + P], ACT.Copy)
            act.activation(sbm["EYE"][:, :], IDENT[:, :], ACT.Copy).then_inc(*T["sb_const"].up())

            def sb_logs(h):
                E = sbm["E"][:, h % 2, :]
                act.wait_ge(T["sb_z"].sem, h + 1)
                if h >= 2:
                    act.wait_ge(T["sb_sl"].sem, h - 1)
                act.activation(E, zs(h)[:, 0:1280], ACT.Abs).then_inc(*st.up())
                act.wait_ge(*st.now())
                act.activation(E, E, ACT.Exp, scale=-1.0).then_inc(*st.up())
                act.wait_ge(*st.now())
                act.activation(E, E, ACT.Ln, bias=1.0).then_inc(*T["sb_ln"].up())

            def sb_weights(h):
                act.wait_ge(T["sb_tri"].sem, h + 1)
                if h == 0:
                    act.wait_ge(*T["sb_const"].now())
                if h >= 2:
                    act.wait_ge(T["sb_o"].sem, h - 1)
                act.activation(sbm["W"][:, h % 2, :], zs(h)[:, 0:1280], ACT.Exp).then_inc(*T["sb_exp"].up())

            def sb_out(h):
                if h % 2:
                    act.wait_ge(T["sb_o"].sem, h + 1)
                    act.activation(HH[:, h // 2, :], PS[:, 6 + h // 2 % 2, :], ACT.Copy).then_inc(*T["y_hi"].up())

            logs_table()
            sb_logs(0)
            for h in range(SBH):
                if h + 1 < SBH:
                    sb_logs(h + 1)
                sb_weights(h)
                if h >= 1:
                    sb_out(h - 1)
            sb_out(SBH - 1)
            residual(RES["sb"], U_SBO, 1, True)
            ffn(3)

            norm(N_NORM["norm1"], lambda kt: MOD[:, kt, 0:1])
            rots = [0]

            def prepare(k):
                split(U_B2 + k + 1)

            def take(k):
                (name, i), b = B2_VISITS[k][1], bank(k)
                act.wait_ge(T["visit_done"].sem, U_B2 + k + 1)
                if name in ("rq", "rk"):
                    scale = P ** -0.5 if name == "rk" else 1.0
                    for m in range(2):
                        if rots[0]:
                            act.wait_ge(T["rope_done"].sem, rots[0])
                        act.activation(b2[name.upper()][:, 2 * i + m, :], PS[:, b + m, :], ACT.Copy, scale=scale)
                        act.activation(b2["SW"][0:64, 0, :], PS[64:128, b + m, :], ACT.Copy, scale=scale)
                        last = act.activation(b2["SW"][64:128, 0, :], PS[0:64, b + m, :], ACT.Copy, scale=scale)
                        rots[0] += 1
                        if m == 0:
                            last.then_inc(*T["rope_sw"].up())
                elif name in ("cmg", "mg"):
                    lo, w = (0, SC) if name == "cmg" else (SC, S)
                    act.activation(gr["IG"][0:36, lo:lo + w], PS[0:36, b, 0:w], ACT.Identity, bias=col("ml_b", 0, rows=36))
                    last = act.activation(gr["FG"][0:36, lo:lo + w], PS[0:36, b + 1, 0:w], ACT.Identity, bias=col("ml_b", 1, rows=36))
                elif name == "rg":
                    last = feat(ml["RG"], i, b, ACT.Silu)
                elif name == "mo":
                    last = feat(mw["MO"], i, b, ACT.Sigmoid)
                elif name in ("br", "bm"):
                    last = feat(po["BG"], i % 2 + (2 if name == "bm" else 0), b, ACT.Sigmoid)
                else:
                    kind, scale = B2_VISITS[k][0], P ** -0.5 if name in ("crk", "mk", "cmk") else 1.0
                    if kind == "feat":
                        last = feat(b2[name.upper()], i, b, scale=scale)
                    else:
                        last = tok(b2[name.upper()], i, b, TB if kind == "tok" else 2, scale)
                last.then_inc(*T["evac"].up())

            prepare(0)
            for k in range(V_RET):
                if k == 2:
                    act.wait_ge(T["const_in"].sem, 16 * 9)
                    act.wait_ge(T["ss_acc"].sem, 8 * (N_NORM["norm1"] + 1))
                    for t in range(KT):
                        if t >= 2:
                            act.wait_ge(T["css_acc"].sem, t - 1)
                        act.activation(SQC(t), b2["CT"][:, t, :], ACT.Square).then_inc(*T["csq"].up())
                if k == 4:
                    logs_table()
                    act.wait_ge(T["css_sum"].sem, 1)
                    root_inverse(RINC, PS[:, 4, 0:SC], D).then_inc(*T["crms"].up())
                    for t in range(KT):
                        act.wait_ge(T["cht"].sem, t + 1)
                        act.activation(b2["HCH"][:, t, :], SQC(t), ACT.Identity, bias=MOD[:, t, 1:2]).then_inc(*T["chh"].up())
                take(k)
                prepare(k + 1)

            def retained(h):
                act.wait_ge(T["rt_o"].sem, h + 1)
                act.activation(b2["RQ"][:, h, :], PS[:, 3, :], ACT.Copy).then_inc(*T["rt_out"].up())

            for h in range(NH):
                act.wait_ge(T["rt_e"].sem, h + 1)
                act.activation(rw["MX"][:, :], rw["MX"][:, :], ACT.Exp).then_inc(*T["rt_x"].up())
                if h:
                    retained(h - 1)
                act.activation(rw["QF"][:, 0, :], rw["POS"][:, :], ACT.Exp, scale=LGS[:, h:h + 1]).then_inc(*T["rt_qx"].up())
                act.activation(rw["QF"][:, 1, :], rw["POS"][:, :], ACT.Exp, scale=LGS[:, 12 + h:13 + h],
                               bias=LGS[:, 16 + h:17 + h]).then_inc(*T["rt_qx"].up())
                if h:
                    act.wait_ge(T["rt_ks"].sem, h)
                act.activation(TE[:, 0:2], CEX[:, 0:2], ACT.Exp, scale=LGS[:, h:h + 1])
                act.activation(TE[:, 2:4], CEX[:, 2:4], ACT.Exp, scale=LGS[:, 4 + h:5 + h]).then_inc(*T["rt_ce"].up())
                take(V_RET + h)
                act.wait_ge(T["rt_st"].sem, h + 1)
                act.activation(rw["ST"][:, :, :].rearrange("p d v -> p (d v)"), PS[:, 2, 0:2 * P], ACT.Copy).then_inc(*T["rt_stc"].up())
                prepare(V_RET + h + 1)
            retained(NH - 1)

            act.wait_ge(T["ml_abs"].sem, 1)
            act.activation(mw["AB"][0:36, :], mw["AB"][0:36, :], ACT.Exp, scale=-1.0).then_inc(*st.up())
            act.wait_ge(*st.now())
            act.activation(mw["AB"][0:36, :], mw["AB"][0:36, :], ACT.Ln, bias=1.0).then_inc(*T["ml_ln"].up())
            take(V_PREP)
            prepare(V_PREP + 1)
            act.wait_ge(T["ml_gt"].sem, 1)
            act.activation(mw["GCOL"][:, :, :].rearrange("p a b -> p (a b)"), PS[:, 0, 0:216], ACT.Copy)
            act.activation(NGC[:, :], PS[:, 1, 0:8], ACT.Copy)
            act.activation(GCP[:, :], PS[:, 1, 0:8], ACT.Copy, scale=-1.0).then_inc(*T["ml_gc"].up())
            act.wait_ge(*T["ml_gc"].now())
            for k in range(2 * NH):
                r = 32 * (k % 2) + k // 2
                act.activation(WS[:, k, :], mw["GCOL"][:, 0:2, r], ACT.Exp, bias=NGC[:, k:k + 1]).then_inc(*T["ml_ws"].up())
            take(V_PREP + 1)
            prepare(V_PREP + 2)
            for h in range(NH):
                act.wait_ge(T["ml_c0"].sem, 2 * h + 2)
                act.activation(ml["C0"][:, h, :], PS[:, h, :], ACT.Copy).then_inc(*T["ml_c0c"].up())
            take(V_PREP + 2)
            prepare(V_PREP + 3)

            for k in range(2 * NH):
                h, d = k // 2, k % 2
                act.wait_ge(T["ml_diag"].sem, k + 1)
                if k >= 2:
                    act.wait_ge(T["ml_h"].sem, k - 1)
                for j in range(TB):
                    lo, hi = (P * (j + 1), S) if d == 0 else (0, P * j)
                    r = 32 * d + h
                    if hi > lo:
                        act.activation(WM[d][:, j, lo:hi], PS[:, 2, lo:hi], ACT.Exp, bias=mw["GCOL"][:, 2 + j, r:r + 1])
                flat = WM[d][:, :, :].rearrange("p j t -> p (j t)")
                for ap in (flat[:, 0:1920].rearrange("p (a c) -> p a c", a=3)[:, :, 0:P], flat[:, 1920:2048]):
                    act.activation(ap, ap, ACT.Exp)
                act.activation(SQT[:, d, :], PS[:, 2, :], ACT.Exp, bias=GCP[:, k:k + 1])
                act.activation(HT[:, d, :], PS[:, 3, :], ACT.Exp).then_inc(*T["ml_w"].up())
                if d:
                    take(V_ML + h)
                    prepare(V_ML + h + 1)

            for t in range(0, 8, 2):
                srcs = [b2["RQ" if t < 4 else "MQ"][:, (t + m) % 4, :] for m in range(2)]
                for m in range(2):
                    act.wait_ge(T["hn_in"].sem, t + m - 3 if t >= 4 else 1)
                    if t:
                        act.wait_ge(T["hn_ss"].sem, t + m - 1)
                    act.activation(SQT[:, m, :], srcs[m], ACT.Square).then_inc(*T["hn_sq"].up())
                take(V_UP + t // 2)
                prepare(V_UP + t // 2 + 1)
                logs_table()
                for m in range(2):
                    act.wait_ge(T["hn_ss"].sem, t + m + 1)
                    if t:
                        act.wait_ge(T["y_f32"].sem, 4 + t + m - 1)
                    root_inverse(HT[:, m, :], PS[:, m, :], P).then_inc(*T["hn_rms"].up())
                for m in range(2):
                    act.wait_ge(T["y_f32"].sem, 4 + t + m + 1)
                    act.activation(po["YH"][:, t + m, :], srcs[m], ACT.Copy).then_inc(*T["y_hi"].up())
            for i in range(2):
                k = V_UP + 6 * i
                if i:
                    for q in range(4):
                        take(k + q)
                        prepare(k + q + 1)
                prepare(k + 5)
                for m in range(4):
                    act.wait_ge(T["up_m"].sem, 4 * i + m + 1)
                    act.activation(po["MH"][:, 4 * i + m, :], SQT[:, m % 2, :], ACT.Copy).then_inc(*T["up_hi"].up())
                if i == 0:
                    prepare(k + 6)
            residual(RES["b2"], U_B2O, 1, False)
            ffn(4, lambda kt: MOD[:, 24 + kt, 0:1])
            norm(N_NORM["final"])

        @block.vector
        def _(dve):
            st, sm = T["dve_step"], T["small"]

            def split_lo(slot, u):
                dve.wait_ge(T["w_hi"].sem, u + 1)
                dve.tensor_tensor(WL[slot][:, :], RAW[slot][:, :], f32(WH[slot][:, :]), ALU.subtract).then_inc(*T["w_lo"].up())

            def split(u):
                if u < N_UNITS:
                    split_lo(u % 2, u)

            def split_at(base, per, i, off):
                split_lo((base + off) % 2, per * i + (base + off))

            def step(ins):
                ins.then_inc(*st.up())
                dve.wait_ge(*st.now())

            def norm(m, gain, shift=None):
                dve.wait_ge(T["rms_ready"].sem, m + 1)
                final = m == N_NORM["final"]

                def scaled(kt):
                    dst = XT[:, kt, :] if final else HT[:, kt % 2, :]
                    if kt >= 2 and not final:
                        dve.wait_ge(T["h_ready"].sem, 8 * m + kt - 1)
                    dve.scalar_tensor_tensor(dst, XT[:, kt, :], gain(kt), RINV[:, :], ALU.mult, ALU.mult).then_inc(*T["ht_ready"].up())

                def low(kt):
                    dve.wait_ge(T["hh_ready"].sem, 8 * m + kt + 1)
                    if shift is None:
                        ins = dve.tensor_tensor(HL[:, kt, :], HT[:, kt % 2, :], f32(HH[:, kt, :]), ALU.subtract)
                    else:
                        ins = dve.scalar_tensor_tensor(HL[:, kt, :], HT[:, kt % 2, :], shift(kt), f32(HH[:, kt, :]), ALU.add, ALU.subtract)
                    ins.then_inc(*T["h_ready"].up())

                scaled(0)
                for kt in range(KT):
                    if kt + 1 < KT:
                        scaled(kt + 1)
                    if not final:
                        low(kt)

            def sum_square(count, slot):
                dve.wait_ge(T["sq_ready"].sem, count + 1)
                dve.wait_ge(T["ss_acc"].sem, count)
                dve.tensor_tensor(SSACC[:, :], SSACC[:, :], SQT[:, slot, :], ALU.add).then_inc(*T["ss_acc"].up())

            def conditioning(u, first=False):
                for k in range(KT):
                    if k % 4 == 0:
                        dve.wait_ge(T["ada_in"].sem, 32 * u + 4 * k + 16)
                    for j in range(2):
                        w, c = ADAW[:, UC * (k % 4):UC * (k % 4) + UC], CS[:, 2 * k + j:2 * k + j + 1]
                        if k == 0:
                            if not first:
                                dve.wait_ge(T["ada_mm"].sem, u)
                            ins = dve.tensor_scalar(ACC[:, j, :], w, c, None, ALU.mult)
                        else:
                            dve.wait_ge(T["ada_step"].sem, 16 * u + (2 * k + j - 1))
                            ins = dve.scalar_tensor_tensor(ACC[:, j, :], w, c, ACC[:, j, :], ALU.mult, ALU.add)
                        ins.then_inc(T["ada_step"].sem, 1)

            def modulation(i, base):
                dve.wait_ge(T["ada_mm"].sem, i + (base + 1))
                for m in range(2):
                    ins = dve.tensor_copy(MOD[:, 2 * i + (2 * base + m), :], PS[:, 7, 2 * m:2 * m + 2])
                ins.then_inc(T["ada_mod"].sem, 1)

            def ffn(n, gain, shift=None, scale=0.5):
                u0 = U_FFN[n]
                norm(N_NORM[("ffn0", "ffn1", "ffn2", "ffn3", "norm2")[n]], gain, shift)

                def gated(i):
                    if not isinstance(i, int) or 22 * n + 2 * i > 0:
                        dve.wait_ge(T["g_ready"].sem, 2 * i + 22 * n)
                    for m in range(2):
                        dve.wait_ge(T["silu_ready"].sem, 2 * i + 22 * n + m + 1)
                        if m == 0:
                            dve.wait_ge(T["visit_done"].sem, 2 * i + u0 + 2)
                        dve.tensor_tensor(G[:, m, :], PS[:, 2 + m, :], SIL[:, m, :], ALU.mult).then_inc(*T["g_mul"].up())
                    dve.wait_ge(T["gh_ready"].sem, i + 11 * n + 1)
                    for m in range(2):
                        dve.tensor_tensor(GL[:, 2 * i + m, :], G[:, m, :], f32(GH[:, 2 * i + m, :]), ALU.subtract).then_inc(*T["g_ready"].up())

                def pair(i, first):
                    split_at(u0, 2, i, 1)
                    if not first:
                        gated(i - 1)
                    split_at(u0, 2, i, 2)
                    if n < N_ADA // ADA_PER:
                        if first:
                            conditioning(ADA_PER * n, n == 0)
                            modulation(0, ADA_PER * n)
                            conditioning(ADA_PER * n + 1)
                        else:
                            modulation(i, ADA_PER * n)
                            conditioning(i + (ADA_PER * n + 1))

                pair(0, True)
                with dve.Fori(1, FFN_IN // 2) as i:
                    pair(i, False)
                gated(FFN_IN // 2 - 1)
                if n < N_ADA // ADA_PER:
                    modulation(ADA_PER - 1, ADA_PER * n)
                residual(RES[f"ffn{n}"], u0 + FFN_IN, 3, n < 4, scale)

            def residual(r, u0, chunks, loop, scale):
                dve.memset(SSACC[:, :], 0.0).then_inc(*st.up())
                cleared = st.n

                def group(i, j):
                    for c in range(chunks):
                        if not (isinstance(i, int) and u0 + chunks * (2 * i + j) + c + 1 >= N_UNITS):
                            split_at(u0, 2 * chunks, i, chunks * j + c + 1)
                    dve.wait_ge(T["visit_done"].sem, 2 * chunks * i + (u0 + chunks * (j + 1)))
                    for m in range(2):
                        t = 4 * i + 2 * j + m
                        dve.scalar_tensor_tensor(XT[:, t, :], PS[:, 4 + 2 * j + m, :], scale if isinstance(scale, float) else scale(t),
                                                 XT[:, t, :], ALU.mult, ALU.add).then_inc(*T["x_upd"].up())
                    dve.wait_ge(st.sem, cleared)
                    for m in range(2):
                        sum_square(4 * i + (8 * (r + 1) + 2 * j + m), m)

                if loop:
                    with dve.Fori(0, 2) as i:
                        group(i, 0)
                        group(i, 1)
                else:
                    for i in range(2):
                        group(i, 0)
                        group(i, 1)

            step(dve.memset(EPSC[:, :], EPS))
            step(dve.memset(SSACC[:, :], 0.0))
            dve.wait_ge(T["vec_in"].sem, 64)
            dve.wait_ge(T["cond_ready"].sem, 1)
            Z = col("soft", 0, 12)
            a, e, u, l, d, t, la, sp = (SPT[:, k, :] for k in range(8))
            dve.scalar_tensor_tensor(a, Z, -1.0, Z, ALU.mult, ALU.max).then_inc(*sm.up())
            dve.wait_ge(sm.sem, 2)
            sm.n = 2
            dve.tensor_scalar(u, e, 1.0, None, ALU.add).then_inc(*sm.up())
            dve.wait_ge(sm.sem, 4)
            step(dve.tensor_scalar(d, u, -1.0, 1e-7, ALU.add, ALU.max))
            step(dve.reciprocal(d, d))
            step(dve.tensor_tensor(l, l, e, ALU.mult))
            step(dve.tensor_tensor(l, l, d, ALU.mult))
            step(dve.scalar_tensor_tensor(t, u, 1.0, e, ALU.is_equal, ALU.mult))
            step(dve.tensor_tensor(l, l, t, ALU.add))
            step(dve.tensor_scalar(t, Z, -1.0, 0.0, ALU.mult, ALU.max))
            step(dve.tensor_tensor(sp, t, l, ALU.add))
            step(dve.tensor_scalar(SPT[:, 6, 0:4], SPT[:, 7, 0:4], -8.0, None, ALU.mult))
            step(dve.tensor_scalar(SPT[:, 6, 4:8], SPT[:, 7, 0:4], 8.0, None, ALU.mult))
            step(dve.tensor_scalar(LGS[:, 0:8], SPT[:, 7, 4:12], -1.0, None, ALU.mult))
            step(dve.tensor_copy(LGS[:, 8:16], SPT[:, 7, 4:12]))
            step(dve.tensor_scalar(LGS[:, 16:20], SPT[:, 7, 8:12], -(S + 1.0), None, ALU.mult))
            step(dve.tensor_scalar(QKG[:, 0:1], col("qk", 0), HD ** -0.5, None, ALU.mult))
            step(dve.tensor_copy(QKG[:, 1:2], col("qk", 1)))
            for t_ in range(KT):
                sum_square(t_, t_ % 2)
            split(0)
            ffn(0, lambda kt: col("ffn0", kt))

            norm(N_NORM["mix0"], lambda kt: col("mix0", kt))
            XC, R, I, UP = hy["XC"], hy["R"], hy["I"], hy["UP"]
            F1, F2, F0, C = hy["PT"][0:8, 0, 0, :], hy["PT"][0:8, 0, 1, :], hy["PT"][0:8, 0, 2, :], hy["PT"][:, 0, 3, :]

            def prepare(k):
                split(U_HY + k + 1)

            def convolve(m):
                taps = [UP[:, m, 1 + j:1 + j + S] for j in range(4)]
                step(dve.tensor_scalar(XC[:, m, :], taps[0], col("conv_w", m), col("conv_b", m), ALU.mult, ALU.add))
                for j in range(1, 4):
                    ins = dve.scalar_tensor_tensor(XC[:, m, :], taps[j], col("conv_w", 4 * j + m), XC[:, m, :], ALU.mult, ALU.add)
                    if j < 3:
                        step(ins)
                ins.then_inc(*T["xc_ready"].up())

            def gain(m):
                dve.wait_ge(T["rg_at"].sem, m + 1)
                if m:
                    dve.wait_ge(*T["rg_b2"].now())
                step(dve.tensor_tensor(HT[:, 0, :], UP[:, m, 0:S], UP[:, m, 0:S], ALU.mult))
                dve.scalar_tensor_tensor(R[:, m, :], HT[:, 0, :], 1.0, R[:, m, :], ALU.add, ALU.mult).then_inc(*T["rg_b2"].up())

            def recur(m):
                dve.wait_ge(T["rg_sq"].sem, m + 1)
                step(dve.tensor_tensor(I[:, m, :], I[:, m, :], R[:, m, :], ALU.mult))
                step(dve.tensor_tensor_scan(XC[:, m, :], UP[:, m, 0:S], I[:, m, :], 0.0, ALU.mult, ALU.add))
                dve.tensor_tensor(XC[:, m, :], XC[:, m, :], hy["GT"][:, m, :], ALU.mult).then_inc(*T["y_f32"].up())

            def normed(t):
                dst = (hy["Q"] if t < 4 else hy["K"])[:, t % 4, :]
                dve.wait_ge(T["qk_rms"].sem, t + 1)
                dve.scalar_tensor_tensor(dst, dst, QKG[:, t // 4:t // 4 + 1], HT[:, t % 2, :], ALU.mult, ALU.mult).then_inc(*T["qk_norm"].up())

            prepare(0)
            prepare(1)
            dve.wait_ge(T["evac"].sem, 2)
            prepare(2)
            convolve(0)
            convolve(1)
            prepare(3)
            convolve(2)
            convolve(3)
            prepare(4)
            prepare(5)
            dve.wait_ge(T["rg_sig"].sem, 8)
            dve.wait_ge(T["xc_ready"].sem, 4)
            for m in range(4):
                step(dve.tensor_tensor(I[:, m, :], I[:, m, :], XC[:, m, :], ALU.mult))
            gain(0)
            gain(1)
            prepare(6)
            gain(2)
            gain(3)
            normed(0)
            normed(1)
            prepare(7)
            normed(2)
            normed(3)
            dve.wait_ge(T["evac"].sem, 8)
            dve.wait_ge(T["rg_mm"].sem, 8)
            recur(0)
            prepare(8)
            recur(1)
            recur(2)
            normed(4)
            normed(5)
            prepare(9)
            dve.wait_ge(T["evac"].sem, 9)
            dve.scalar_tensor_tensor(F1, F0, -1.0, F0, ALU.mult, ALU.max).then_inc(*T["f_abs"].up())
            step(dve.memset(F2, 1.0))
            step(dve.memset(C, 0.0))
            recur(3)
            normed(6)
            normed(7)
            dve.wait_ge(T["f_ln"].sem, 1)
            step(dve.scalar_tensor_tensor(F0, F0, 0.0, F1, ALU.min, ALU.subtract))
            dve.tensor_tensor_scan(C[0:8, :], F2, F0, 0.0, ALU.mult, ALU.add).then_inc(*T["c_ready"].up())
            prepare(10)
            dve.wait_ge(T["c_hi"].sem, 1)
            dve.tensor_tensor(hy["CH"][:, 1, :], C, f32(hy["CH"][:, 0, :]), ALU.subtract).then_inc(*T["c_lo"].up())
            for m in range(4):
                dve.wait_ge(T["y_hi"].sem, m + 1)
                dve.tensor_tensor(HL[:, m, :], XC[:, m, :], f32(HH[:, m, :]), ALU.subtract).then_inc(*T["y_ready"].up())

            def fox_max(h):
                if h >= 2:
                    dve.wait_ge(T["fx_p"].sem, TB * (h - 1))
                for i in range(TB):
                    dve.wait_ge(T["fx_s"].sem, TB * h + i + 1)
                    dve.tensor_reduce(hy["ST"][:, h % 2, i:i + 1], PS[:, i, 0:P * (i + 1)], AX, ALU.max, negate=True).then_inc(*T["fx_max"].up())

            def fox_norm(h):
                dve.wait_ge(T["fx_exp"].sem, TB * (h + 1))
                sums = hy["ST"][:, h % 2, TB:2 * TB]
                step(dve.reciprocal(sums, sums))
                for i in range(TB):
                    p = PX(h)[:, i, 0:P * (i + 1)]
                    dve.tensor_scalar(p, p, hy["ST"][:, h % 2, TB + i:TB + i + 1], None, ALU.mult).then_inc(*T["fx_p"].up())

            def out_low(y0, p, tile):
                dve.wait_ge(T["y_hi"].sem, y0 + 1)
                dve.tensor_tensor(HL[:, tile, :], PS[:, 6 + p % 2, :], f32(HH[:, tile, :]), ALU.subtract).then_inc(*T["y_ready"].up())

            for h in range(FOXH):
                fox_max(h)
                fox_norm(h)
                if h % 2:
                    out_low(4 + h // 2, h // 2, 4 + h // 2)
            residual(RES["hy"], U_HYO, 1, True, 1.0)
            ffn(1, lambda kt: col("ffn1", kt))

            for j in range(2):
                step(dve.tensor_tensor(MOD[:, :, j], MOD[:, :, j], col("b_ada", 0, 48), ALU.add))
            for k, (g, lo, j) in enumerate((("norm1", 8, 0), ("norm1", 8, 1), ("norm2", 32, 0))):
                ins = dve.scalar_tensor_tensor(CSC[:, k, :], MOD[:, lo:lo + 8, j], 1.0, col(g, 0, 8), ALU.add, ALU.mult)
                if k < 2:
                    step(ins)
            ins.then_inc(*T["mod_ready"].up())
            dve.wait_ge(*T["mod_ready"].now())
            ffn(2, lambda kt: col("ffn2", kt))

            norm(N_NORM["mix1"], lambda kt: col("mix1", kt))
            for u_ in range(U_SB + 1, U_SBO + 1):
                split(u_)
            def sb_soft(h):
                E = sbm["E"][:, h % 2, :]
                dve.wait_ge(T["sb_ln"].sem, h + 1)
                if h >= 2:
                    dve.wait_ge(T["sb_tri"].sem, h - 1)
                step(dve.scalar_tensor_tensor(E, zs(h)[:, 0:1280], 0.0, E, ALU.max, ALU.add))
                step(dve.tensor_copy(sbm["SH"][:, h % 2, :], E))
                dve.tensor_tensor(sbm["SL"][:, h % 2, :], E, f32(sbm["SH"][:, h % 2, :]), ALU.subtract).then_inc(*T["sb_sl"].up())

            def sb_low(h):
                if h % 2:
                    out_low(8 + h // 2, h // 2, h // 2)

            for h in range(SBH):
                sb_soft(h)
                if h >= 1:
                    sb_low(h - 1)
            sb_low(SBH - 1)
            residual(RES["sb"], U_SBO, 1, True, 1.0)
            ffn(3, lambda kt: col("ffn3", kt))

            norm(N_NORM["norm1"], lambda kt: CSC[:, 0, kt:kt + 1], lambda kt: MOD[:, kt, 0:1])

            def prepare(k):
                split(U_B2 + k + 1)

            prepare(0)
            for k in range(V_RET):
                if k == 2:
                    step(dve.memset(SSC, 0.0))
                    for t_ in range(KT):
                        dve.wait_ge(T["csq"].sem, t_ + 1)
                        dve.tensor_tensor(SSC, SSC, SQC(t_), ALU.add).then_inc(*T["css_acc"].up())
                        dve.wait_ge(*T["css_acc"].now())
                if k == 4:
                    dve.wait_ge(T["crms"].sem, 1)
                    for t_ in range(KT):
                        if t_ >= 2:
                            dve.wait_ge(T["ch_ready"].sem, t_ - 1)
                        dve.scalar_tensor_tensor(SQC(t_), b2["CT"][:, t_, :], CSC[:, 1, t_:t_ + 1], RINC, ALU.mult, ALU.mult).then_inc(*T["cht"].up())
                        dve.wait_ge(T["chh"].sem, t_ + 1)
                        dve.scalar_tensor_tensor(b2["HCL"][:, t_, :], SQC(t_), MOD[:, t_, 1:2], f32(b2["HCH"][:, t_, :]), ALU.add,
                                                 ALU.subtract).then_inc(*T["ch_ready"].up())
                name, i = B2_VISITS[k][1]
                if name in ("rq", "rk"):
                    dve.wait_ge(T["const_in"].sem, 16 * 9)
                    for m in range(2):
                        q = b2[name.upper()][:, 2 * i + m, :]
                        if m == 0:
                            dve.wait_ge(T["rope_sw"].sem, T["rot_in"].n + 1)
                            T["rot_in"].n += 1
                        else:
                            dve.wait_ge(T["evac"].sem, ev(k))
                        step(dve.tensor_tensor(b2["SW"][:, 0, :], b2["SW"][:, 0, :], b2["ROPE"][:, 1, :], ALU.mult))
                        step(dve.tensor_tensor(q, q, b2["ROPE"][:, 0, :], ALU.mult))
                        dve.tensor_tensor(q, q, b2["SW"][:, 0, :], ALU.add).then_inc(*T["rope_done"].up())
                prepare(k + 1)

            dve.wait_ge(T["const_in"].sem, 16 * 11)
            dve.wait_ge(T["evac"].sem, ev(V_RET - 1))
            MX, SM, KS = rw["MX"], rw["SM"], rw["KS"]
            for h in range(NH):
                if h:
                    dve.wait_ge(T["rt_sm"].sem, TB * h)
                step(dve.tensor_scalar(MX[:, :], rw["REL"][:, :], LGS[:, 12 + h:13 + h], None, ALU.mult))
                dve.scalar_tensor_tensor(MX[:, :], rw["REL"][:, :], LGS[:, h:h + 1], MX[:, :], ALU.mult, ALU.min).then_inc(*T["rt_e"].up())
                dve.wait_ge(T["rt_x"].sem, h + 1)
                step(dve.tensor_tensor(MX[:, 384:512], MX[:, 384:512], IDENT[:, :], ALU.add))
                for d_ in range(2):
                    dve.wait_ge(T["rt_qx"].sem, 2 * h + d_ + 1)
                    dve.tensor_tensor(rw["QF"][:, d_, :], rw["QF"][:, d_, :], b2["RQ"][:, h, :], ALU.mult).then_inc(*T["rt_q"].up())
                dve.wait_ge(T["rt_ce"].sem, h + 1)
                if h:
                    dve.wait_ge(T["rt_st"].sem, h)
                for k in range(4):
                    last = dve.tensor_scalar(KS[:, k, :], b2["CRK"][:, k % 2, P * h:P * h + P], TE[:, k:k + 1], None, ALU.mult)
                last.then_inc(*T["rt_ks"].up())
                if h:
                    dve.wait_ge(T["rt_o"].sem, h)
                for j in range(TB):
                    dve.wait_ge(T["rt_s"].sem, TB * h + j + 1)
                    dve.tensor_tensor(SM[:, j, :], PS[:, j % 2, :], MX[:, 384 - P * j:896 - P * j], ALU.mult).then_inc(*T["rt_sm"].up())
                prepare(V_RET + h + 1)

            IG, FG, F, GM, ONE = gr["IG"], gr["FG"], mw["F"], mw["GM"], mw["ONE"]
            dve.wait_ge(T["rt_out"].sem, NH)
            dve.scalar_tensor_tensor(mw["AB"][0:36, :], FG[0:36, :], -1.0, FG[0:36, :], ALU.mult, ALU.max).then_inc(*T["ml_abs"].up())
            step(dve.memset(F[0:36, :], 0.0))
            step(dve.memset(GM[0:36, :], 0.0))
            step(dve.memset(ONE[0:36, :], 1.0))
            dve.wait_ge(T["ml_ln"].sem, 1)
            step(dve.scalar_tensor_tensor(FG[0:36, :], FG[0:36, :], 0.0, mw["AB"][0:36, :], ALU.min, ALU.subtract))

            def both_scans(dst, src, op):
                for rows, c, x, end in ((slice(0, 4), (lambda t: t[0:4, 0:SC]), (lambda t: t[0:4, SC:SC + S]), dst[0:4, SC - 1:SC]),
                                        (slice(32, 36), (lambda t: t[32:36, 0:SC][:, ::-1]), (lambda t: t[32:36, SC:SC + S][:, ::-1]), dst[32:36, 0:1])):
                    step(dve.tensor_tensor_scan(c(dst), ONE[rows, 0:SC], c(src), 0.0, ALU.mult, op))
                    step(dve.tensor_tensor_scan(x(dst), ONE[rows, 0:S], x(src), end, ALU.mult, op))

            both_scans(F, FG, ALU.add)
            step(dve.tensor_tensor(IG[0:36, :], IG[0:36, :], F[0:36, :], ALU.subtract))
            both_scans(GM, IG, ALU.max)
            dve.tensor_tensor(F[0:36, :], F[0:36, :], GM[0:36, :], ALU.add).then_inc(*T["ml_rows"].up())
            prepare(V_PREP + 1)
            for k in range(2 * NH):
                dve.wait_ge(T["ml_ws"].sem, k + 1)
                if k >= 2:
                    dve.wait_ge(T["ml_c0"].sem, k - 1)
                for c in range(2):
                    last = dve.tensor_scalar(mw["KS"][:, k % 2, c, :], b2["CMK"][:, c, P * (k // 2):P * (k // 2) + P], WS[:, k, c:c + 1], None, ALU.mult)
                last.then_inc(*T["ml_ks"].up())
            prepare(V_PREP + 2)
            prepare(V_PREP + 3)
            def own_keys(k):
                d_, r = k % 2, 32 * (k % 2) + k // 2
                dve.wait_ge(T["ml_g"].sem, k + 1)
                for j in range(TB):
                    t = slice(P * j, P * j + P)
                    last = dve.scalar_tensor_tensor(WM[d_][:, j, t], PS[:, 2, t], mw["GCOL"][:, 2 + j, r:r + 1], mw["MSK"][:, d_, :], ALU.add, ALU.add)
                last.then_inc(*T["ml_diag"].up())

            dve.wait_ge(T["const_in"].sem, 16 * 13)
            own_keys(0)
            own_keys(1)
            for h in range(NH):
                for d_ in range(2):
                    dve.wait_ge(T["ml_w"].sem, 2 * h + d_ + 1)
                    if h:
                        dve.wait_ge(T["ml_nd"].sem, 2 * h + d_ - 1)
                    dve.tensor_tensor(mw["QW"][:, d_, :], b2["MQ"][:, h, :], SQT[:, d_, :], ALU.mult).then_inc(*T["ml_qw"].up())
                for j in range(TB):
                    dve.wait_ge(T["ml_s"].sem, TB * h + j + 1)
                    for d_ in range(2):
                        lo, hi = span(d_, j)
                        last = dve.tensor_tensor(WM[d_][:, j, lo:hi], PS[:, j % 2, lo:hi], WM[d_][:, j, lo:hi], ALU.mult)
                    last.then_inc(*T["ml_sm"].up())
                prepare(V_ML + h + 1)
                for d_ in range(2):
                    k = 2 * h + d_
                    dve.wait_ge(T["ml_nd"].sem, k + 1)
                    den = HT[:, d_, :]
                    step(dve.scalar_tensor_tensor(den, PS[:, 5, :], -1.0, den, ALU.mult, ALU.max))
                    step(dve.tensor_tensor(den, PS[:, 5, :], den, ALU.max))
                    step(dve.reciprocal(den, den))
                    if d_ == 0:
                        dve.tensor_tensor(SSACC[:, :], PS[:, 4, :], den, ALU.mult).then_inc(*T["ml_h"].up())
                    else:
                        step(dve.tensor_tensor(den, PS[:, 4, :], den, ALU.mult))
                        dve.wait_ge(T["ml_h"].sem, k)
                        dve.tensor_tensor(b2["MQ"][:, h, :], SSACC[:, :], den, ALU.add).then_inc(*T["ml_h"].up())
                    if h + 1 < NH:
                        own_keys(k + 2)

            dve.wait_ge(T["evac"].sem, ev(V_UP - 1))
            for m in range(4):
                dve.wait_ge(*T["ml_h"].now())
                dve.tensor_tensor(b2["MQ"][:, m, :], b2["MQ"][:, m, :], mw["MO"][:, m, :], ALU.mult).then_inc(*T["hn_in"].up())
            for t_ in range(8):
                y = b2["RQ" if t_ < 4 else "MQ"][:, t_ % 4, :]
                dve.wait_ge(T["hn_rms"].sem, t_ + 1)
                dve.wait_ge(T["hn_in"].sem, 4)
                ins = dve.tensor_tensor(y, y, HT[:, t_ % 2, :], ALU.mult)
                if t_ < 4:
                    step(ins)
                    ins = dve.tensor_tensor(y, y, ml["RG"][:, t_, :], ALU.mult)
                ins.then_inc(*T["y_f32"].up())
                if t_ % 2:
                    for t in (t_ - 1, t_):
                        dve.wait_ge(T["y_f32"].sem, 4 + t + 1)
                        dve.wait_ge(T["y_hi"].sem, 16 + t + 1)
                        y = b2["RQ" if t < 4 else "MQ"][:, t % 4, :]
                        dve.tensor_tensor(po["YL"][:, t, :], y, f32(po["YH"][:, t, :]), ALU.subtract).then_inc(*T["y_ready"].up())
                    prepare(V_UP + t_ // 2 + 1)
            for i in range(2):
                k = V_UP + 6 * i
                if i:
                    for q in range(4):
                        prepare(k + q + 1)
                prepare(k + 5)
                dve.wait_ge(T["evac"].sem, ev(k + 3))
                dve.wait_ge(T["visit_done"].sem, U_B2 + k + 6)
                for m in range(4):
                    a, b = HT[:, m % 2, :], SQT[:, m % 2, :]
                    if 4 * i + m >= 2:
                        dve.wait_ge(T["m_ready"].sem, 4 * i + m - 1)
                    step(dve.tensor_tensor(a, PS[:, m, :], po["BG"][:, m, :], ALU.mult))
                    step(dve.tensor_tensor(b, PS[:, 4 + m, :], po["BG"][:, 4 + m, :], ALU.mult))
                    dve.tensor_tensor(b, a, b, ALU.add).then_inc(*T["up_m"].up())
                    dve.wait_ge(*T["up_m"].now())
                    dve.wait_ge(T["up_hi"].sem, 4 * i + m + 1)
                    dve.tensor_tensor(po["ML"][:, 4 * i + m, :], b, f32(po["MH"][:, 4 * i + m, :]), ALU.subtract).then_inc(*T["m_ready"].up())
                if i == 0:
                    prepare(k + 6)
            residual(RES["b2"], U_B2O, 1, False, lambda t: MOD[:, 16 + t, 0:1])
            ffn(4, lambda kt: CSC[:, 2, kt:kt + 1], lambda kt: MOD[:, 24 + kt, 0:1], lambda t: MOD[:, 40 + t, 0:1])
            norm(N_NORM["final"], lambda kt: col("final", kt))

        @block.tensor
        def _(pe):
            def three(out, wh, wl, xh, xl, start, stop):
                pe.matmul(out, wh, xh, start=start, stop=False)
                pe.matmul(out, wh, xl, start=False, stop=False)
                return pe.matmul(out, wl, xh, start=False, stop=stop)

            def feature_major(slot, xh, xl, banks, tokens=S, k0=0, n=KT, start=True, stop=True, width=UC, ready=None):
                wh, wl = (w[slot][:, :].rearrange("p (k c) -> p k c", c=width) for w in (WH, WL))
                for k in range(n):
                    if ready is not None:
                        pe.wait_ge(T["h_ready"].sem, ready + k + 1)
                    for m, b in enumerate(banks):
                        c = slice(P * m, P * m + P)
                        last = three(PS[:, b, 0:tokens], wh[:, k, c], wl[:, k, c], xh[:, k0 + k, 0:tokens], xl[:, k0 + k, 0:tokens],
                                     start and k == 0, stop and k == n - 1)
                return last

            def token_major(slot, xh, xl, b, blocks):
                wh, wl = (w[slot][:, :].rearrange("p (k c) -> p k c", c=UC) for w in (WH, WL))
                for t in range(blocks):
                    out = PS[:, b + t // 2, UC * (t % 2):UC * (t % 2) + UC]
                    c = slice(P * t, P * t + P)
                    for k in range(KT):
                        last = three(out, xh[:, k, c], xl[:, k, c], wh[:, k, :], wl[:, k, :], k == 0, k == KT - 1)
                return last

            def norm(m):
                pe.wait_ge(T["ss_acc"].sem, 8 * (m + 1))
                pe.matmul(PS[:, 4, :], ONES[:, :], SSACC[:, :], start=True, stop=True).then_inc(*T["ss_sum"].up())

            def ffn(n):
                m = N_NORM[("ffn0", "ffn1", "ffn2", "ffn3", "norm2")[n]]
                u0 = U_FFN[n]
                norm(m)

                carries = n < N_ADA // ADA_PER

                def conditioning(i):
                    u = i + ADA_PER * n
                    pe.wait_ge(T["ada_step"].sem, 16 * i + (16 * ADA_PER * n + 16))
                    if not isinstance(i, int) or u > 0:
                        pe.wait_ge(T["ada_mod"].sem, u)
                    for m in range(2):
                        for j in range(2):
                            last = pe.matmul(PS[:, 7, 2 * m + j:2 * m + j + 1], ACC[:, j, P * m:P * m + P], ONES[:, 0:1], start=True, stop=True)
                    last.then_inc(T["ada_mm"].sem, 1)

                def pair(i, first):
                    for s, banks in ((0, (0, 1)), (1, (2, 3))):
                        pe.wait_ge(T["w_lo"].sem, 2 * i + (u0 + s + 1))
                        if not first:
                            pe.wait_ge(T["g_mul" if s else "silu_ready"].sem, 2 * i + 22 * n)
                        feature_major((u0 + s) % 2, HH, HL, banks, ready=8 * m if first and s == 0 else None)\
                            .then_inc(*T["visit_done"].up())
                        if carries and (s == 1 if first else s == 0):
                            conditioning(i)

                pair(0, True)
                with pe.Fori(1, FFN_IN // 2) as i:
                    pair(i, False)
                if carries:
                    conditioning(ADA_PER - 1)
                residual(RES[f"ffn{n}"], u0 + FFN_IN, FFN_CHUNKS, GH, GL, n < 4, 22 * n)

            def residual(r, u0, chunks, xh, xl, loop, g0=None):
                def group(i, j):
                    for c, n in enumerate(chunks):
                        u = u0 + len(chunks) * j + c
                        pe.wait_ge(T["w_lo"].sem, 2 * len(chunks) * i + (u + 1))
                        if g0 is not None:
                            pe.wait_ge(T["g_ready"].sem, g0 + sum(chunks[:c + 1]))
                        if c == 0:
                            pe.wait_ge(T["x_upd"].sem, 4 * i + (X0 + 8 * r + 2 * j - 2))
                        feature_major(u % 2, xh, xl, (4 + 2 * j, 5 + 2 * j), k0=sum(chunks[:c]), n=n, start=c == 0,
                                      stop=c == len(chunks) - 1).then_inc(*T["visit_done"].up())

                if loop:
                    with pe.Fori(0, 2) as i:
                        group(i, 0)
                        group(i, 1)
                else:
                    for i in range(2):
                        group(i, 0)
                        group(i, 1)

            def project(u, kind, b, ready=None):
                pe.wait_ge(T["w_lo"].sem, u + 1)
                if kind in ("feat", "gates", "gates1"):
                    last = feature_major(u % 2, HH, HL, (b,) if kind == "gates1" else (b, b + 1), ready=ready)
                elif kind == "cgates":
                    last = feature_major(u % 2, b2["HCH"], b2["HCL"], (b, b + 1), tokens=SC)
                elif kind == "tok":
                    last = token_major(u % 2, HH, HL, b, TB)
                else:
                    last = token_major(u % 2, b2["HCH"], b2["HCL"], b, 2)
                last.then_inc(*T["visit_done"].up())

            def visits(name, vis, m):
                for k, (kind, what) in enumerate(vis):
                    if k >= 4:
                        pe.wait_ge(T["evac"].sem, EV[name] + k - 3)
                    project(V0[name] + k, kind, 2 * (k % 4), 8 * m if k == 0 else None)

            pe.wait_ge(*T["vec_in"].now())
            ffn(0)

            norm(N_NORM["mix0"])
            def visit(k):
                if k >= 4:
                    pe.wait_ge(T["evac"].sem, EV["hy"] + k - 1)
                project(U_HY + k, HY_VISITS[k][0], hy_bank(k), 8 * N_NORM["mix0"] if k == 0 else None)

            def gates(g):
                for m in range(4):
                    pe.wait_ge(T["xc_ready"].sem, m + 1)
                    if g:
                        pe.wait_ge(T["rg_sig"].sem, m + 1)
                    pe.matmul(PS[:, m, :], hy["BD"][:, 4 * g + m, :], hy["XC"][:, m, :], start=True, stop=True).then_inc(*T["rg_mm"].up())

            def head_sums(t0):
                for t in (t0, t0 + 1):
                    pe.wait_ge(T["qk_sq"].sem, t + 1)
                    if t >= 2:
                        pe.wait_ge(T["qk_rms"].sem, t - 1)
                    pe.matmul(PS[:, t % 2, :], hy["B64"][:, :], SQT[:, t % 2, :], start=True, stop=True).then_inc(*T["qk_ss"].up())

            for k in range(5):
                visit(k)
            pe.wait_ge(T["const_in"].sem, 16 * 4)
            gates(0)
            visit(5)
            gates(1)
            visit(6)
            pe.wait_ge(T["rg_sig"].sem, 8)
            head_sums(0)
            visit(7)
            head_sums(2)
            visit(8)
            head_sums(4)
            visit(9)
            head_sums(6)
            visit(10)
            pe.wait_ge(T["evac"].sem, EV["sb"])

            def fox_scores(h):
                r = slice(64 * (h % 2), 64 * (h % 2) + 64)
                for i in range(TB):
                    w = P * (i + 1)
                    if h:
                        pe.wait_ge(T["fx_exp"].sem, TB * (h - 1) + i + 1)
                    o = PS[:, i, 0:w]
                    pe.matmul(o, hy["Q"][r, h // 2, P * i:w], hy["K"][r, h // 2, 0:w], start=True, stop=False)
                    pe.matmul(PS[:, i, P * i:w], hy["EYE"][:, :], hy["MASK"][:, :], start=False, stop=False, skip_group_check=True)
                    pe.matmul(o, hy["SEL"][:, h, :], hy["CH"][:, 0, 0:w], start=False, stop=False)
                    pe.matmul(o, hy["SEL"][:, h, :], hy["CH"][:, 1, 0:w], start=False, stop=True)\
                        .then_inc(*T["fx_s"].up())

            def values(out_bank, h, v, probs, widths):
                r = slice(64 * (h % 2), 64 * (h % 2) + 64)
                for j in range(TB):
                    last = pe.matmul(PS[r, out_bank, P * j:S], v[:, j, HD * h:HD * h + HD], probs(j), start=j == 0, stop=True,
                                     skip_group_check=True)
                return last

            pe.wait_ge(T["qk_norm"].sem, 8)
            pe.wait_ge(T["c_lo"].sem, 1)
            pe.wait_ge(T["fx_const"].sem, 1)
            fox_scores(0)
            for h in range(FOXH):
                if h + 1 < FOXH:
                    fox_scores(h + 1)
                for j in range(TB):
                    n = TB * h + j
                    if n >= 2:
                        pe.wait_ge(T["fx_pt"].sem, n - 1)
                    for i in range(j, TB):
                        pe.wait_ge(T["fx_p"].sem, TB * h + i + 1)
                        last = pe.transpose(PS[:, 4 + j % 2, P * (i - j):P * (i - j) + P], PX(h)[:, i, P * j:P * j + P], IDENT[:, :])
                    last.then_inc(*T["fx_t"].up())
                pe.wait_ge(T["fx_pt"].sem, TB * (h + 1))
                if h >= 4 and h % 2 == 0:
                    pe.wait_ge(T["y_ready"].sem, 4 + h // 2 - 1)
                values(6 + h // 2 % 2, h, hy["V"], lambda j: hy["PT"][:, h % 2, j, 0:S - P * j], None).then_inc(*T["fx_o"].up())
            pe.wait_ge(T["y_ready"].sem, 8)
            residual(RES["hy"], U_HYO, (8,), HH, HL, True)
            ffn(1)
            ffn(2)

            norm(N_NORM["mix1"])
            visits("sb", SB_VISITS, N_NORM["mix1"])
            pe.wait_ge(T["evac"].sem, EV["b2"])
            pe.wait_ge(T["sb_const"].sem, 1)

            def sb_scores(h):
                r = slice(64 * (h % 2), 64 * (h % 2) + 64)
                if h >= 2:
                    pe.wait_ge(T["sb_exp"].sem, h - 1)
                for i in (0, 1, 3, 2):
                    last = pe.matmul(zs(h)[:, OFF[i]:OFF[i] + S - P * i], sbm["K"][r, h // 2, P * i:P * i + P], sbm["Q"][r, h // 2, P * i:S],
                                     start=i != 3, stop=True, skip_group_check=True)
                for i in range(TB):
                    last = pe.matmul(zs(h)[:, OFF[i]:OFF[i] + P], sbm["EYE"][:, :], sbm["MASK"][:, :], start=False, stop=True, skip_group_check=True)
                last.then_inc(*T["sb_z"].up())

            def sb_logs(h):
                pe.wait_ge(T["sb_sl"].sem, h + 1)
                for i in range(TB):
                    for j in range(i, TB):
                        w = S - P * j
                        o = OFF[i] + P * (j - i)
                        for part in ("SH", "SL"):
                            last = pe.matmul(zs(h)[:, o:o + w], sbm["TRI" if i == j else "NONE"][:, :], sbm[part][:, h % 2, OFF[j]:OFF[j] + w],
                                             start=False, stop=True, skip_group_check=True)
                last.then_inc(*T["sb_tri"].up())

            def sb_values(h):
                pe.wait_ge(T["sb_exp"].sem, h + 1)
                if h >= 4 and h % 2 == 0:
                    pe.wait_ge(T["y_ready"].sem, 8 + h // 2 - 1)
                values(6 + h // 2 % 2, h, sbm["V"], lambda j: sbm["W"][:, h % 2, OFF[j]:OFF[j] + S - P * j], None).then_inc(*T["sb_o"].up())

            sb_scores(0)
            for h in range(SBH):
                if h + 1 < SBH:
                    sb_scores(h + 1)
                sb_logs(h)
                if h >= 1:
                    sb_values(h - 1)
            sb_values(SBH - 1)
            pe.wait_ge(T["y_ready"].sem, 16)
            residual(RES["sb"], U_SBO, (8,), HH, HL, True)
            ffn(3)

            norm(N_NORM["norm1"])

            def visit(k):
                if k >= V_UP + 4:
                    pe.wait_ge(T["up_m"].sem, 2 if k == V_UP + 6 else 4)
                elif k == V_UP:
                    pe.wait_ge(T["ml_h"].sem, 2 * NH)
                elif k >= 4:
                    pe.wait_ge(T["evac"].sem, ev(k - 4 if k < V_RET else k - 1 if V_ML <= k <= V_UP + 1 else k - 2))
                project(U_B2 + k, B2_VISITS[k][0], bank(k), 8 * N_NORM["norm1"] if k == 0 else None)

            for k in range(V_RET):
                if k == 4:
                    pe.wait_ge(T["css_acc"].sem, 8)
                    pe.wait_ge(T["evac"].sem, ev(2))
                    pe.matmul(PS[:, 4, 0:SC], ONES[:, :], SSC, start=True, stop=True).then_inc(*T["css_sum"].up())
                if k == 6:
                    pe.wait_ge(T["crms"].sem, 1)
                    pe.wait_ge(T["ch_ready"].sem, 8)
                visit(k)
            pe.wait_ge(T["evac"].sem, ev(V_RET - 1))
            pe.wait_ge(T["rope_done"].sem, 8)

            def ret_scores(h, j):
                if TB * h + j >= 2:
                    pe.wait_ge(T["rt_sm"].sem, TB * h + j - 1)
                pe.matmul(PS[:, j % 2, :], b2["RK"][:, h, P * j:P * j + P], b2["RQ"][:, h, :], start=True, stop=True).then_inc(*T["rt_s"].up())

            def ret_values(h, j):
                if j == 0 and h:
                    pe.wait_ge(T["rt_out"].sem, h)
                pe.wait_ge(T["rt_sm"].sem, TB * h + j + 1)
                pe.matmul(PS[:, 3, :], b2["RV"][:, j, P * h:P * h + P], rw["SM"][:, j, :], start=j == 0, stop=False)

            for h in range(NH):
                ret_scores(h, 0)
                ret_scores(h, 1)
                visit(V_RET + h)
                pe.wait_ge(T["rt_ks"].sem, h + 1)
                if h:
                    pe.wait_ge(T["rt_stc"].sem, h)
                for d in range(2):
                    for b in range(2):
                        last = pe.matmul(PS[:, 2, P * d:P * d + P], rw["KS"][:, 2 * d + b, :], b2["CRV"][:, b, P * h:P * h + P], start=b == 0, stop=b == 1)
                last.then_inc(*T["rt_st"].up())
                ret_values(h, 0)
                ret_scores(h, 2)
                ret_values(h, 1)
                ret_scores(h, 3)
                ret_values(h, 2)
                ret_values(h, 3)
                pe.wait_ge(T["rt_q"].sem, 2 * h + 2)
                pe.wait_ge(T["rt_stc"].sem, h + 1)
                for d in range(2):
                    last = pe.matmul(PS[:, 3, :], rw["ST"][:, d, :], rw["QF"][:, d, :], start=False, stop=d == 1)
                last.then_inc(*T["rt_o"].up())

            visit(V_PREP)
            pe.wait_ge(T["ml_rows"].sem, 1)
            pe.wait_ge(T["const_in"].sem, 16 * 13)
            for b in range(6):
                pe.transpose(PS[:, 0, 36 * b:36 * b + 36], gr["IG"][0:36, P * b:P * b + P], IDENT[0:36, 0:36])
            for k in range(2 * NH):
                e = 0 if k % 2 else SC - 1
                last = pe.matmul(PS[:, 1, k:k + 1], mw["SEL"][0:36, k, :], mw["GM"][0:36, e:e + 1], start=True, stop=True)
            last.then_inc(*T["ml_gt"].up())
            visit(V_PREP + 1)
            pe.wait_ge(T["ml_gc"].sem, 1)
            pe.wait_ge(T["rt_out"].sem, NH)
            for k in range(2 * NH):
                pe.wait_ge(T["ml_ks"].sem, k + 1)
                for part in range(2):
                    for b in range(2):
                        v = b2["CMV"][:, b, P * (k // 2):P * (k // 2) + P] if part == 0 else ONES[:, :]
                        o = 256 * (k % 2) + P * part
                        last = pe.matmul(PS[:, k // 2, o:o + P], mw["KS"][:, k % 2, b, :], v, start=b == 0, stop=b == 1)
                last.then_inc(*T["ml_c0"].up())
            visit(V_PREP + 2)
            pe.wait_ge(T["ml_c0c"].sem, NH)
            pe.wait_ge(T["evac"].sem, ev(V_ML - 1))

            def spread(k):
                if k:
                    pe.wait_ge(T["ml_w"].sem, k)
                pe.matmul(PS[:, 2, :], mw["SEL"][0:36, k, :], mw["GM"][0:36, SC:SC + S], start=True, stop=True)
                pe.matmul(PS[:, 3, :], mw["SEL"][0:36, k, :], mw["F"][0:36, SC:SC + S], start=True, stop=True).then_inc(*T["ml_g"].up())

            def ml_scores(h, j):
                if TB * h + j >= 2:
                    pe.wait_ge(T["ml_sm"].sem, TB * h + j - 1)
                pe.matmul(PS[:, j % 2, :], b2["MK"][:, h, P * j:P * j + P], b2["MQ"][:, h, :], start=True, stop=True).then_inc(*T["ml_s"].up())

            def ml_values(k):
                h, d = k // 2, k % 2
                pe.wait_ge(T["ml_sm"].sem, TB * (h + 1))
                pe.wait_ge(T["ml_qw"].sem, k + 1)
                if k:
                    pe.wait_ge(T["ml_h"].sem, k)
                for b, v, inter in ((4, lambda j: b2["MV"][:, j, P * h:P * h + P], C0N(k)[:, 0:P]), (5, lambda j: ONES[:, :], C0N(k)[:, P:2 * P])):
                    order = range(TB) if d == 0 else range(TB - 1, -1, -1)
                    for n, j in enumerate(order):
                        lo, hi = span(d, j)
                        pe.matmul(PS[:, b, lo:hi], v(j), WM[d][:, j, lo:hi], start=n == 0, stop=True, skip_group_check=n > 0)
                    last = pe.matmul(PS[:, b, :], inter, mw["QW"][:, d, :], start=False, stop=True, skip_group_check=True)
                last.then_inc(*T["ml_nd"].up())

            spread(0)
            ml_scores(0, 0)
            ml_scores(0, 1)
            for h in range(NH):
                spread(2 * h + 1)
                visit(V_ML + h)
                ml_scores(h, 2)
                ml_scores(h, 3)
                ml_values(2 * h)
                if h + 1 < NH:
                    spread(2 * h + 2)
                    ml_scores(h + 1, 0)
                    ml_scores(h + 1, 1)
                ml_values(2 * h + 1)

            for p in range(4):
                visit(V_UP + p)
                for t in (2 * p, 2 * p + 1):
                    pe.wait_ge(T["hn_sq"].sem, t + 1)
                    if t >= 2:
                        pe.wait_ge(T["hn_rms"].sem, t - 1)
                    pe.matmul(PS[:, t % 2, :], ONES[:, :], SQT[:, t % 2, :], start=True, stop=True).then_inc(*T["hn_ss"].up())
            pe.wait_ge(T["y_ready"].sem, 24)
            for i in range(2):
                if i:
                    for q in range(4):
                        visit(V_UP + 6 + q)
                pe.wait_ge(T["evac"].sem, ev(V_UP + 6 * i + 3))
                for s in range(2):
                    u = U_B2 + V_UP + 6 * i + 4 + s
                    pe.wait_ge(T["w_lo"].sem, u + 1)
                    feature_major(u % 2, po["YH"], po["YL"], range(4 * s, 4 * s + 4), k0=4 * s, n=4, width=512).then_inc(*T["visit_done"].up())
            pe.wait_ge(T["m_ready"].sem, 8)
            residual(RES["b2"], U_B2O, (8,), po["MH"], po["ML"], False)
            ffn(4)
            norm(N_NORM["final"])


def _tiles(w, cols):
    w = np.asarray(w)[:, cols]
    return w.reshape(w.shape[0] // P, P, w.shape[1]).transpose(1, 0, 2)


def _unit(w, cols):
    t = _tiles(w, cols)
    out = np.zeros((P, UNIT // UC, UC) if t.shape[2] <= UC else (P, UNIT // t.shape[2], t.shape[2]), np.float32)
    out[:, :t.shape[1], :t.shape[2]] = t
    return out.reshape(P, UNIT)


def _ffn_units(w_in, w_out):
    units = []
    for i in range(FT // 2):
        units += [_unit(w_in, slice(UC * i, UC * i + UC)), _unit(w_in, slice(FF + UC * i, FF + UC * i + UC))]
    for j in range(D // UC):
        at = 0
        for n in FFN_CHUNKS:
            units.append(_unit(w_out[at:at + P * n], slice(UC * j, UC * j + UC)))
            at += P * n
    return units


def _columns(w, lo, n):
    return [_unit(w, slice(lo + UC * i, lo + UC * i + UC)) for i in range(n // UC)]


def _placed(w, places):
    t = np.zeros((w.shape[0], UC), np.float32)
    for p, c in places:
        t[:, p] = w[:, c]
    return _unit(t, slice(0, UC))


def _col(v):
    return np.asarray(v).reshape(-1, P).T


def _constants():
    f = np.float32
    r = np.arange(P)
    t = np.arange(S)
    row, colm = (t // 64).astype(f), (t % 64).astype(f)
    inv = (10000.0 ** (-np.arange(32, dtype=np.float64) / 32)).astype(f)
    ang = np.concatenate([row[:, None] * inv, colm[:, None] * inv], -1).T.astype(np.float64)
    rope = np.stack([np.concatenate([np.cos(ang), np.cos(ang)]), np.concatenate([-np.sin(ang), np.sin(ang)])], 1)
    sel_fox = np.zeros((P, 8, P))
    for h in range(8):
        sel_fox[h, h] = -1
    sel_ml = np.zeros((P, 8, P))
    for k in range(8):
        sel_ml[32 * (k % 2) + k // 2, k] = -1
    s = np.arange(P)[:, None]
    cex = np.stack([255 - r, 127 - r, r, 128 + r], 1)
    return {k: np.ascontiguousarray(v, dtype=f) for k, v in {
        "c_ident": np.eye(P), "c_ones": np.ones((P, P)), "c_cex": cex,
        "c_b64": np.kron(np.eye(2), np.ones((64, 64))), "c_causal": np.where(r[None, :] <= s, 0.0, NEG), "c_sel_fox": sel_fox.reshape(P, 2, 512),
        "c_tri": np.where(s >= r[None, :], -1.0, 0.0), "c_negones": -np.ones((P, P)),
        "c_strict": np.where(s < r[None, :], 0.0, NEG), "c_rope": rope,
        "c_rel": (np.arange(896) - 384)[None, :] - s, "c_pos": np.broadcast_to(t + 1.0, (P, S)),
        "c_sel_ml": sel_ml, "c_msk_ml": np.stack([np.where(r[None, :] >= s, 0.0, NEG), np.where(r[None, :] <= s, 0.0, NEG)], 1),
    }.items()}


def _pack(a):
    g = {k: np.asarray(v) for k, v in a.items()}
    hy, b2, out = g["hy_w_in"][0], g["w_in_2"][0], {}
    out["w_ada"] = np.stack(_columns(g["w_ada_2"][0], 0, 6 * D))
    ffn = [_ffn_units(g["ffn_w_in"][l, k], g["ffn_w_out"][l, k]) for l in range(2) for k in range(2)]
    units = ffn[0] + _columns(hy, 0, 512) + _columns(hy, D, D) + _columns(hy, 512, 512)
    units += [_placed(hy, [(h, 2560 + h) for h in range(8)])] + _columns(hy, 2 * D, 512) + _columns(g["hy_w_out"][0], 0, D)
    units += ffn[1] + ffn[2] + _columns(g["sb_w_qkv"][0], 0, 3 * D) + _columns(g["sb_w_out"][0], 0, D) + ffn[3]
    part = lambda i: _columns(b2, 512 * i, 512)
    gates = [(32 * d + h, 4096 + 8 * d + h) for d in range(2) for h in range(4)]
    gates += [(P + 32 * d + h, 4096 + 8 * d + 4 + h) for d in range(2) for h in range(4)]
    gates = [_placed(b2, gates)]
    units += part(1) + part(2) + part(0) + part(1) + part(2) + part(5) + part(6) + gates + gates + part(5) + part(6) + part(4) + part(3) + part(7)
    for i in range(2):
        units += _columns(b2, 4112 + 512 * i, 512) + _columns(b2, 4112 + D + 512 * i, 512)
        units += [_unit(g[n][0], slice(512 * i, 512 * i + 512)) for n in ("w_ret_up_2", "w_ml_up_2")]
    units += _columns(g["w_out_2"][0], 0, D) + _ffn_units(g["w_ffn_in_2"][0], g["w_ffn_out_2"][0])
    assert len(units) == N_UNITS
    out["weights"] = np.stack(units)
    vec = np.zeros((P, NVEC), np.float32)

    def put(name, v):
        c, n = VCOLS[name]
        assert v.shape[1] == n
        vec[0:v.shape[0], c:c + n] = v

    for l in range(2):
        for k in range(2):
            put(f"ffn{2 * l + k}", _col(g["ffn_norm"][l, k]))
        put(f"mix{l}", _col(g["mix_norm"][l]))
    put("norm1", _col(g["norm1_gain_2"][0]))
    put("norm2", _col(g["norm2_gain_2"][0]))
    put("final", _col(g["final_gain_2"]))
    put("b_ada", _col(g["b_ada_2"][0]))
    put("conv_w", _col(g["rg_conv_w"][0]))
    put("conv_b", _col(g["rg_conv_b"][0]))
    put("gate_b", _col(g["rg_gate_b"][0]))
    put("soft", np.concatenate([_col(g["rg_lambda"][0]), np.broadcast_to(g["ret_decay_logit_2"][0].reshape(1, 8), (P, 8))], 1))
    put("qk", np.concatenate([g["fox_qk_norm"][0]] * 2, 1).T)
    put("fox_b", g["fox_fgate_b"][0][:, None])
    mb, b = g["mlstm_gate_bias_2"][0], np.zeros((36, 2), np.float32)
    for d in range(2):
        b[32 * d:32 * d + 4, 0], b[32 * d:32 * d + 4, 1] = mb[2 * d], mb[2 * d + 1]
    put("ml_b", b)
    put("cond", np.stack([_col(g["c_2"][0]), _col(g["c_ctx_2"])], 2).reshape(P, 16))
    out["vec"] = vec
    gw = g["rg_gate_w"][0]
    bd = np.zeros((P, 8, P), np.float32)
    for k in range(2):
        for m in range(4):
            for q in range(2):
                bd[64 * q:64 * q + 64, 4 * k + m, 64 * q:64 * q + 64] = gw[k, 2 * m + q]
    out["c_gates"] = bd
    out["x"] = _tiles(g["x"][0].T, slice(0, S))
    out["ctx"] = _tiles(g["ctx_2"][0].T, slice(0, SC))
    out.update(_constants())
    return {k: np.ascontiguousarray(v) for k, v in out.items()}


def kernel(**inputs):
    import concourse.bacc as _bacc
    from concourse.bass_utils import run_bass_kernel_spmd as _run

    nc = _bacc.Bacc("TRN2", target_bir_lowering=False, num_devices=1)
    arrays, A = {}, {}
    for name, a in _pack(inputs).items():
        arrays["in_" + name] = a
        A[name] = nc.dram_tensor("in_" + name, a.shape, F32, kind="ExternalInput").ap()
    A["out"] = nc.dram_tensor("out_t", (P, KT, S), F32, kind="ExternalOutput").ap()
    build(nc, A)
    got = _run(nc, [arrays], core_ids=[0]).results[0]["out_t"]
    return np.ascontiguousarray(got.transpose(2, 1, 0).reshape(1, S, D))
```

```python
from contextlib import ExitStack

import numpy as np
import concourse.bass as bass
from concourse import mybir

P = 128
D, S, SC = 1024, 512, 256
KT = D // P
FF = 2816
FT = FF // P
UNIT = 2048
UC = 256
FOXH, SBH, HD = 8, 16, 64
NH = 4
TB = S // P
EPS = 1e-6
NEG = -1e30
F32, F32R = mybir.dt.float32, mybir.dt.float32r
ALU, ACT, AX = mybir.AluOpType, mybir.ActivationFunctionType, mybir.AxisListType.X

VCOLS = {}
_n = 0
for _name, _k in (("ffn0", 8), ("ffn1", 8), ("ffn2", 8), ("ffn3", 8), ("mix0", 8), ("mix1", 8), ("norm1", 8),
                  ("norm2", 8), ("final", 8), ("b_ada", 48), ("conv_w", 16), ("conv_b", 4), ("gate_b", 8),
                  ("soft", 12), ("qk", 2), ("fox_b", 1), ("ml_b", 2), ("cond", 16)):
    VCOLS[_name] = (_n, _k)
    _n += _k
NVEC = _n

N_ADA, ADA_PER = 24, 8
FFN_IN, FFN_OUT = 22, 12
FFN_UNITS = FFN_IN + FFN_OUT
FFN_CHUNKS = (8, 8, 6)
U_FFN = [0, 49, 83, 133, 209]
U_HY, U_HYO, U_SB, U_SBO, U_B2, U_B2O = 34, 45, 117, 129, 167, 205
N_UNITS = 243


class Tally:

    def __init__(self, sem):
        self.sem, self.n = sem, 0

    def up(self, k=1):
        self.n += k
        return self.sem, k

    def now(self):
        return self.sem, self.n


HY_VISITS = ([("feat", (n, i)) for n in ("u", "q", "k", "gate") for i in range(2)] + [("gates1", ("f", 0))]
             + [("tok", ("v", i)) for i in range(2)])
SB_VISITS = [(kind, (n, i)) for i in range(4) for n, kind in (("q", "feat"), ("k", "feat"), ("v", "tok"))]


def sb_halves(h):
    v = 3 * (h // 4) + 3
    return [[(v, 0), (v, 1)], [(v + 1, 0)], [(v + 1, 1), (v + 2, 0)], [(v + 2, 1)]][h % 4] if v < len(SB_VISITS) else []


B2_VISITS = [(kind, (n, i)) for n, kind, k in (
    ("rk", "feat", 2), ("rv", "tok", 2), ("rq", "feat", 2), ("crk", "ctok", 2), ("crv", "ctok", 2), ("cmk", "ctok", 2),
    ("cmv", "ctok", 2), ("cmg", "cgates", 1), ("mg", "gates", 1), ("mk", "feat", 2), ("mv", "tok", 2), ("mq", "feat", 2),
    ("rg", "feat", 2), ("mo", "feat", 2)) for i in range(k)]
V_RET, V_PREP, V_ML = 15, 19, 22
UP_VISITS = [v for h in range(2) for v in [("feat", (n, i)) for n in ("br", "bm") for i in range(2)] + [("up", (n, h)) for n in ("ret", "ml")]]
V_UP = len(B2_VISITS)
B2_VISITS = B2_VISITS + UP_VISITS

N_NORM = {"ffn0": 0, "mix0": 1, "ffn1": 2, "ffn2": 3, "mix1": 4, "ffn3": 5, "norm1": 6, "norm2": 7, "final": 8}
N_LATE = 6
FFN_NORM = ("ffn0", "ffn1", "ffn2", "ffn3", "norm2")


def build(nc, A):
    ctx = ExitStack()
    with ctx:
        def sb(name, shape, dt=F32):
            return ctx.enter_context(nc.sbuf_tensor("sb_" + name, shape, dt))

        def layout(tag, items):
            with ExitStack() as phase:
                return {n: phase.enter_context(nc.sbuf_tensor(f"{tag}_{n}", s, dt)) for n, s, dt in items}

        def sem(name):
            return ctx.enter_context(nc.semaphore(name))

        PS = ctx.enter_context(nc.psum_tensor("PS", [P, 8, 512], F32))
        XT = sb("XT", [P, KT, S])
        HH, HL = sb("HH", [P, KT, S], F32R), sb("HL", [P, KT, S], F32R)
        RAW = [sb(f"RAW{s}", [P, UNIT]) for s in range(2)]
        WH = [sb(f"WH{s}", [P, UNIT], F32R) for s in range(2)]
        WL = [sb(f"WL{s}", [P, UNIT], F32R) for s in range(2)]
        VEC = sb("VEC", [P, NVEC])
        IDENT, ONES = sb("IDENT", [P, P]), sb("ONES", [P, P])
        EPSC = sb("EPSC", [P, 1])
        SQT, SSACC, RINV = sb("SQT", [P, 2, S]), sb("SSACC", [P, S]), sb("RINV", [P, S])
        HT = sb("HT", [P, 2, S])
        SPT = sb("SPT", [P, 8, 12])
        MOD = sb("MOD", [P, 48, 2])
        CSC = sb("CSC", [P, 3, KT])
        QKG = sb("QKG", [P, 2])
        RCOL = sb("RCOL", [P, TB])
        CS = sb("CS", [P, 16])
        LGS = sb("LGS", [P, 20])
        NGC, GCP, WS = sb("NGC", [P, 8]), sb("GCP", [P, 8]), sb("WS", [P, 8, 2])
        CEX, TE = sb("CEX", [P, 4]), sb("TE", [P, 4])
        SIL, G = HT, SQT

        ff = layout("ff", [("GH", [P, FT, S], F32R), ("GL", [P, FT, S], F32R), ("ADAW", [P, 1024], F32), ("ACC", [P, 2, UC], F32)])
        GH, GL, ADAW, ACC = ff["GH"], ff["GL"], ff["ADAW"], ff["ACC"]
        hy = layout("hy", [("UP", [P, 4, S + 4], F32), ("GT", [P, 4, S], F32), ("Q", [P, 4, S], F32), ("K", [P, 4, S], F32),
                           ("V", [P, TB, 512], F32), ("CH", [P, 2, S], F32R), ("XC", [P, 4, S], F32), ("R", [P, 4, S], F32),
                           ("I", [P, 4, S], F32), ("PT", [P, 2, TB, S], F32), ("BD", [P, 8, P], F32), ("B64", [P, P], F32),
                           ("MASK", [P, P], F32R), ("SEL", [P, 8, P], F32R), ("EYE", [P, P], F32R), ("ST", [P, 2, 2 * TB], F32)])
        sbm = layout("sbm", [("Q", [P, 8, S], F32), ("K", [P, 8, S], F32), ("V", [P, TB, D], F32), ("E", [P, 2, 1280], F32),
                             ("SH", [P, 2, 1280], F32R), ("SL", [P, 2, 1280], F32R), ("W", [P, 2, 1280], F32), ("TRI", [P, P], F32R),
                             ("NONE", [P, P], F32R), ("MASK", [P, P], F32R), ("EYE", [P, P], F32R)])
        hyy = layout("hyy", [("YL0", [P, 4, S + 4], F32R), ("YH0", [P, 4, S], F32R), ("YH1", [P, 4, S], F32R), ("YL1", [P, 4, S], F32R)])
        HY_YH = [hyy["YH0"][:, m, :] for m in range(4)] + [hyy["YH1"][:, m, :] for m in range(4)]
        HY_YL = [hyy["YL0"][:, m, 0:S] for m in range(4)] + [hyy["YL1"][:, m, :] for m in range(4)]
        sby = layout("sby", [("YH", [P, 8, S], F32R), ("YL", [P, 8, S], F32R)])
        lead = [("RQ", [P, 4, S], F32), ("MQ", [P, 4, S], F32), ("RK", [P, 4, S], F32), ("RV", [P, TB, 512], F32),
                ("MK", [P, 4, S], F32), ("MV", [P, TB, 512], F32), ("CRK", [P, 2, 512], F32),
                ("CRV", [P, 2, 512], F32), ("CMK", [P, 2, 512], F32), ("CMV", [P, 2, 512], F32)]
        b2 = layout("b2", lead + [("CT", [P, KT, SC], F32), ("HCH", [P, KT, SC], F32R), ("HCL", [P, KT, SC], F32R),
                                  ("ROPE", [P, 2, S], F32), ("SW", [P, 2, S], F32)])
        gr = layout("gr", lead + [("IG", [P, S + SC], F32), ("FG", [P, S + SC], F32)])
        rw = layout("rw", lead + [("CT", [P, KT, SC], F32), ("REL", [P, 896], F32), ("MX", [P, 896], F32), ("POS", [P, S], F32),
                                  ("QF", [P, 2, S], F32), ("SM", [P, TB, S], F32), ("KS", [P, 4, P], F32), ("ST", [P, 2, P], F32)])
        mw = layout("mw", lead + [("MO", [P, 4, S], F32), ("F", [P, S + SC], F32), ("GM", [P, S + SC], F32),
                                  ("AB", [P, S + SC], F32), ("SEL", [P, 8, P], F32), ("GCOL", [P, 6, 36], F32), ("ONE", [P, S], F32),
                                  ("MSK", [P, 2, P], F32), ("KS", [P, 2, 2, P], F32), ("QW", [P, 2, S], F32)])
        ml = layout("ml", lead[:2] + [("W0", [P, TB, S], F32), ("C0", [P, 4, S], F32)] + lead[4:6] + [("W1", [P, TB, S], F32), ("RG", [P, 4, S], F32)])
        po = layout("po", [("MH", [P, KT, S], F32R), ("YH", [P, KT, S], F32R), ("YL", [P, KT, S], F32R), ("ML", [P, KT, S], F32R),
                           ("CT", [P, KT, SC], F32), ("BG", [P, 8, S], F32)])

        def col(name, i=0, n=1, rows=P):
            c = VCOLS[name][0] + i
            return VEC[0:rows, c:c + n]

        def gain_of(name, t):
            return VEC[:, :].rearrange("p (n o) -> p n o", o=1)[:, t + VCOLS[name][0], :]

        def f32(ap):
            return ap.bitcast(F32)

        raw_loaded = [sem(f"raw_loaded{s}") for s in range(2)]
        T = {n: Tally(sem(n)) for n in (
            "vec_in", "small_in", "x_upd", "const_in", "ada_in", "ada_step", "ada_mm", "ada_mod", "mod_ready", "small", "act_step", "dve_step",
            "w_hi", "w_lo", "visit_done", "evac", "sq_ready", "ss_acc", "ss_sum", "rms_ready", "ht_ready", "hh_ready",
            "h_ready", "rcol_mm", "rcol_ready", "a_ready", "silu_ready", "g_scaled", "g_mul", "gelu_ready", "gh_ready", "g_ready", "out_stored",
            "xc_ready", "rg_mm", "rg_sig", "rg_at", "rg_b2", "rg_sq", "y_f32", "y_hi", "y_ready", "up_clear",
            "qk_sq", "qk_ss", "qk_rms", "qk_norm", "f_abs", "f_ln", "c_ready", "c_hi", "c_lo", "fx_const", "sb_const", "sb_sl", "sb_half", "sb_half_out",
            "fx_s", "fx_max", "fx_exp", "fx_p", "fx_t", "fx_pt", "fx_o",
            "sb_z", "sb_ln", "sb_tri", "sb_exp", "sb_o",
            "csq", "css_acc", "css_sum", "crms", "cht", "chh", "ch_ready", "rope_sw", "rope_done",
            "rt_e", "rt_x", "rt_qx", "rt_q", "rt_ce", "rt_ks", "rt_st", "rt_stc", "rt_s", "rt_sm", "rt_o", "rt_out",
            "ml_abs", "ml_ln", "ml_rows", "ml_gt", "ml_gc", "ml_ws", "ml_ks", "ml_c0", "ml_c0c", "ml_s", "ml_g",
            "ml_w", "ml_diag", "ml_qw", "ml_sm", "ml_num", "ml_den", "ml_den_in", "ml_den_read", "ml_h", "hn_in", "hn_sq", "hn_ss", "hn_rms",
            "up_c", "up_m", "up_hi", "m_ready", "rot_in")}
        X0 = 16

        T["cond_ready"] = Tally(sem("cond_ready"))
        block = ctx.enter_context(nc.Block())
        EV = {"hy": 0, "sb": len(HY_VISITS)}
        EV["b2"] = EV["sb"] + len(SB_VISITS)

        def ev(k):
            return EV["b2"] + 1 + k - sum(kind == "up" for kind, _ in B2_VISITS[:k])

        RES = {"ffn0": 0, "hy": 1, "ffn1": 2, "ffn2": 3, "sb": 4, "ffn3": 5, "b2": 6, "ffn4": 7}
        Y0 = {"hy": 0, "sb": 8, "b2": 16}
        OFF = {0: 0, 1: 512, 3: 896, 2: 1024}

        def zs(h):
            return PS[:, 3 * (h % 2):3 * (h % 2) + 3, :].rearrange("p b c -> p (b c)")

        def PX(h):
            return hy["R"] if h % 2 == 0 else hy["I"]

        def LA(m):
            return SPT[:, 6, m:m + 1]

        def LAN(m):
            return SPT[:, 6, 4 + m:5 + m]

        def SQC(t):
            return SQT[:, t % 2, 0:SC]

        SSC, RINC = HT[:, 0, 0:SC], HT[:, 1, 0:SC]

        DSUM = mw["KS"][:, :, :, :].rearrange("p a b c -> p (a b c)")
        WM = (ml["W0"], ml["W1"])

        def C0N(k):
            return ml["C0"][:, k // 2, 256 * (k % 2):256 * (k % 2) + 256]

        def hy_bank(k):
            return 2 * k if k < 4 else 4 + 2 * (k % 2)

        def bank(k):
            if k < V_RET:
                return 2 * (k % 4)
            if k < V_ML:
                return 4 + 2 * (k % 2)
            if V_UP <= k < V_UP + 4:
                return 2 + 4 * ((k - V_UP) % 2)
            return 6 if k < V_UP else 2 * (k - V_UP - 6)

        def span(d, j):
            return (P * j, S) if d == 0 else (0, P * (j + 1))

        @block.sync
        def _(sp):
            def load(slot, unit):
                sp.dma_start(RAW[slot][:, :], A["weights"][unit]).then_inc(raw_loaded[slot], 16)

            sp.dma_start(XT[:, :, :], A["x"]).then_inc(*T["x_upd"].up(16))
            load(0, 0)
            load(1, 1)
            with sp.Fori(0, (N_UNITS - 2) // 2) as i:
                for s in range(2):
                    sp.wait_ge(T["w_lo"].sem, 2 * i + s + 1)
                    load(s, 2 * i + s + 2)
            sp.wait_ge(T["w_lo"].sem, N_UNITS - 2)
            load((N_UNITS - 1) % 2, N_UNITS - 1)
            for t in range(0, KT, 2):
                sp.wait_ge(T["ht_ready"].sem, 8 * (N_NORM["final"] - N_LATE) + t + 2)
                sp.dma_start(A["out"][:, t:t + 2, :], XT[:, t:t + 2, :]).then_inc(*T["out_stored"].up(16))
            sp.wait_ge(*T["out_stored"].now())

        @block.gpsimd
        def _(pool):
            def const(dst, src):
                pool.dma_start(dst, src).then_inc(*T["const_in"].up(16))

            def conditioning(f):
                def half(u, h):
                    pool.dma_start(ADAW[:, :], A["w_ada"][u, :, 1024 * h:1024 * h + 1024]).then_inc(*T["ada_in"].up(16))

                if f:
                    pool.wait_ge(T["ada_step"].sem, 16 * ADA_PER * f)
                half(ADA_PER * f, 0)
                with pool.Fori(0, ADA_PER - 1) as i:
                    pool.wait_ge(T["ada_step"].sem, 16 * i + (16 * ADA_PER * f + 8))
                    half(i + ADA_PER * f, 1)
                    pool.wait_ge(T["ada_step"].sem, 16 * i + (16 * ADA_PER * f + 16))
                    half(i + (ADA_PER * f + 1), 0)
                pool.wait_ge(T["ada_step"].sem, 16 * ADA_PER * (f + 1) - 8)
                half(ADA_PER * (f + 1) - 1, 1)

            conditioning(0)
            pool.wait_ge(T["ada_mod"].sem, ADA_PER)
            pool.wait_ge(T["visit_done"].sem, U_HY)
            pool.memset(hy["UP"][:, :, 0:4], 0.0).then_inc(*T["up_clear"].up())
            const(hy["BD"][:, :, :], A["c_gates"])
            const(hy["B64"][:, :], A["c_b64"])
            const(hy["PT"][:, 1, 2, 0:P], A["c_causal"])
            const(hy["PT"][:, 1, 0:2, :], A["c_sel_fox"])
            pool.wait_ge(T["visit_done"].sem, U_FFN[1])
            conditioning(1)
            conditioning(2)
            pool.wait_ge(T["ada_mod"].sem, N_ADA)
            pool.wait_ge(T["visit_done"].sem, U_SB)
            for n, (name, src) in enumerate((("TRI", "c_tri"), ("NONE", "c_negones"), ("MASK", "c_strict"))):
                const(sbm["W"][:, 0, P * n:P * n + P], A[src])
            pool.wait_ge(T["visit_done"].sem, U_B2)
            const(b2["CT"][:, :, :], A["ctx"])
            const(b2["ROPE"][:, :, :], A["c_rope"])
            pool.wait_ge(T["rope_done"].sem, 8)
            pool.wait_ge(T["visit_done"].sem, U_B2 + V_RET)
            const(rw["REL"][:, :], A["c_rel"])
            const(rw["POS"][:, :], A["c_pos"])
            pool.wait_ge(T["rt_out"].sem, 4)
            const(mw["SEL"][:, :, :], A["c_sel_ml"])
            const(mw["MSK"][:, :, :], A["c_msk_ml"])

        @block.scalar
        def _(act):
            st, sm = T["act_step"], T["small"]

            def split_hi(slot, free):
                if free is not None:
                    act.wait_ge(T["visit_done"].sem, free)
                act.activation(WH[slot][:, :], RAW[slot][:, :], ACT.Copy).then_inc(*T["w_hi"].up())

            def split(u):
                if u < N_UNITS:
                    act.wait_ge(raw_loaded[u % 2], 16 * (u // 2 + 1))
                    split_hi(u % 2, u - 1 if u >= 2 else None)

            def split_at(base, per, i, off):
                u = base + off
                free = per * i + (base + off - 1)
                act.wait_ge(raw_loaded[u % 2], per * 8 * i + 16 * (u // 2 + 1))
                split_hi(u % 2, free if not isinstance(free, int) or free > 0 else None)

            def logs_table():
                act.preload_act_table_set("natural_log_exp_and_others")

            def root_inverse(dst, src, width):
                act.activation(dst, src, ACT.Ln, scale=1.0 / width, bias=EPSC[:, 0:1]).then_inc(*st.up())
                act.wait_ge(*st.now())
                return act.activation(dst, dst, ACT.Exp, scale=-0.5)

            def inverse(m):
                logs_table()
                act.wait_ge(T["ss_sum"].sem, m + 1)
                root_inverse(RINV[:, :], PS[:, 4, :], D).then_inc(*T["rms_ready"].up())

            def high_x(name, t):
                act.activation(HH[:, t, :], XT[:, t, :], ACT.Copy, scale=gain_of(name, t)).then_inc(*T["hh_ready"].up())

            def norm(m, shift=None):
                inverse(m)
                if m == N_NORM["final"]:
                    return
                for kt in range(KT):
                    act.wait_ge(T["ht_ready"].sem, 8 * (m - N_LATE) + kt + 1)
                    if shift is None:
                        ins = act.activation(HH[:, kt, :], HT[:, kt % 2, :], ACT.Copy)
                    else:
                        ins = act.activation(HH[:, kt, :], HT[:, kt % 2, :], ACT.Identity, bias=shift(kt))
                    ins.then_inc(*T["hh_ready"].up())

            def ffn(n, shift=None, lead=None):
                u0, v0, m_ = U_FFN[n], U_FFN[n], N_NORM[FFN_NORM[n]]
                late = m_ < N_LATE
                if not late:
                    norm(m_, shift)

                def high_g(i):
                    act.wait_ge(T["g_mul"].sem, 22 * n + 2 * i + 2)
                    for m in range(2):
                        last = act.activation(GH[:, 2 * i + m, :], G[:, m, :], ACT.Copy)
                    last.then_inc(*T["gh_ready"].up())

                def pair(i, first):
                    split_at(u0, 2, i, 1)
                    if not first:
                        high_g(i - 1)
                    elif late:
                        if lead:
                            lead()
                        inverse(m_)
                    split_at(u0, 2, i, 2)
                    if not late:
                        act.wait_ge(T["visit_done"].sem, 2 * i + v0 + 1)
                    for m in range(2):
                        if late:
                            act.wait_ge(T["a_ready"].sem, 2 * i + (22 * n + m + 1))
                        act.activation(SIL[:, m, :], SIL[:, m, :] if late else PS[:, m, :], ACT.Silu).then_inc(*T["silu_ready"].up())

                pair(0, True)
                with act.Fori(1, FFN_IN // 2) as i:
                    pair(i, False)
                high_g(FFN_IN // 2 - 1)
                residual(RES[f"ffn{n}"], u0 + FFN_IN, 3, n < 4, ("mix0", "ffn2", "mix1", None, None)[n])

            def residual(r, u0, chunks, loop, then=None):
                def group(i, j):
                    for c in range(chunks):
                        if not (isinstance(i, int) and u0 + chunks * (2 * i + j) + c + 1 >= N_UNITS):
                            split_at(u0, 2 * chunks, i, chunks * j + c + 1)
                    act.wait_ge(T["ss_acc"].sem, 4 * i + (8 * (r + 1) + 2 * j))
                    act.wait_ge(T["x_upd"].sem, 4 * i + (X0 + 8 * r + 2 * j + 2))
                    for m in range(2 * (then is not None)):
                        high_x(then, 4 * i + (2 * j + m))
                    for m in range(2):
                        act.activation(SQT[:, m, :], XT[:, 4 * i + 2 * j + m, :], ACT.Square).then_inc(*T["sq_ready"].up())

                if loop:
                    with act.Fori(0, 2) as i:
                        group(i, 0)
                        group(i, 1)
                else:
                    for i in range(2):
                        group(i, 0)
                        group(i, 1)

            def feat(dst, i, b, func=ACT.Copy, scale=1.0):
                for m in range(2):
                    last = act.activation(dst[:, 2 * i + m, :], PS[:, b + m, :], func, scale=scale)
                return last

            def tok(dst, i, b, blocks=TB, scale=1.0):
                for t in range(0, blocks, 2):
                    last = act.activation(dst[:, t:t + 2, UC * i:UC * i + UC],
                                          PS[:, b + t // 2, :].rearrange("p (t c) -> p t c", t=2), ACT.Copy, scale=scale)
                return last

            act.dma_start(VEC[:, :], A["vec"]).then_inc(*T["vec_in"].up(16))
            for dst, name in ((IDENT, "c_ident"), (ONES, "c_ones"), (CEX, "c_cex")):
                act.dma_start(dst[:, :], A[name]).then_inc(*T["small_in"].up(16))
            act.wait_ge(T["vec_in"].sem, 16)
            act.activation(CS[:, :], col("cond", 0, 16), ACT.Silu).then_inc(*T["cond_ready"].up())
            act.wait_ge(T["x_upd"].sem, X0)
            for t in range(KT):
                high_x("ffn0", t)
                if t == 1:
                    split(0)

            def start_sums():
                for t in range(KT):
                    if t >= 2:
                        act.wait_ge(T["ss_acc"].sem, t - 1)
                    act.activation(SQT[:, t % 2, :], XT[:, t, :], ACT.Square).then_inc(*T["sq_ready"].up())
                act.wait_ge(*T["small_in"].now())
                logs_table()
                act.wait_ge(sm.sem, 1)
                act.activation(SPT[:, 1, :], SPT[:, 0, :], ACT.Exp, scale=-1.0).then_inc(*sm.up())
                act.wait_ge(sm.sem, 3)
                act.activation(SPT[:, 3, :], SPT[:, 2, :], ACT.Ln).then_inc(*sm.up())

            ffn(0, lead=start_sums)

            def prepare(k):
                split(U_HY + k + 1)

            def gate(g, dst):
                for m in range(4):
                    act.wait_ge(T["rg_mm"].sem, 4 * g + m + 1)
                    act.activation(dst[:, m, :], PS[:, m, :], ACT.Sigmoid, bias=col("gate_b", 4 * g + m)).then_inc(*T["rg_sig"].up())

            def squares(t0):
                act.wait_ge(T["evac"].sem, 4 if t0 < 4 else 6)
                for t in (t0, t0 + 1):
                    src = (hy["Q"] if t < 4 else hy["K"])[:, t % 4, :]
                    if t >= 2:
                        act.wait_ge(T["qk_ss"].sem, t - 1)
                    act.activation(SQT[:, t % 2, :], src, ACT.Square).then_inc(*T["qk_sq"].up())

            def roots(t0):
                logs_table()
                for t in (t0, t0 + 1):
                    act.wait_ge(T["qk_ss"].sem, t + 1)
                    if t >= 2:
                        act.wait_ge(T["qk_norm"].sem, t - 1)
                    else:
                        act.wait_ge(T["rg_b2"].sem, 4)
                    root_inverse(HT[:, t % 2, :], PS[:, t % 2, :], HD).then_inc(*T["qk_rms"].up())

            def gelu(i):
                act.wait_ge(T["evac"].sem, 7 + i)
                act.activation(hy["GT"][:, 2 * i:2 * i + 2, :], hy["GT"][:, 2 * i:2 * i + 2, :], ACT.Gelu_apprx_tanh).then_inc(*T["gelu_ready"].up())

            prepare(0)
            inverse(N_NORM["mix0"])
            for k in range(1, 5):
                prepare(k)
            gate(0, hy["R"])
            prepare(5)
            gate(1, hy["I"])
            prepare(6)
            act.wait_ge(*T["rg_sig"].now())
            act.wait_ge(T["xc_ready"].sem, 4)
            for m in range(4):
                act.activation(hy["UP"][:, m, 0:S], hy["R"][:, m, :], ACT.Exp, scale=LA(m)).then_inc(*st.up())
            act.wait_ge(*st.now())
            for m in range(4):
                act.activation(hy["R"][:, m, :], hy["R"][:, m, :], ACT.Tanh, scale=LAN(m)).then_inc(*T["rg_at"].up())
            squares(0)
            gelu(0)
            prepare(7)
            roots(0)
            squares(2)
            gelu(1)
            prepare(8)
            roots(2)
            squares(4)
            for m in range(4):
                act.wait_ge(T["rg_b2"].sem, m + 1)
                act.activation(hy["R"][:, m, :], hy["R"][:, m, :], ACT.Sqrt).then_inc(*T["rg_sq"].up())
            prepare(9)
            roots(4)
            squares(6)
            prepare(10)
            roots(6)
            act.wait_ge(T["f_abs"].sem, 1)
            fa = hy["PT"][0:8, 0, 0, :]
            act.activation(fa, fa, ACT.Exp, scale=-1.0).then_inc(*st.up())
            act.wait_ge(*st.now())
            act.activation(fa, fa, ACT.Ln, bias=1.0).then_inc(*T["f_ln"].up())
            act.wait_ge(T["const_in"].sem, 16 * 4)
            act.activation(hy["MASK"][:, :], hy["PT"][:, 1, 2, 0:P], ACT.Copy)
            act.activation(hy["EYE"][:, :], IDENT[:, :], ACT.Copy)
            act.activation(hy["SEL"][:, :, :].rearrange("p h q -> p (h q)"), hy["PT"][:, 1, 0:2, :].rearrange("p a c -> p (a c)"), ACT.Copy)\
                .then_inc(*T["fx_const"].up())
            act.wait_ge(T["c_ready"].sem, 1)
            act.activation(hy["CH"][:, 0, :], hy["PT"][:, 0, 3, :], ACT.Copy).then_inc(*T["c_hi"].up())
            for m in range(4):
                act.wait_ge(T["y_f32"].sem, m + 1)
                act.activation(HY_YH[m], hy["XC"][:, m, :], ACT.Copy).then_inc(*T["y_hi"].up())

            def fox_exp(h):
                for i in range(TB):
                    act.wait_ge(T["fx_max"].sem, TB * h + i + 1)
                    w = P * (i + 1)
                    act.activation(PX(h)[:, i, 0:w], PS[:, i, 0:w], ACT.Exp, bias=hy["ST"][:, h % 2, i:i + 1],
                                   accum_out=hy["ST"][:, h % 2, TB + i:TB + i + 1]).then_inc(*T["fx_exp"].up())

            def fox_pt(h):
                for j in range(TB):
                    act.wait_ge(T["fx_t"].sem, TB * h + j + 1)
                    if h >= 2:
                        act.wait_ge(T["fx_o"].sem, h - 1)
                    w = S - P * j
                    act.activation(hy["PT"][:, h % 2, j, 0:w], PS[:, 4 + j % 2, 0:w], ACT.Copy).then_inc(*T["fx_pt"].up())

            def fox_out(p):
                act.wait_ge(T["fx_o"].sem, 2 * p + 2)
                act.activation(HY_YH[4 + p], PS[:, 6 + p % 2, :], ACT.Copy).then_inc(*T["y_hi"].up())

            for h in range(FOXH):
                fox_exp(h)
                if h and h % 2 == 0:
                    fox_out(h // 2 - 1)
                fox_pt(h)
            fox_out(FOXH // 2 - 1)
            residual(RES["hy"], U_HYO, 1, True, "ffn1")
            ffn(1)
            ffn(2)

            act.wait_ge(T["const_in"].sem, 16 * 7)
            for n, name in enumerate(("TRI", "NONE", "MASK")):
                act.activation(sbm[name][:, :], sbm["W"][:, 0, P * n:P * n + P], ACT.Copy)
            act.activation(sbm["EYE"][:, :], IDENT[:, :], ACT.Copy).then_inc(*T["sb_const"].up())

            def sb_logs(h):
                E = sbm["E"][:, h % 2, :]
                act.wait_ge(T["sb_z"].sem, h + 1)
                if h >= 2:
                    act.wait_ge(T["sb_sl"].sem, h - 1)
                act.activation(E, zs(h)[:, 0:1280], ACT.Abs).then_inc(*st.up())
                act.wait_ge(*st.now())
                act.activation(E, E, ACT.Exp, scale=-1.0).then_inc(*st.up())
                act.wait_ge(*st.now())
                act.activation(E, E, ACT.Ln, bias=1.0).then_inc(*T["sb_ln"].up())

            def sb_weights(h):
                act.wait_ge(T["sb_tri"].sem, h + 1)
                if h == 0:
                    act.wait_ge(*T["sb_const"].now())
                if h >= 2:
                    act.wait_ge(T["sb_o"].sem, h - 1)
                act.activation(sbm["W"][:, h % 2, :], zs(h)[:, 0:1280], ACT.Exp).then_inc(*T["sb_exp"].up())

            def sb_out(h):
                if h % 2:
                    act.wait_ge(T["sb_o"].sem, h + 1)
                    act.activation(sby["YH"][:, h // 2, :], PS[:, 6, :], ACT.Copy).then_inc(*T["y_hi"].up())

            split(U_SB + 1)
            inverse(N_NORM["mix1"])
            split(U_SB + 2)
            split(U_SB + 3)
            logs_table()
            sb_logs(0)
            for h in range(SBH):
                if h + 1 < SBH:
                    sb_logs(h + 1)
                sb_weights(h)
                for k, s in sb_halves(h):
                    if s == 0:
                        split(U_SB + k + 1)
                if h >= 1:
                    sb_out(h - 1)
            sb_out(SBH - 1)
            residual(RES["sb"], U_SBO, 1, True, "ffn3")
            ffn(3)

            norm(N_NORM["norm1"], lambda kt: MOD[:, kt, 0:1])
            rots = [0]

            def prepare(k):
                split(U_B2 + k + 1)

            def take(k):
                (name, i), b = B2_VISITS[k][1], bank(k)
                act.wait_ge(T["visit_done"].sem, U_B2 + k + 1)
                if name in ("rq", "rk"):
                    scale = P ** -0.5 if name == "rk" else 1.0
                    for m in range(2):
                        if rots[0]:
                            act.wait_ge(T["rope_done"].sem, rots[0])
                        act.activation(b2[name.upper()][:, 2 * i + m, :], PS[:, b + m, :], ACT.Copy, scale=scale)
                        act.activation(b2["SW"][0:64, 0, :], PS[64:128, b + m, :], ACT.Copy, scale=scale)
                        last = act.activation(b2["SW"][64:128, 0, :], PS[0:64, b + m, :], ACT.Copy, scale=scale)
                        rots[0] += 1
                        if m == 0:
                            last.then_inc(*T["rope_sw"].up())
                elif name in ("cmg", "mg"):
                    lo, w = (0, SC) if name == "cmg" else (SC, S)
                    act.activation(gr["IG"][0:36, lo:lo + w], PS[0:36, b, 0:w], ACT.Identity, bias=col("ml_b", 0, rows=36))
                    last = act.activation(gr["FG"][0:36, lo:lo + w], PS[0:36, b + 1, 0:w], ACT.Identity, bias=col("ml_b", 1, rows=36))
                elif name == "rg":
                    last = feat(ml["RG"], i, b, ACT.Silu)
                elif name == "mo":
                    last = feat(mw["MO"], i, b, ACT.Sigmoid)
                elif name in ("br", "bm"):
                    last = feat(po["BG"], i % 2 + (2 if name == "bm" else 0), b, ACT.Sigmoid)
                else:
                    kind, scale = B2_VISITS[k][0], P ** -0.5 if name in ("crk", "mk", "cmk") else 1.0
                    if kind == "feat":
                        last = feat(b2[name.upper()], i, b, scale=scale)
                    else:
                        last = tok(b2[name.upper()], i, b, TB if kind == "tok" else 2, scale)
                last.then_inc(*T["evac"].up())

            prepare(0)
            for k in range(V_RET):
                if k == 2:
                    act.wait_ge(T["const_in"].sem, 16 * 9)
                    act.wait_ge(T["ss_acc"].sem, 8 * (N_NORM["norm1"] + 1))
                    for t in range(KT):
                        if t >= 2:
                            act.wait_ge(T["css_acc"].sem, t - 1)
                        act.activation(SQC(t), b2["CT"][:, t, :], ACT.Square).then_inc(*T["csq"].up())
                if k == 4:
                    logs_table()
                    act.wait_ge(T["css_sum"].sem, 1)
                    root_inverse(RINC, PS[:, 4, 0:SC], D).then_inc(*T["crms"].up())
                    for t in range(KT):
                        act.wait_ge(T["cht"].sem, t + 1)
                        act.activation(b2["HCH"][:, t, :], SQC(t), ACT.Identity, bias=MOD[:, t, 1:2]).then_inc(*T["chh"].up())
                take(k)
                prepare(k + 1)

            def retained(h):
                act.wait_ge(T["rt_o"].sem, h + 1)
                act.activation(b2["RQ"][:, h, :], PS[:, 3, :], ACT.Copy).then_inc(*T["rt_out"].up())

            for h in range(NH):
                act.wait_ge(T["rt_e"].sem, h + 1)
                act.activation(rw["MX"][:, :], rw["MX"][:, :], ACT.Exp).then_inc(*T["rt_x"].up())
                if h:
                    retained(h - 1)
                act.activation(rw["QF"][:, 0, :], rw["POS"][:, :], ACT.Exp, scale=LGS[:, h:h + 1]).then_inc(*T["rt_qx"].up())
                act.activation(rw["QF"][:, 1, :], rw["POS"][:, :], ACT.Exp, scale=LGS[:, 12 + h:13 + h],
                               bias=LGS[:, 16 + h:17 + h]).then_inc(*T["rt_qx"].up())
                if h:
                    act.wait_ge(T["rt_ks"].sem, h)
                act.activation(TE[:, 0:2], CEX[:, 0:2], ACT.Exp, scale=LGS[:, h:h + 1])
                act.activation(TE[:, 2:4], CEX[:, 2:4], ACT.Exp, scale=LGS[:, 4 + h:5 + h]).then_inc(*T["rt_ce"].up())
                take(V_RET + h)
                act.wait_ge(T["rt_st"].sem, h + 1)
                act.activation(rw["ST"][:, :, :].rearrange("p d v -> p (d v)"), PS[:, 2, 0:2 * P], ACT.Copy).then_inc(*T["rt_stc"].up())
                prepare(V_RET + h + 1)
            retained(NH - 1)

            act.wait_ge(T["ml_abs"].sem, 1)
            act.activation(mw["AB"][0:36, :], mw["AB"][0:36, :], ACT.Exp, scale=-1.0).then_inc(*st.up())
            act.wait_ge(*st.now())
            act.activation(mw["AB"][0:36, :], mw["AB"][0:36, :], ACT.Ln, bias=1.0).then_inc(*T["ml_ln"].up())
            take(V_PREP)
            prepare(V_PREP + 1)
            act.wait_ge(T["ml_gt"].sem, 1)
            act.activation(mw["GCOL"][:, :, :].rearrange("p a b -> p (a b)"), PS[:, 0, 0:216], ACT.Copy)
            act.activation(NGC[:, :], PS[:, 1, 0:8], ACT.Copy)
            act.activation(GCP[:, :], PS[:, 1, 0:8], ACT.Copy, scale=-1.0).then_inc(*T["ml_gc"].up())
            act.wait_ge(*T["ml_gc"].now())
            for k in range(2 * NH):
                r = 32 * (k % 2) + k // 2
                act.activation(WS[:, k, :], mw["GCOL"][:, 0:2, r], ACT.Exp, bias=NGC[:, k:k + 1]).then_inc(*T["ml_ws"].up())
            take(V_PREP + 1)
            prepare(V_PREP + 2)
            for h in range(NH):
                act.wait_ge(T["ml_c0"].sem, 2 * h + 2)
                act.activation(ml["C0"][:, h, :], PS[:, h, :], ACT.Copy).then_inc(*T["ml_c0c"].up())
            def weights(k):
                h, d = k // 2, k % 2
                act.wait_ge(T["ml_diag"].sem, k + 1)
                if k >= 2:
                    act.wait_ge(T["ml_num"].sem, k - 1)
                for j in range(TB):
                    lo, hi = (P * (j + 1), S) if d == 0 else (0, P * j)
                    r = 32 * d + h
                    if hi > lo:
                        act.activation(WM[d][:, j, lo:hi], PS[:, 2, lo:hi], ACT.Exp, bias=mw["GCOL"][:, 2 + j, r:r + 1])
                flat = WM[d][:, :, :].rearrange("p j t -> p (j t)")
                for ap in (flat[:, 0:1920].rearrange("p (a c) -> p a c", a=3)[:, :, 0:P], flat[:, 1920:2048]):
                    act.activation(ap, ap, ACT.Exp)
                act.activation(SQT[:, d, :], PS[:, 2, :], ACT.Exp, bias=GCP[:, k:k + 1])
                if k >= 2:
                    act.wait_ge(T["ml_den_read"].sem, k - 1)
                act.activation(HT[:, d, :], PS[:, 3, :], ACT.Exp).then_inc(*T["ml_w"].up())

            weights(0)
            take(V_PREP + 2)
            prepare(V_PREP + 3)
            weights(1)
            for h in range(NH):
                if h + 1 < NH:
                    weights(2 * h + 2)
                take(V_ML + h)
                prepare(V_ML + h + 1)
                if h + 1 < NH:
                    weights(2 * h + 3)

            for t in range(0, 8, 2):
                srcs = [b2["RQ" if t < 4 else "MQ"][:, (t + m) % 4, :] for m in range(2)]
                if t in (2, 4):
                    take(V_UP + t // 2)
                    prepare(V_UP + t // 2 + 1)
                for m in range(2):
                    act.wait_ge(T["hn_in"].sem, t + m - 3 if t >= 4 else 1)
                    if t:
                        act.wait_ge(T["hn_ss"].sem, t + m - 1)
                    act.activation(SQT[:, m, :], srcs[m], ACT.Square).then_inc(*T["hn_sq"].up())
                if t in (0, 4):
                    take(V_UP + 3 * t // 4)
                    prepare(V_UP + 3 * t // 4 + 1)
                logs_table()
                for m in range(2):
                    act.wait_ge(T["hn_ss"].sem, t + m + 1)
                    if t:
                        act.wait_ge(T["y_f32"].sem, 4 + t + m - 1)
                    root_inverse(HT[:, m, :], PS[:, m, :], P).then_inc(*T["hn_rms"].up())
                for m in range(2):
                    act.wait_ge(T["y_f32"].sem, 4 + t + m + 1)
                    act.activation(po["YH"][:, t + m, :], srcs[m], ACT.Copy).then_inc(*T["y_hi"].up())
            for i in range(2):
                k = V_UP + 6 * i
                if i:
                    for q in range(4):
                        take(k + q)
                        prepare(k + q + 1)
                prepare(k + 5)
                for m in range(4):
                    act.wait_ge(T["up_m"].sem, 4 * i + m + 1)
                    act.activation(po["MH"][:, 4 * i + m, :], SQT[:, m % 2, :], ACT.Copy).then_inc(*T["up_hi"].up())
                if i == 0:
                    prepare(k + 6)
            residual(RES["b2"], U_B2O, 1, False)
            ffn(4, lambda kt: MOD[:, 24 + kt, 0:1])
            norm(N_NORM["final"])

        @block.vector
        def _(dve):
            st, sm = T["dve_step"], T["small"]

            def split_lo(slot, u):
                dve.wait_ge(T["w_hi"].sem, u + 1)
                dve.tensor_tensor(WL[slot][:, :], RAW[slot][:, :], f32(WH[slot][:, :]), ALU.subtract).then_inc(*T["w_lo"].up())

            def split(u):
                if u < N_UNITS:
                    split_lo(u % 2, u)

            def split_at(base, per, i, off):
                split_lo((base + off) % 2, per * i + (base + off))

            def step(ins):
                ins.then_inc(*st.up())
                dve.wait_ge(*st.now())

            def low_x(m, name, t):
                dve.wait_ge(T["hh_ready"].sem, t + (8 * m + 1))
                dve.scalar_tensor_tensor(HL[:, t, :], XT[:, t, :], gain_of(name, t), f32(HH[:, t, :]), ALU.mult, ALU.subtract)\
                    .then_inc(*T["h_ready"].up())

            def norm(m, gain, shift=None):
                dve.wait_ge(T["rms_ready"].sem, m + 1)
                final = m == N_NORM["final"]

                def scaled(kt):
                    dst = XT[:, kt, :] if final else HT[:, kt % 2, :]
                    if kt >= 2 and not final:
                        dve.wait_ge(T["h_ready"].sem, 8 * m + kt - 1)
                    dve.scalar_tensor_tensor(dst, XT[:, kt, :], gain(kt), RINV[:, :], ALU.mult, ALU.mult).then_inc(*T["ht_ready"].up())

                def low(kt):
                    dve.wait_ge(T["hh_ready"].sem, 8 * m + kt + 1)
                    if shift is None:
                        ins = dve.tensor_tensor(HL[:, kt, :], HT[:, kt % 2, :], f32(HH[:, kt, :]), ALU.subtract)
                    else:
                        ins = dve.scalar_tensor_tensor(HL[:, kt, :], HT[:, kt % 2, :], shift(kt), f32(HH[:, kt, :]), ALU.add, ALU.subtract)
                    ins.then_inc(*T["h_ready"].up())

                scaled(0)
                for kt in range(KT):
                    if kt + 1 < KT:
                        scaled(kt + 1)
                    if not final:
                        low(kt)

            def sum_square(count, slot):
                dve.wait_ge(T["sq_ready"].sem, count + 1)
                dve.wait_ge(T["ss_acc"].sem, count)
                dve.tensor_tensor(SSACC[:, :], SSACC[:, :], SQT[:, slot, :], ALU.add).then_inc(*T["ss_acc"].up())

            def rms_columns():
                dve.wait_ge(T["rcol_mm"].sem, T["rcol_ready"].n + 1)
                dve.tensor_copy(RCOL[:, :], PS[:, 2 if T["rcol_ready"].n == 0 else 7, 0:TB]).then_inc(*T["rcol_ready"].up())
                dve.wait_ge(*T["rcol_ready"].now())

            def over_rms(dst, i, b, t0, blocks):
                for t in range(blocks):
                    last = dve.tensor_scalar(dst[:, t0 + t, UC * i:UC * i + UC], PS[:, b + t // 2, UC * (t % 2):UC * (t % 2) + UC],
                                             RCOL[:, t0 + t:t0 + t + 1], None, ALU.mult)
                return last

            def conditioning(u, h):
                dve.wait_ge(T["ada_in"].sem, 32 * u + 16 * h + 16)
                for k in range(4 * h, 4 * h + 4):
                    for j in range(2):
                        w, c = ADAW[:, UC * (k % 4):UC * (k % 4) + UC], CS[:, 2 * k + j:2 * k + j + 1]
                        if k == 0:
                            if not isinstance(u, int) or u > 0:
                                dve.wait_ge(T["ada_mm"].sem, u)
                            ins = dve.tensor_scalar(ACC[:, j, :], w, c, None, ALU.mult)
                        else:
                            dve.wait_ge(T["ada_step"].sem, 16 * u + (2 * k + j - 1))
                            ins = dve.scalar_tensor_tensor(ACC[:, j, :], w, c, ACC[:, j, :], ALU.mult, ALU.add)
                        ins.then_inc(T["ada_step"].sem, 1)

            def modulation(i, base):
                dve.wait_ge(T["ada_mm"].sem, i + (base + 1))
                for m in range(2):
                    ins = dve.tensor_copy(MOD[:, 2 * i + (2 * base + m), :], PS[:, 7, 2 * m:2 * m + 2])
                ins.then_inc(T["ada_mod"].sem, 1)

            def ffn(n, gain=None, shift=None, scale=0.5, lead=None):
                u0, m_ = U_FFN[n], N_NORM[FFN_NORM[n]]
                late = m_ < N_LATE
                if not late:
                    norm(m_, gain, shift)

                def scaled(i, first):
                    if first:
                        dve.wait_ge(T["rms_ready"].sem, m_ + 1)
                    if not first or n:
                        dve.wait_ge(T["g_mul"].sem, 2 * i + 22 * n)
                    dve.wait_ge(T["visit_done"].sem, 2 * i + (u0 + 1))
                    for m in range(2):
                        dve.tensor_tensor(SIL[:, m, :], PS[:, m, :], RINV[:, :], ALU.mult).then_inc(*T["a_ready"].up())

                def gated(i):
                    if not isinstance(i, int) or 22 * n + 2 * i > 0:
                        dve.wait_ge(T["g_ready"].sem, 2 * i + 22 * n)
                    for m in range(2):
                        dve.wait_ge(T["silu_ready"].sem, 2 * i + 22 * n + m + 1)
                        if m == 0:
                            dve.wait_ge(T["visit_done"].sem, 2 * i + u0 + 2)
                        if late:
                            dve.tensor_tensor(G[:, m, :], PS[:, 2 + m, :], RINV[:, :], ALU.mult).then_inc(*T["g_scaled"].up())
                        else:
                            dve.tensor_tensor(G[:, m, :], PS[:, 2 + m, :], SIL[:, m, :], ALU.mult).then_inc(*T["g_mul"].up())
                    for m in range(2 * late):
                        dve.wait_ge(T["g_scaled"].sem, 2 * i + (22 * n + m + 1))
                        dve.tensor_tensor(G[:, m, :], G[:, m, :], SIL[:, m, :], ALU.mult).then_inc(*T["g_mul"].up())
                    dve.wait_ge(T["gh_ready"].sem, i + 11 * n + 1)
                    for m in range(2):
                        dve.tensor_tensor(GL[:, 2 * i + m, :], G[:, m, :], f32(GH[:, 2 * i + m, :]), ALU.subtract).then_inc(*T["g_ready"].up())

                def pair(i, first, carry):
                    split_at(u0, 2, i, 1)
                    if not first:
                        gated(i - 1)
                    elif lead:
                        lead()
                    if carry:
                        if not first:
                            modulation(i - 1, ADA_PER * n)
                        conditioning(i + ADA_PER * n, 0)
                    split_at(u0, 2, i, 2)
                    if late:
                        scaled(i, first)
                    if carry:
                        conditioning(i + ADA_PER * n, 1)

                carries = n < N_ADA // ADA_PER
                pair(0, True, carries)
                with dve.Fori(1, ADA_PER) as i:
                    pair(i, False, carries)
                if carries:
                    modulation(ADA_PER - 1, ADA_PER * n)
                with dve.Fori(ADA_PER, FFN_IN // 2) as i:
                    pair(i, False, False)
                gated(FFN_IN // 2 - 1)
                residual(RES[f"ffn{n}"], u0 + FFN_IN, 3, n < 4, scale, ("mix0", "ffn2", "mix1", None, None)[n])

            def residual(r, u0, chunks, loop, scale, then=None):
                dve.memset(SSACC[:, :], 0.0).then_inc(*st.up())
                cleared = st.n

                def group(i, j):
                    for c in range(chunks):
                        if not (isinstance(i, int) and u0 + chunks * (2 * i + j) + c + 1 >= N_UNITS):
                            split_at(u0, 2 * chunks, i, chunks * j + c + 1)
                    dve.wait_ge(T["visit_done"].sem, 2 * chunks * i + (u0 + chunks * (j + 1)))
                    for m in range(2):
                        t = 4 * i + 2 * j + m
                        dve.scalar_tensor_tensor(XT[:, t, :], PS[:, 4 + 2 * j + m, :], scale if isinstance(scale, float) else scale(t),
                                                 XT[:, t, :], ALU.mult, ALU.add).then_inc(*T["x_upd"].up())
                    for m in range(2 * (then is not None)):
                        low_x(N_NORM[then], then, 4 * i + (2 * j + m))
                    dve.wait_ge(st.sem, cleared)
                    for m in range(2):
                        sum_square(4 * i + (8 * (r + 1) + 2 * j + m), m)

                if loop:
                    with dve.Fori(0, 2) as i:
                        group(i, 0)
                        group(i, 1)
                else:
                    for i in range(2):
                        group(i, 0)
                        group(i, 1)

            step(dve.memset(EPSC[:, :], EPS))
            step(dve.memset(SSACC[:, :], 0.0))
            dve.wait_ge(T["vec_in"].sem, 16)
            Z = col("soft", 0, 12)
            a, e, u, l, d, t, la, sp = (SPT[:, k, :] for k in range(8))
            dve.scalar_tensor_tensor(a, Z, -1.0, Z, ALU.mult, ALU.max).then_inc(*sm.up())
            for t_ in range(KT):
                low_x(N_NORM["ffn0"], "ffn0", t_)
                if t_ == 1:
                    split(0)

            def start_sums():
                for t_ in range(KT):
                    sum_square(t_, t_ % 2)
                dve.wait_ge(T["small_in"].sem, 48)
                dve.wait_ge(T["cond_ready"].sem, 1)
                dve.wait_ge(sm.sem, 2)
                sm.n = 2
                dve.tensor_scalar(u, e, 1.0, None, ALU.add).then_inc(*sm.up())
                dve.wait_ge(sm.sem, 4)
                step(dve.tensor_scalar(d, u, -1.0, 1e-7, ALU.add, ALU.max))
                step(dve.reciprocal(d, d))
                step(dve.tensor_tensor(l, l, e, ALU.mult))
                step(dve.tensor_tensor(l, l, d, ALU.mult))
                step(dve.scalar_tensor_tensor(t, u, 1.0, e, ALU.is_equal, ALU.mult))
                step(dve.tensor_tensor(l, l, t, ALU.add))
                step(dve.tensor_scalar(t, Z, -1.0, 0.0, ALU.mult, ALU.max))
                step(dve.tensor_tensor(sp, t, l, ALU.add))
                step(dve.tensor_scalar(SPT[:, 6, 0:4], SPT[:, 7, 0:4], -8.0, None, ALU.mult))
                step(dve.tensor_scalar(SPT[:, 6, 4:8], SPT[:, 7, 0:4], 8.0, None, ALU.mult))
                step(dve.tensor_scalar(LGS[:, 0:8], SPT[:, 7, 4:12], -1.0, None, ALU.mult))
                step(dve.tensor_copy(LGS[:, 8:16], SPT[:, 7, 4:12]))
                step(dve.tensor_scalar(LGS[:, 16:20], SPT[:, 7, 8:12], -(S + 1.0), None, ALU.mult))
                step(dve.tensor_scalar(QKG[:, 0:1], col("qk", 0), HD ** -0.5, None, ALU.mult))
                step(dve.tensor_copy(QKG[:, 1:2], col("qk", 1)))

            ffn(0, lead=start_sums)

            XC, R, I, UP = hy["XC"], hy["R"], hy["I"], hy["UP"]
            F1, F2, F0, C = hy["PT"][0:8, 0, 0, :], hy["PT"][0:8, 0, 1, :], hy["PT"][0:8, 0, 2, :], hy["PT"][:, 0, 3, :]

            def prepare(k):
                split(U_HY + k + 1)

            def convolve(m):
                taps = [UP[:, m, 1 + j:1 + j + S] for j in range(4)]
                step(dve.tensor_scalar(XC[:, m, :], taps[0], col("conv_w", m), col("conv_b", m), ALU.mult, ALU.add))
                for j in range(1, 4):
                    ins = dve.scalar_tensor_tensor(XC[:, m, :], taps[j], col("conv_w", 4 * j + m), XC[:, m, :], ALU.mult, ALU.add)
                    if j < 3:
                        step(ins)
                ins.then_inc(*T["xc_ready"].up())

            def gain(m):
                dve.wait_ge(T["rg_at"].sem, m + 1)
                if m:
                    dve.wait_ge(*T["rg_b2"].now())
                step(dve.tensor_tensor(HT[:, 0, :], UP[:, m, 0:S], UP[:, m, 0:S], ALU.mult))
                dve.scalar_tensor_tensor(R[:, m, :], HT[:, 0, :], 1.0, R[:, m, :], ALU.add, ALU.mult).then_inc(*T["rg_b2"].up())

            def recur(m):
                dve.wait_ge(T["rg_sq"].sem, m + 1)
                step(dve.tensor_tensor(I[:, m, :], I[:, m, :], R[:, m, :], ALU.mult))
                step(dve.tensor_tensor_scan(XC[:, m, :], UP[:, m, 0:S], I[:, m, :], 0.0, ALU.mult, ALU.add))
                dve.tensor_tensor(XC[:, m, :], XC[:, m, :], hy["GT"][:, m, :], ALU.mult).then_inc(*T["y_f32"].up())

            def normed(t):
                dst = (hy["Q"] if t < 4 else hy["K"])[:, t % 4, :]
                dve.wait_ge(T["qk_rms"].sem, t + 1)
                dve.scalar_tensor_tensor(dst, dst, QKG[:, t // 4:t // 4 + 1], HT[:, t % 2, :], ALU.mult, ALU.mult).then_inc(*T["qk_norm"].up())

            def take(k):
                (name, i), b = HY_VISITS[k][1], hy_bank(k)
                dve.wait_ge(T["visit_done"].sem, U_HY + k + 1)
                if name == "v":
                    last = over_rms(hy["V"], i, b, 0, TB)
                elif name == "f":
                    last = dve.tensor_tensor(F0, PS[0:8, b, :], RINV[0:8, :], ALU.mult)
                else:
                    dst, o = (UP, 4) if name == "u" else (hy["GT" if name == "gate" else name.upper()], 0)
                    for m in range(2):
                        last = dve.tensor_tensor(dst[:, 2 * i + m, o:S + o], PS[:, b + m, :], RINV[:, :], ALU.mult)
                last.then_inc(*T["evac"].up())

            prepare(0)
            dve.wait_ge(T["rms_ready"].sem, N_NORM["mix0"] + 1)
            dve.wait_ge(T["up_clear"].sem, 1)
            take(0)
            prepare(1)
            take(1)
            prepare(2)
            dve.wait_ge(T["evac"].sem, 2)
            convolve(0)
            convolve(1)
            take(2)
            prepare(3)
            convolve(2)
            convolve(3)
            take(3)
            prepare(4)
            take(4)
            prepare(5)
            take(5)
            dve.wait_ge(T["rg_sig"].sem, 8)
            dve.wait_ge(T["xc_ready"].sem, 4)
            for m in range(4):
                step(dve.tensor_tensor(I[:, m, :], I[:, m, :], XC[:, m, :], ALU.mult))
            gain(0)
            gain(1)
            prepare(6)
            gain(2)
            gain(3)
            take(6)
            prepare(7)
            normed(0)
            normed(1)
            take(7)
            prepare(8)
            normed(2)
            normed(3)
            take(8)
            rms_columns()
            dve.wait_ge(T["gelu_ready"].sem, 2)
            dve.wait_ge(T["rg_mm"].sem, 8)
            recur(0)
            prepare(9)
            recur(1)
            recur(2)
            normed(4)
            normed(5)
            take(9)
            dve.wait_ge(T["evac"].sem, 9)
            step(dve.tensor_scalar(F0, F0, col("fox_b", rows=8), None, ALU.add))
            dve.scalar_tensor_tensor(F1, F0, -1.0, F0, ALU.mult, ALU.max).then_inc(*T["f_abs"].up())
            step(dve.memset(F2, 1.0))
            step(dve.memset(C, 0.0))
            recur(3)
            prepare(10)
            normed(6)
            normed(7)
            dve.wait_ge(T["f_ln"].sem, 1)
            step(dve.scalar_tensor_tensor(F0, F0, 0.0, F1, ALU.min, ALU.subtract))
            dve.tensor_tensor_scan(C[0:8, :], F2, F0, 0.0, ALU.mult, ALU.add).then_inc(*T["c_ready"].up())
            take(10)
            dve.wait_ge(T["c_hi"].sem, 1)
            dve.tensor_tensor(hy["CH"][:, 1, :], C, f32(hy["CH"][:, 0, :]), ALU.subtract).then_inc(*T["c_lo"].up())
            for m in range(4):
                dve.wait_ge(T["y_hi"].sem, m + 1)
                dve.tensor_tensor(HY_YL[m], XC[:, m, :], f32(HY_YH[m]), ALU.subtract).then_inc(*T["y_ready"].up())

            def fox_max(h):
                if h >= 2:
                    dve.wait_ge(T["fx_p"].sem, TB * (h - 1))
                for i in range(TB):
                    dve.wait_ge(T["fx_s"].sem, TB * h + i + 1)
                    dve.tensor_reduce(hy["ST"][:, h % 2, i:i + 1], PS[:, i, 0:P * (i + 1)], AX, ALU.max, negate=True).then_inc(*T["fx_max"].up())

            def fox_norm(h):
                dve.wait_ge(T["fx_exp"].sem, TB * (h + 1))
                sums = hy["ST"][:, h % 2, TB:2 * TB]
                step(dve.reciprocal(sums, sums))
                for i in range(TB):
                    p = PX(h)[:, i, 0:P * (i + 1)]
                    dve.tensor_scalar(p, p, hy["ST"][:, h % 2, TB + i:TB + i + 1], None, ALU.mult).then_inc(*T["fx_p"].up())

            def out_low(y, hi, lo, src):
                dve.wait_ge(T["y_hi"].sem, y)
                dve.tensor_tensor(lo, src, f32(hi), ALU.subtract).then_inc(*T["y_ready"].up())

            for h in range(FOXH):
                fox_max(h)
                fox_norm(h)
                if h and h % 2 == 0 or h == FOXH - 1:
                    p = (h - 1) // 2
                    out_low(5 + p, HY_YH[4 + p], HY_YL[4 + p], PS[:, 6 + p % 2, :])
            residual(RES["hy"], U_HYO, 1, True, 1.0, "ffn1")
            ffn(1)
            ffn(2)

            dve.wait_ge(T["ada_mod"].sem, N_ADA)
            for j in range(2):
                step(dve.tensor_tensor(MOD[:, :, j], MOD[:, :, j], col("b_ada", 0, 48), ALU.add))
            for k, (g, lo, j) in enumerate((("norm1", 8, 0), ("norm1", 8, 1), ("norm2", 32, 0))):
                ins = dve.scalar_tensor_tensor(CSC[:, k, :], MOD[:, lo:lo + 8, j], 1.0, col(g, 0, 8), ALU.add, ALU.mult)
                if k < 2:
                    step(ins)
            ins.then_inc(*T["mod_ready"].up())
            dve.wait_ge(*T["mod_ready"].now())

            def take_half(k, s, b=None):
                name, i = SB_VISITS[k][1]
                if s or b is not None:
                    dve.wait_ge(T["visit_done"].sem, U_SB + k + 1)
                else:
                    dve.wait_ge(T["sb_half"].sem, k - 2)
                if name == "v":
                    last = over_rms(sbm["V"], i, 7 if b is None else b, 2 * s, 2)
                else:
                    last = dve.scalar_tensor_tensor(sbm[name.upper()][:, 2 * i + s, :], PS[:, 7 if b is None else b, :],
                                                    HD ** -0.5 if name == "q" else 1.0, RINV[:, :], ALU.mult, ALU.mult)
                if s:
                    last.then_inc(*T["evac"].up())
                elif b is None:
                    last.then_inc(*T["sb_half_out"].up())

            for k in range(3):
                split(U_SB + k + 1)
                if k == 0:
                    dve.wait_ge(T["rms_ready"].sem, N_NORM["mix1"] + 1)
                if k == 2:
                    rms_columns()
                take_half(k, 0, 2 * k)
                take_half(k, 1, 2 * k + 1)

            def sb_soft(h):
                E = sbm["E"][:, h % 2, :]
                dve.wait_ge(T["sb_ln"].sem, h + 1)
                if h >= 2:
                    dve.wait_ge(T["sb_tri"].sem, h - 1)
                step(dve.scalar_tensor_tensor(E, zs(h)[:, 0:1280], 0.0, E, ALU.max, ALU.add))
                step(dve.tensor_copy(sbm["SH"][:, h % 2, :], E))
                dve.tensor_tensor(sbm["SL"][:, h % 2, :], E, f32(sbm["SH"][:, h % 2, :]), ALU.subtract).then_inc(*T["sb_sl"].up())

            def sb_low(h):
                if h % 2:
                    out_low(9 + h // 2, sby["YH"][:, h // 2, :], sby["YL"][:, h // 2, :], PS[:, 6, :])

            for h in range(SBH):
                sb_soft(h)
                for k, s in sb_halves(h):
                    take_half(k, s)
                    if s == 0:
                        split(U_SB + k + 1)
                if h >= 1:
                    sb_low(h - 1)
            sb_low(SBH - 1)
            residual(RES["sb"], U_SBO, 1, True, 1.0, "ffn3")
            ffn(3)

            norm(N_NORM["norm1"], lambda kt: CSC[:, 0, kt:kt + 1], lambda kt: MOD[:, kt, 0:1])

            def prepare(k):
                split(U_B2 + k + 1)

            prepare(0)
            for k in range(V_RET):
                if k == 2:
                    step(dve.memset(SSC, 0.0))
                    for t_ in range(KT):
                        dve.wait_ge(T["csq"].sem, t_ + 1)
                        dve.tensor_tensor(SSC, SSC, SQC(t_), ALU.add).then_inc(*T["css_acc"].up())
                        dve.wait_ge(*T["css_acc"].now())
                if k == 4:
                    dve.wait_ge(T["crms"].sem, 1)
                    for t_ in range(KT):
                        if t_ >= 2:
                            dve.wait_ge(T["ch_ready"].sem, t_ - 1)
                        dve.scalar_tensor_tensor(SQC(t_), b2["CT"][:, t_, :], CSC[:, 1, t_:t_ + 1], RINC, ALU.mult, ALU.mult).then_inc(*T["cht"].up())
                        dve.wait_ge(T["chh"].sem, t_ + 1)
                        dve.scalar_tensor_tensor(b2["HCL"][:, t_, :], SQC(t_), MOD[:, t_, 1:2], f32(b2["HCH"][:, t_, :]), ALU.add,
                                                 ALU.subtract).then_inc(*T["ch_ready"].up())
                name, i = B2_VISITS[k][1]
                if name in ("rq", "rk"):
                    dve.wait_ge(T["const_in"].sem, 16 * 9)
                    for m in range(2):
                        q = b2[name.upper()][:, 2 * i + m, :]
                        if m == 0:
                            dve.wait_ge(T["rope_sw"].sem, T["rot_in"].n + 1)
                            T["rot_in"].n += 1
                        else:
                            dve.wait_ge(T["evac"].sem, ev(k))
                        step(dve.tensor_tensor(b2["SW"][:, 0, :], b2["SW"][:, 0, :], b2["ROPE"][:, 1, :], ALU.mult))
                        step(dve.tensor_tensor(q, q, b2["ROPE"][:, 0, :], ALU.mult))
                        dve.tensor_tensor(q, q, b2["SW"][:, 0, :], ALU.add).then_inc(*T["rope_done"].up())
                prepare(k + 1)

            dve.wait_ge(T["const_in"].sem, 16 * 11)
            dve.wait_ge(T["evac"].sem, ev(V_RET - 1))
            MX, SM, KS = rw["MX"], rw["SM"], rw["KS"]
            for h in range(NH):
                if h:
                    dve.wait_ge(T["rt_sm"].sem, TB * h)
                step(dve.tensor_scalar(MX[:, :], rw["REL"][:, :], LGS[:, 12 + h:13 + h], None, ALU.mult))
                dve.scalar_tensor_tensor(MX[:, :], rw["REL"][:, :], LGS[:, h:h + 1], MX[:, :], ALU.mult, ALU.min).then_inc(*T["rt_e"].up())
                dve.wait_ge(T["rt_x"].sem, h + 1)
                step(dve.tensor_tensor(MX[:, 384:512], MX[:, 384:512], IDENT[:, :], ALU.add))
                for d_ in range(2):
                    dve.wait_ge(T["rt_qx"].sem, 2 * h + d_ + 1)
                    dve.tensor_tensor(rw["QF"][:, d_, :], rw["QF"][:, d_, :], b2["RQ"][:, h, :], ALU.mult).then_inc(*T["rt_q"].up())
                dve.wait_ge(T["rt_ce"].sem, h + 1)
                if h:
                    dve.wait_ge(T["rt_st"].sem, h)
                for k in range(4):
                    last = dve.tensor_scalar(KS[:, k, :], b2["CRK"][:, k % 2, P * h:P * h + P], TE[:, k:k + 1], None, ALU.mult)
                last.then_inc(*T["rt_ks"].up())
                if h:
                    dve.wait_ge(T["rt_o"].sem, h)
                for j in range(TB):
                    dve.wait_ge(T["rt_s"].sem, TB * h + j + 1)
                    dve.tensor_tensor(SM[:, j, :], PS[:, j % 2, :], MX[:, 384 - P * j:896 - P * j], ALU.mult).then_inc(*T["rt_sm"].up())
                prepare(V_RET + h + 1)

            IG, FG, F, GM, ONE = gr["IG"], gr["FG"], mw["F"], mw["GM"], mw["ONE"]
            dve.wait_ge(T["rt_out"].sem, NH)
            dve.scalar_tensor_tensor(mw["AB"][0:36, :], FG[0:36, :], -1.0, FG[0:36, :], ALU.mult, ALU.max).then_inc(*T["ml_abs"].up())
            step(dve.memset(F[0:36, :], 0.0))
            step(dve.memset(GM[0:36, :], 0.0))
            step(dve.memset(ONE[0:36, :], 1.0))
            dve.wait_ge(T["ml_ln"].sem, 1)
            step(dve.scalar_tensor_tensor(FG[0:36, :], FG[0:36, :], 0.0, mw["AB"][0:36, :], ALU.min, ALU.subtract))

            def both_scans(dst, src, op):
                for rows, c, x, end in ((slice(0, 4), (lambda t: t[0:4, 0:SC]), (lambda t: t[0:4, SC:SC + S]), dst[0:4, SC - 1:SC]),
                                        (slice(32, 36), (lambda t: t[32:36, 0:SC][:, ::-1]), (lambda t: t[32:36, SC:SC + S][:, ::-1]), dst[32:36, 0:1])):
                    step(dve.tensor_tensor_scan(c(dst), ONE[rows, 0:SC], c(src), 0.0, ALU.mult, op))
                    step(dve.tensor_tensor_scan(x(dst), ONE[rows, 0:S], x(src), end, ALU.mult, op))

            both_scans(F, FG, ALU.add)
            step(dve.tensor_tensor(IG[0:36, :], IG[0:36, :], F[0:36, :], ALU.subtract))
            both_scans(GM, IG, ALU.max)
            dve.tensor_tensor(F[0:36, :], F[0:36, :], GM[0:36, :], ALU.add).then_inc(*T["ml_rows"].up())
            prepare(V_PREP + 1)
            for k in range(2 * NH):
                dve.wait_ge(T["ml_ws"].sem, k + 1)
                if k >= 2:
                    dve.wait_ge(T["ml_c0"].sem, k - 1)
                for c in range(2):
                    last = dve.tensor_scalar(mw["KS"][:, k % 2, c, :], b2["CMK"][:, c, P * (k // 2):P * (k // 2) + P], WS[:, k, c:c + 1], None, ALU.mult)
                last.then_inc(*T["ml_ks"].up())
            prepare(V_PREP + 2)

            def own_keys(k):
                d_, r = k % 2, 32 * (k % 2) + k // 2
                dve.wait_ge(T["ml_g"].sem, k + 1)
                for j in range(TB):
                    t = slice(P * j, P * j + P)
                    last = dve.scalar_tensor_tensor(WM[d_][:, j, t], PS[:, 2, t], mw["GCOL"][:, 2 + j, r:r + 1], mw["MSK"][:, d_, :], ALU.add, ALU.add)
                last.then_inc(*T["ml_diag"].up())

            def key_sums(k):
                d_ = k % 2
                order = range(TB) if d_ == 0 else range(TB - 1, -1, -1)
                if k:
                    dve.wait_ge(T["ml_den"].sem, k)
                dve.wait_ge(T["ml_qw"].sem, k + 1)
                dve.wait_ge(T["ml_sm"].sem, TB * (k // 2 + 1))
                for n, j in enumerate(order):
                    lo, hi = span(d_, j)
                    if n == 0:
                        ins = dve.scalar_tensor_tensor(DSUM, mw["QW"][:, d_, :], C0N(k)[:, P:P + 1], WM[d_][:, j, :], ALU.mult, ALU.add)
                    else:
                        ins = dve.tensor_tensor(DSUM[:, lo:hi], DSUM[:, lo:hi], WM[d_][:, j, lo:hi], ALU.add)
                    if n < TB - 1:
                        step(ins)
                ins.then_inc(*T["ml_den_in"].up())

            dve.wait_ge(T["const_in"].sem, 16 * 13)
            own_keys(0)
            prepare(V_PREP + 3)
            own_keys(1)
            for h in range(NH):
                def inter(d_):
                    if h:
                        dve.wait_ge(T["ml_num"].sem, 2 * h + d_ - 1)
                    dve.tensor_tensor(mw["QW"][:, d_, :], b2["MQ"][:, h, :], SQT[:, d_, :], ALU.mult).then_inc(*T["ml_qw"].up())

                dve.wait_ge(T["ml_w"].sem, 2 * h + 1)
                inter(0)
                dve.wait_ge(T["ml_w"].sem, 2 * h + 2)
                for j in range(TB):
                    dve.wait_ge(T["ml_s"].sem, TB * h + j + 1)
                    for d_ in range(2):
                        lo, hi = span(d_, j)
                        last = dve.tensor_tensor(WM[d_][:, j, lo:hi], PS[:, j % 2, lo:hi], WM[d_][:, j, lo:hi], ALU.mult)
                    last.then_inc(*T["ml_sm"].up())
                    if j == 1:
                        inter(1)
                for d_ in range(2):
                    k = 2 * h + d_
                    if d_ == 0:
                        key_sums(k)
                    den = RINV[:, :]
                    if k:
                        dve.wait_ge(T["ml_h"].sem, k)
                    dve.wait_ge(T["ml_den"].sem, k + 1)
                    step(dve.scalar_tensor_tensor(den, PS[:, 5, :], -1.0, HT[:, d_, :], ALU.mult, ALU.max))
                    dve.tensor_tensor(den, PS[:, 5, :], den, ALU.max).then_inc(*T["ml_den_read"].up())
                    dve.wait_ge(*T["ml_den_read"].now())
                    step(dve.reciprocal(den, den))
                    if d_ and h + 1 < NH:
                        own_keys(k + 2)
                    dve.wait_ge(T["ml_num"].sem, k + 1)
                    if d_ == 0:
                        dve.tensor_tensor(SSACC[:, :], PS[:, 4, :], den, ALU.mult).then_inc(*T["ml_h"].up())
                        key_sums(k + 1)
                        if h + 1 < NH:
                            own_keys(k + 2)
                    else:
                        step(dve.tensor_tensor(den, PS[:, 4, :], den, ALU.mult))
                        dve.wait_ge(T["ml_h"].sem, k)
                        dve.tensor_tensor(b2["MQ"][:, h, :], SSACC[:, :], den, ALU.add).then_inc(*T["ml_h"].up())
                        prepare(V_ML + h + 1)

            dve.wait_ge(T["evac"].sem, ev(V_UP - 1))
            for m in range(4):
                dve.wait_ge(*T["ml_h"].now())
                dve.tensor_tensor(b2["MQ"][:, m, :], b2["MQ"][:, m, :], mw["MO"][:, m, :], ALU.mult).then_inc(*T["hn_in"].up())
            for t_ in range(8):
                y = b2["RQ" if t_ < 4 else "MQ"][:, t_ % 4, :]
                if t_ % 2 == 0:
                    prepare(V_UP + t_ // 2 + 1)
                dve.wait_ge(T["hn_rms"].sem, t_ + 1)
                dve.wait_ge(T["hn_in"].sem, 4)
                ins = dve.tensor_tensor(y, y, HT[:, t_ % 2, :], ALU.mult)
                if t_ < 4:
                    step(ins)
                    ins = dve.tensor_tensor(y, y, ml["RG"][:, t_, :], ALU.mult)
                ins.then_inc(*T["y_f32"].up())
                if t_ % 2:
                    for t in (t_ - 1, t_):
                        dve.wait_ge(T["y_f32"].sem, 4 + t + 1)
                        dve.wait_ge(T["y_hi"].sem, 16 + t + 1)
                        y = b2["RQ" if t < 4 else "MQ"][:, t % 4, :]
                        dve.tensor_tensor(po["YL"][:, t, :], y, f32(po["YH"][:, t, :]), ALU.subtract).then_inc(*T["y_ready"].up())
            for i in range(2):
                k = V_UP + 6 * i
                if i:
                    for q in range(4):
                        prepare(k + q + 1)
                prepare(k + 5)
                dve.wait_ge(T["evac"].sem, ev(k + 3))

                def products_ret(m):
                    t = 4 * i + m
                    if t >= 2:
                        dve.wait_ge(T["m_ready"].sem, t - 1)
                    dve.wait_ge(T["visit_done"].sem, U_B2 + k + 5)
                    dve.tensor_tensor(HT[:, m % 2, :], PS[:, 4 + m, :], po["BG"][:, m, :], ALU.mult).then_inc(*T["up_c"].up())

                def products_ml(m):
                    dve.wait_ge(T["visit_done"].sem, U_B2 + k + 6)
                    dve.tensor_tensor(SQT[:, m % 2, :], PS[:, m, :], po["BG"][:, 4 + m, :], ALU.mult).then_inc(*T["up_c"].up())

                def merged(m):
                    dve.wait_ge(T["up_c"].sem, 8 * i + (4 if m < 2 else 2 * m + 2))
                    dve.tensor_tensor(SQT[:, m % 2, :], HT[:, m % 2, :], SQT[:, m % 2, :], ALU.add).then_inc(*T["up_m"].up())

                def low(m):
                    dve.wait_ge(T["up_hi"].sem, 4 * i + m + 1)
                    dve.tensor_tensor(po["ML"][:, 4 * i + m, :], SQT[:, m % 2, :], f32(po["MH"][:, 4 * i + m, :]), ALU.subtract)\
                        .then_inc(*T["m_ready"].up())

                products_ret(0)
                products_ret(1)
                products_ml(0)
                products_ml(1)
                for m in (0, 2):
                    merged(m)
                    merged(m + 1)
                    for q in (m, m + 1):
                        low(q)
                        if m == 0:
                            products_ret(q + 2)
                            products_ml(q + 2)
                if i == 0:
                    prepare(k + 6)
            residual(RES["b2"], U_B2O, 1, False, lambda t: MOD[:, 16 + t, 0:1])
            ffn(4, lambda kt: CSC[:, 2, kt:kt + 1], lambda kt: MOD[:, 24 + kt, 0:1], lambda t: MOD[:, 40 + t, 0:1])
            norm(N_NORM["final"], lambda kt: col("final", kt))

        @block.tensor
        def _(pe):
            def three(out, wh, wl, xh, xl, start, stop):
                pe.matmul(out, wh, xh, start=start, stop=False)
                pe.matmul(out, wh, xl, start=False, stop=False)
                return pe.matmul(out, wl, xh, start=False, stop=stop)

            def tile(x, k, tokens):
                return x[k][:, 0:tokens] if isinstance(x, list) else x[:, k, 0:tokens]

            def feature_major(slot, xh, xl, banks, tokens=S, k0=0, n=KT, start=True, stop=True, width=UC, ready=None, by=None, m0=0,
                              w0=0):
                wh, wl = (w[slot][:, :].rearrange("p (k c) -> p k c", c=width) for w in (WH, WL))
                for k in range(n):
                    if ready is not None:
                        pe.wait_ge(by or T["h_ready"].sem, ready + k + 1)
                    for m, b in enumerate(banks):
                        c = slice(P * (m0 + m), P * (m0 + m) + P)
                        last = three(PS[:, b, 0:tokens], wh[:, w0 + k, c], wl[:, w0 + k, c], tile(xh, k0 + k, tokens), tile(xl, k0 + k, tokens),
                                     start and k == 0, stop and k == n - 1)
                return last

            def token_major(slot, xh, xl, b, blocks, t0=0):
                wh, wl = (w[slot][:, :].rearrange("p (k c) -> p k c", c=UC) for w in (WH, WL))
                for t in range(blocks):
                    out = PS[:, b + t // 2, UC * (t % 2):UC * (t % 2) + UC]
                    c = slice(P * (t0 + t), P * (t0 + t) + P)
                    for k in range(KT):
                        last = three(out, xh[:, k, c], xl[:, k, c], wh[:, k, :], wl[:, k, :], k == 0, k == KT - 1)
                return last

            def norm(m):
                pe.wait_ge(T["ss_acc"].sem, 8 * (m + 1))
                pe.matmul(PS[:, 4, :], ONES[:, :], SSACC[:, :], start=True, stop=True).then_inc(*T["ss_sum"].up())

            def rms_columns(b):
                for t in range(TB):
                    last = pe.matmul(PS[:, b, t:t + 1], RINV[:, P * t:P * t + P], IDENT[:, 0:1], start=True, stop=True)
                last.then_inc(*T["rcol_mm"].up())

            def ffn(n):
                m = N_NORM[FFN_NORM[n]]
                u0, late = U_FFN[n], m < N_LATE
                if not late:
                    norm(m)

                carries = n < N_ADA // ADA_PER

                def conditioning(i):
                    u = i + ADA_PER * n
                    pe.wait_ge(T["ada_step"].sem, 16 * i + (16 * ADA_PER * n + 16))
                    if not isinstance(i, int) or u > 0:
                        pe.wait_ge(T["ada_mod"].sem, u)
                    for m in range(2):
                        for j in range(2):
                            last = pe.matmul(PS[:, 7, 2 * m + j:2 * m + j + 1], ACC[:, j, P * m:P * m + P], ONES[:, 0:1], start=True, stop=True)
                    last.then_inc(T["ada_mm"].sem, 1)

                def pair(i, first, carry):
                    for s, banks in ((0, (0, 1)), (1, (2, 3))):
                        pe.wait_ge(T["w_lo"].sem, 2 * i + (u0 + s + 1))
                        if not first:
                            pe.wait_ge(T["g_mul" if s else "a_ready" if late else "silu_ready"].sem, 2 * i + 22 * n)
                        feature_major((u0 + s) % 2, HH, HL, banks, ready=8 * m if first and s == 0 else None)\
                            .then_inc(*T["visit_done"].up())
                        if late and first and s == 0:
                            norm(m)
                    if carry:
                        conditioning(i)

                pair(0, True, carries)
                with pe.Fori(1, ADA_PER) as i:
                    pair(i, False, carries)
                with pe.Fori(ADA_PER, FFN_IN // 2) as i:
                    pair(i, False, False)
                residual(RES[f"ffn{n}"], u0 + FFN_IN, FFN_CHUNKS, GH, GL, n < 4, 22 * n)

            def residual(r, u0, chunks, xh, xl, loop, g0=None, tiles=None):
                def group(i, j):
                    for c, n in enumerate(chunks):
                        u = u0 + len(chunks) * j + c
                        pe.wait_ge(T["w_lo"].sem, 2 * len(chunks) * i + (u + 1))
                        if g0 is not None:
                            pe.wait_ge(T["g_ready"].sem, g0 + sum(chunks[:c + 1]))
                        if c == 0:
                            pe.wait_ge(T["x_upd"].sem, 4 * i + (X0 + 8 * r + 2 * j - 2))
                        feature_major(u % 2, xh, xl, (4 + 2 * j, 5 + 2 * j), k0=sum(chunks[:c]), n=n, start=c == 0,
                                      ready=0 if tiles is not None and u == u0 and isinstance(i, int) and i == 0 else None, by=tiles,
                                      stop=c == len(chunks) - 1).then_inc(*T["visit_done"].up())

                if loop:
                    with pe.Fori(0, 2) as i:
                        group(i, 0)
                        group(i, 1)
                else:
                    for i in range(2):
                        group(i, 0)
                        group(i, 1)

            def project(u, kind, b, ready=None):
                pe.wait_ge(T["w_lo"].sem, u + 1)
                if kind in ("feat", "gates", "gates1"):
                    last = feature_major(u % 2, HH, HL, (b,) if kind == "gates1" else (b, b + 1), ready=ready)
                elif kind == "cgates":
                    last = feature_major(u % 2, b2["HCH"], b2["HCL"], (b, b + 1), tokens=SC)
                elif kind == "tok":
                    last = token_major(u % 2, HH, HL, b, TB)
                else:
                    last = token_major(u % 2, b2["HCH"], b2["HCL"], b, 2)
                last.then_inc(*T["visit_done"].up())

            pe.wait_ge(*T["small_in"].now())
            ffn(0)

            def visit(k):
                if k >= 4:
                    pe.wait_ge(T["evac"].sem, EV["hy"] + k - 1)
                project(U_HY + k, HY_VISITS[k][0], hy_bank(k), 8 * N_NORM["mix0"] if k == 0 else None)

            def gates(g):
                for m in range(4):
                    pe.wait_ge(T["xc_ready"].sem, m + 1)
                    if g:
                        pe.wait_ge(T["rg_sig"].sem, m + 1)
                    pe.matmul(PS[:, m, :], hy["BD"][:, 4 * g + m, :], hy["XC"][:, m, :], start=True, stop=True).then_inc(*T["rg_mm"].up())

            def head_sums(t0):
                for t in (t0, t0 + 1):
                    pe.wait_ge(T["qk_sq"].sem, t + 1)
                    if t >= 2:
                        pe.wait_ge(T["qk_rms"].sem, t - 1)
                    pe.matmul(PS[:, t % 2, :], hy["B64"][:, :], SQT[:, t % 2, :], start=True, stop=True).then_inc(*T["qk_ss"].up())

            for k in range(5):
                if k == 2:
                    pe.wait_ge(T["rms_ready"].sem, N_NORM["mix0"] + 1)
                visit(k)
                if k == 0:
                    norm(N_NORM["mix0"])
            pe.wait_ge(T["const_in"].sem, 16 * 4)
            gates(0)
            visit(5)
            gates(1)
            visit(6)
            pe.wait_ge(T["rg_sig"].sem, 8)
            head_sums(0)
            visit(7)
            head_sums(2)
            rms_columns(2)
            visit(8)
            head_sums(4)
            visit(9)
            head_sums(6)
            visit(10)
            pe.wait_ge(T["evac"].sem, EV["sb"])

            def fox_scores(h):
                r = slice(64 * (h % 2), 64 * (h % 2) + 64)
                for i in range(TB):
                    w = P * (i + 1)
                    if h:
                        pe.wait_ge(T["fx_exp"].sem, TB * (h - 1) + i + 1)
                    o = PS[:, i, 0:w]
                    pe.matmul(o, hy["Q"][r, h // 2, P * i:w], hy["K"][r, h // 2, 0:w], start=True, stop=False)
                    pe.matmul(PS[:, i, P * i:w], hy["EYE"][:, :], hy["MASK"][:, :], start=False, stop=False, skip_group_check=True)
                    pe.matmul(o, hy["SEL"][:, h, :], hy["CH"][:, 0, 0:w], start=False, stop=False)
                    pe.matmul(o, hy["SEL"][:, h, :], hy["CH"][:, 1, 0:w], start=False, stop=True)\
                        .then_inc(*T["fx_s"].up())

            def values(out_bank, h, v, probs, widths):
                r = slice(64 * (h % 2), 64 * (h % 2) + 64)
                for j in range(TB):
                    last = pe.matmul(PS[r, out_bank, P * j:S], v[:, j, HD * h:HD * h + HD], probs(j), start=j == 0, stop=True,
                                     skip_group_check=True)
                return last

            pe.wait_ge(T["qk_norm"].sem, 8)
            pe.wait_ge(T["c_lo"].sem, 1)
            pe.wait_ge(T["fx_const"].sem, 1)
            fox_scores(0)
            for h in range(FOXH):
                if h + 1 < FOXH:
                    fox_scores(h + 1)
                for j in range(TB):
                    n = TB * h + j
                    if n >= 2:
                        pe.wait_ge(T["fx_pt"].sem, n - 1)
                    for i in range(j, TB):
                        pe.wait_ge(T["fx_p"].sem, TB * h + i + 1)
                        last = pe.transpose(PS[:, 4 + j % 2, P * (i - j):P * (i - j) + P], PX(h)[:, i, P * j:P * j + P], IDENT[:, :])
                    last.then_inc(*T["fx_t"].up())
                pe.wait_ge(T["fx_pt"].sem, TB * (h + 1))
                if h >= 4 and h % 2 == 0:
                    pe.wait_ge(T["y_ready"].sem, 4 + h // 2 - 1)
                values(6 + h // 2 % 2, h, hy["V"], lambda j: hy["PT"][:, h % 2, j, 0:S - P * j], None).then_inc(*T["fx_o"].up())
            pe.wait_ge(T["y_ready"].sem, 8)
            residual(RES["hy"], U_HYO, (8,), HY_YH, HY_YL, True)
            ffn(1)
            ffn(2)

            for k in range(3):
                if k == 2:
                    pe.wait_ge(T["rms_ready"].sem, N_NORM["mix1"] + 1)
                    rms_columns(7)
                project(U_SB + k, SB_VISITS[k][0], 2 * k, 8 * N_NORM["mix1"] if k == 0 else None)
                if k == 0:
                    norm(N_NORM["mix1"])
            pe.wait_ge(T["rcol_ready"].sem, 2)
            pe.wait_ge(T["sb_const"].sem, 1)

            def half(k, s):
                u = U_SB + k
                if s == 0:
                    pe.wait_ge(T["w_lo"].sem, u + 1)
                    pe.wait_ge(T["evac"].sem, EV["sb"] + k)
                else:
                    pe.wait_ge(T["sb_half_out"].sem, k - 2)
                if SB_VISITS[k][0] == "feat":
                    last = feature_major(u % 2, HH, HL, (7,), m0=s)
                else:
                    last = token_major(u % 2, HH, HL, 7, 2, t0=2 * s)
                last.then_inc(*T["visit_done" if s else "sb_half"].up())

            def sb_scores(h):
                r = slice(64 * (h % 2), 64 * (h % 2) + 64)
                if h % 4 == 0:
                    pe.wait_ge(T["evac"].sem, EV["sb"] + 3 * (h // 4) + (2 if h else 3))
                if h >= 2:
                    pe.wait_ge(T["sb_exp"].sem, h - 1)
                for i in (0, 1, 3, 2):
                    last = pe.matmul(zs(h)[:, OFF[i]:OFF[i] + S - P * i], sbm["K"][r, h // 2, P * i:P * i + P], sbm["Q"][r, h // 2, P * i:S],
                                     start=i != 3, stop=True, skip_group_check=True)
                for i in range(TB):
                    last = pe.matmul(zs(h)[:, OFF[i]:OFF[i] + P], sbm["EYE"][:, :], sbm["MASK"][:, :], start=False, stop=True, skip_group_check=True)
                last.then_inc(*T["sb_z"].up())

            def sb_logs(h):
                pe.wait_ge(T["sb_sl"].sem, h + 1)
                for i in range(TB):
                    for j in range(i, TB):
                        w = S - P * j
                        o = OFF[i] + P * (j - i)
                        for part in ("SH", "SL"):
                            last = pe.matmul(zs(h)[:, o:o + w], sbm["TRI" if i == j else "NONE"][:, :], sbm[part][:, h % 2, OFF[j]:OFF[j] + w],
                                             start=False, stop=True, skip_group_check=True)
                last.then_inc(*T["sb_tri"].up())

            def sb_values(h):
                pe.wait_ge(T["sb_exp"].sem, h + 1)
                if h % 4 == 0:
                    pe.wait_ge(T["evac"].sem, EV["sb"] + 3 * (h // 4) + 3)
                if h >= 2 and h % 2 == 0:
                    pe.wait_ge(T["y_ready"].sem, 8 + h // 2)
                values(6, h, sbm["V"], lambda j: sbm["W"][:, h % 2, OFF[j]:OFF[j] + S - P * j], None).then_inc(*T["sb_o"].up())

            sb_scores(0)
            for h in range(SBH):
                halves = sb_halves(h)
                if h + 1 < SBH:
                    sb_scores(h + 1)
                for k, s in halves[:1]:
                    half(k, s)
                sb_logs(h)
                for k, s in halves[1:]:
                    half(k, s)
                if h >= 1:
                    sb_values(h - 1)
            sb_values(SBH - 1)
            pe.wait_ge(T["y_ready"].sem, 16)
            residual(RES["sb"], U_SBO, (8,), sby["YH"], sby["YL"], True)
            ffn(3)

            norm(N_NORM["norm1"])

            def visit(k):
                if k >= V_UP + 4:
                    pe.wait_ge(T["up_m"].sem, 2 if k == V_UP + 6 else 4)
                elif k == V_UP:
                    pe.wait_ge(T["ml_w"].sem, 2 * NH)
                elif k >= 4:
                    pe.wait_ge(T["evac"].sem, ev(k - 4 if k < V_RET else k - 1 if V_ML <= k < V_UP else k - 2))
                project(U_B2 + k, B2_VISITS[k][0], bank(k), 8 * N_NORM["norm1"] if k == 0 else None)

            for k in range(V_RET):
                if k == 4:
                    pe.wait_ge(T["css_acc"].sem, 8)
                    pe.wait_ge(T["evac"].sem, ev(2))
                    pe.matmul(PS[:, 4, 0:SC], ONES[:, :], SSC, start=True, stop=True).then_inc(*T["css_sum"].up())
                if k == 6:
                    pe.wait_ge(T["crms"].sem, 1)
                    pe.wait_ge(T["ch_ready"].sem, 8)
                visit(k)
            pe.wait_ge(T["evac"].sem, ev(V_RET - 1))
            pe.wait_ge(T["rope_done"].sem, 8)

            def ret_scores(h, j):
                if TB * h + j >= 2:
                    pe.wait_ge(T["rt_sm"].sem, TB * h + j - 1)
                pe.matmul(PS[:, j % 2, :], b2["RK"][:, h, P * j:P * j + P], b2["RQ"][:, h, :], start=True, stop=True).then_inc(*T["rt_s"].up())

            def ret_values(h, j):
                if j == 0 and h:
                    pe.wait_ge(T["rt_out"].sem, h)
                pe.wait_ge(T["rt_sm"].sem, TB * h + j + 1)
                pe.matmul(PS[:, 3, :], b2["RV"][:, j, P * h:P * h + P], rw["SM"][:, j, :], start=j == 0, stop=False)

            for h in range(NH):
                ret_scores(h, 0)
                ret_scores(h, 1)
                visit(V_RET + h)
                pe.wait_ge(T["rt_ks"].sem, h + 1)
                if h:
                    pe.wait_ge(T["rt_stc"].sem, h)
                for d in range(2):
                    for b in range(2):
                        last = pe.matmul(PS[:, 2, P * d:P * d + P], rw["KS"][:, 2 * d + b, :], b2["CRV"][:, b, P * h:P * h + P], start=b == 0, stop=b == 1)
                last.then_inc(*T["rt_st"].up())
                ret_values(h, 0)
                ret_scores(h, 2)
                ret_values(h, 1)
                ret_scores(h, 3)
                ret_values(h, 2)
                ret_values(h, 3)
                pe.wait_ge(T["rt_q"].sem, 2 * h + 2)
                pe.wait_ge(T["rt_stc"].sem, h + 1)
                for d in range(2):
                    last = pe.matmul(PS[:, 3, :], rw["ST"][:, d, :], rw["QF"][:, d, :], start=False, stop=d == 1)
                last.then_inc(*T["rt_o"].up())

            visit(V_PREP)
            pe.wait_ge(T["ml_rows"].sem, 1)
            pe.wait_ge(T["const_in"].sem, 16 * 13)
            for b in range(6):
                pe.transpose(PS[:, 0, 36 * b:36 * b + 36], gr["IG"][0:36, P * b:P * b + P], IDENT[0:36, 0:36])
            for k in range(2 * NH):
                e = 0 if k % 2 else SC - 1
                last = pe.matmul(PS[:, 1, k:k + 1], mw["SEL"][0:36, k, :], mw["GM"][0:36, e:e + 1], start=True, stop=True)
            last.then_inc(*T["ml_gt"].up())
            visit(V_PREP + 1)
            pe.wait_ge(T["ml_gc"].sem, 1)
            pe.wait_ge(T["rt_out"].sem, NH)
            for k in range(2 * NH):
                pe.wait_ge(T["ml_ks"].sem, k + 1)
                for part in range(2):
                    for b in range(2):
                        v = b2["CMV"][:, b, P * (k // 2):P * (k // 2) + P] if part == 0 else ONES[:, :]
                        o = 256 * (k % 2) + P * part
                        last = pe.matmul(PS[:, k // 2, o:o + P], mw["KS"][:, k % 2, b, :], v, start=b == 0, stop=b == 1)
                last.then_inc(*T["ml_c0"].up())
            def spread(k):
                if k:
                    pe.wait_ge(T["ml_w"].sem, k)
                pe.matmul(PS[:, 2, :], mw["SEL"][0:36, k, :], mw["GM"][0:36, SC:SC + S], start=True, stop=True)
                pe.matmul(PS[:, 3, :], mw["SEL"][0:36, k, :], mw["F"][0:36, SC:SC + S], start=True, stop=True).then_inc(*T["ml_g"].up())

            def ml_scores(h, j):
                if TB * h + j >= 2:
                    pe.wait_ge(T["ml_sm"].sem, TB * h + j - 1)
                pe.matmul(PS[:, j % 2, :], b2["MK"][:, h, P * j:P * j + P], b2["MQ"][:, h, :], start=True, stop=True).then_inc(*T["ml_s"].up())

            def ml_values(k):
                h, d = k // 2, k % 2
                if k:
                    pe.wait_ge(T["ml_den_read"].sem, k)
                pe.wait_ge(T["ml_den_in"].sem, k + 1)
                pe.matmul(PS[:, 5, :], ONES[:, :], DSUM, start=True, stop=True).then_inc(*T["ml_den"].up())
                pe.wait_ge(T["ml_sm"].sem, TB * (h + 1))
                pe.wait_ge(T["ml_qw"].sem, k + 1)
                if k:
                    pe.wait_ge(T["ml_h"].sem, k)
                order = range(TB) if d == 0 else range(TB - 1, -1, -1)
                for n, j in enumerate(order):
                    lo, hi = span(d, j)
                    pe.matmul(PS[:, 4, lo:hi], b2["MV"][:, j, P * h:P * h + P], WM[d][:, j, lo:hi], start=n == 0, stop=True, skip_group_check=n > 0)
                pe.matmul(PS[:, 4, :], C0N(k)[:, 0:P], mw["QW"][:, d, :], start=False, stop=True, skip_group_check=True)\
                    .then_inc(*T["ml_num"].up())

            def part(v, m, k0, k1):
                u = U_B2 + v
                if k0 + m == 0:
                    pe.wait_ge(T["evac"].sem, ev(v - (1 if v >= V_ML else 2)))
                    pe.wait_ge(T["w_lo"].sem, u + 1)
                return feature_major(u % 2, HH, HL, (6 + m,), k0=k0, n=k1 - k0, w0=k0, m0=m, start=k0 == 0, stop=k1 == KT)

            part(V_PREP + 2, 0, 0, KT)
            pe.wait_ge(T["ml_c0c"].sem, NH)
            spread(0)
            part(V_PREP + 2, 1, 0, KT).then_inc(*T["visit_done"].up())
            pe.wait_ge(T["evac"].sem, ev(V_ML - 1))
            ml_scores(0, 0)
            ml_scores(0, 1)
            for h in range(NH):
                spread(2 * h + 1)
                part(V_ML + h, 0, 0, KT)
                part(V_ML + h, 1, 0, 3)
                ml_scores(h, 2)
                ml_scores(h, 3)
                part(V_ML + h, 1, 3, 6)
                ml_values(2 * h)
                if h + 1 < NH:
                    spread(2 * h + 2)
                    ml_scores(h + 1, 0)
                    ml_scores(h + 1, 1)
                part(V_ML + h, 1, 6, KT).then_inc(*T["visit_done"].up())
                if h + 1 == NH:
                    visit(V_UP)
                ml_values(2 * h + 1)

            def head_sums(t0):
                for t in (t0, t0 + 1):
                    pe.wait_ge(T["hn_sq"].sem, t + 1)
                    if t >= 2:
                        pe.wait_ge(T["hn_rms"].sem, t - 1)
                    pe.matmul(PS[:, t % 2, :], ONES[:, :], SQT[:, t % 2, :], start=True, stop=True).then_inc(*T["hn_ss"].up())

            for p in range(3):
                visit(V_UP + p + 1)
                head_sums(2 * p)
            for i in range(2):
                if i:
                    for q in range(4):
                        visit(V_UP + 6 + q)
                pe.wait_ge(T["evac"].sem, ev(V_UP + 6 * i + 3))
                for s in range(2):
                    u = U_B2 + V_UP + 6 * i + 4 + s
                    pe.wait_ge(T["w_lo"].sem, u + 1)
                    pe.wait_ge(T["y_ready"].sem, 20 + 4 * s)
                    for c in (0, 2):
                        last = feature_major(u % 2, po["YH"], po["YL"], range(4 - 4 * s, 8 - 4 * s), k0=4 * s + c, n=2, w0=c, width=512,
                                             start=c == 0, stop=c == 2)
                        if i + s + c == 0:
                            head_sums(6)
                    last.then_inc(*T["visit_done"].up())
            pe.wait_ge(T["up_m"].sem, 6)
            residual(RES["b2"], U_B2O, (8,), po["MH"], po["ML"], False, tiles=T["m_ready"].sem)
            ffn(4)
            norm(N_NORM["final"])


def _tiles(w, cols):
    w = np.asarray(w)[:, cols]
    return w.reshape(w.shape[0] // P, P, w.shape[1]).transpose(1, 0, 2)


def _unit(w, cols):
    t = _tiles(w, cols)
    out = np.zeros((P, UNIT // UC, UC) if t.shape[2] <= UC else (P, UNIT // t.shape[2], t.shape[2]), np.float32)
    out[:, :t.shape[1], :t.shape[2]] = t
    return out.reshape(P, UNIT)


def _ffn_units(w_in, w_out):
    units = []
    for i in range(FT // 2):
        units += [_unit(w_in, slice(UC * i, UC * i + UC)), _unit(w_in, slice(FF + UC * i, FF + UC * i + UC))]
    for j in range(D // UC):
        at = 0
        for n in FFN_CHUNKS:
            units.append(_unit(w_out[at:at + P * n], slice(UC * j, UC * j + UC)))
            at += P * n
    return units


def _columns(w, lo, n):
    return [_unit(w, slice(lo + UC * i, lo + UC * i + UC)) for i in range(n // UC)]


def _placed(w, places):
    t = np.zeros((w.shape[0], UC), np.float32)
    for p, c in places:
        t[:, p] = w[:, c]
    return _unit(t, slice(0, UC))


def _col(v):
    return np.asarray(v).reshape(-1, P).T


def _constants():
    f = np.float32
    r = np.arange(P)
    t = np.arange(S)
    row, colm = (t // 64).astype(f), (t % 64).astype(f)
    inv = (10000.0 ** (-np.arange(32, dtype=np.float64) / 32)).astype(f)
    ang = np.concatenate([row[:, None] * inv, colm[:, None] * inv], -1).T.astype(np.float64)
    rope = np.stack([np.concatenate([np.cos(ang), np.cos(ang)]), np.concatenate([-np.sin(ang), np.sin(ang)])], 1)
    sel_fox = np.zeros((P, 8, P))
    for h in range(8):
        sel_fox[h, h] = -1
    sel_ml = np.zeros((P, 8, P))
    for k in range(8):
        sel_ml[32 * (k % 2) + k // 2, k] = -1
    s = np.arange(P)[:, None]
    cex = np.stack([255 - r, 127 - r, r, 128 + r], 1)
    return {k: np.ascontiguousarray(v, dtype=f) for k, v in {
        "c_ident": np.eye(P), "c_ones": np.ones((P, P)), "c_cex": cex,
        "c_b64": np.kron(np.eye(2), np.ones((64, 64))), "c_causal": np.where(r[None, :] <= s, 0.0, NEG), "c_sel_fox": sel_fox.reshape(P, 2, 512),
        "c_tri": np.where(s >= r[None, :], -1.0, 0.0), "c_negones": -np.ones((P, P)),
        "c_strict": np.where(s < r[None, :], 0.0, NEG), "c_rope": rope,
        "c_rel": (np.arange(896) - 384)[None, :] - s, "c_pos": np.broadcast_to(t + 1.0, (P, S)),
        "c_sel_ml": sel_ml, "c_msk_ml": np.stack([np.where(r[None, :] >= s, 0.0, NEG), np.where(r[None, :] <= s, 0.0, NEG)], 1),
    }.items()}


def _pack(a):
    g = {k: np.asarray(v) for k, v in a.items()}
    hy, b2, out = g["hy_w_in"][0], g["w_in_2"][0], {}
    out["w_ada"] = np.stack(_columns(g["w_ada_2"][0], 0, 6 * D))
    ffn = [_ffn_units(g["ffn_w_in"][l, k], g["ffn_w_out"][l, k]) for l in range(2) for k in range(2)]
    units = ffn[0] + _columns(hy, 0, 512) + _columns(hy, D, D) + _columns(hy, 512, 512)
    units += [_placed(hy, [(h, 2560 + h) for h in range(8)])] + _columns(hy, 2 * D, 512) + _columns(g["hy_w_out"][0], 0, D)
    units += ffn[1] + ffn[2] + [_unit(g["sb_w_qkv"][0], slice(D * n + UC * i, D * n + UC * i + UC)) for i in range(4) for n in range(3)] + _columns(g["sb_w_out"][0], 0, D) + ffn[3]
    part = lambda i: _columns(b2, 512 * i, 512)
    gates = [(32 * d + h, 4096 + 8 * d + h) for d in range(2) for h in range(4)]
    gates += [(P + 32 * d + h, 4096 + 8 * d + 4 + h) for d in range(2) for h in range(4)]
    gates = [_placed(b2, gates)]
    units += part(1) + part(2) + part(0) + part(1) + part(2) + part(5) + part(6) + gates + gates + part(5) + part(6) + part(4) + part(3) + part(7)
    for i in range(2):
        units += _columns(b2, 4112 + 512 * i, 512) + _columns(b2, 4112 + D + 512 * i, 512)
        units += [_unit(g[n][0], slice(512 * i, 512 * i + 512)) for n in ("w_ret_up_2", "w_ml_up_2")]
    units += _columns(g["w_out_2"][0], 0, D) + _ffn_units(g["w_ffn_in_2"][0], g["w_ffn_out_2"][0])
    assert len(units) == N_UNITS
    out["weights"] = np.stack(units)
    vec = np.zeros((P, NVEC), np.float32)

    def put(name, v):
        c, n = VCOLS[name]
        assert v.shape[1] == n
        vec[0:v.shape[0], c:c + n] = v

    for l in range(2):
        for k in range(2):
            put(f"ffn{2 * l + k}", _col(g["ffn_norm"][l, k]))
        put(f"mix{l}", _col(g["mix_norm"][l]))
    put("norm1", _col(g["norm1_gain_2"][0]))
    put("norm2", _col(g["norm2_gain_2"][0]))
    put("final", _col(g["final_gain_2"]))
    put("b_ada", _col(g["b_ada_2"][0]))
    put("conv_w", _col(g["rg_conv_w"][0]))
    put("conv_b", _col(g["rg_conv_b"][0]))
    put("gate_b", _col(g["rg_gate_b"][0]))
    put("soft", np.concatenate([_col(g["rg_lambda"][0]), np.broadcast_to(g["ret_decay_logit_2"][0].reshape(1, 8), (P, 8))], 1))
    put("qk", np.concatenate([g["fox_qk_norm"][0]] * 2, 1).T)
    put("fox_b", g["fox_fgate_b"][0][:, None])
    mb, b = g["mlstm_gate_bias_2"][0], np.zeros((36, 2), np.float32)
    for d in range(2):
        b[32 * d:32 * d + 4, 0], b[32 * d:32 * d + 4, 1] = mb[2 * d], mb[2 * d + 1]
    put("ml_b", b)
    put("cond", np.stack([_col(g["c_2"][0]), _col(g["c_ctx_2"])], 2).reshape(P, 16))
    out["vec"] = vec
    gw = g["rg_gate_w"][0]
    bd = np.zeros((P, 8, P), np.float32)
    for k in range(2):
        for m in range(4):
            for q in range(2):
                bd[64 * q:64 * q + 64, 4 * k + m, 64 * q:64 * q + 64] = gw[k, 2 * m + q]
    out["c_gates"] = bd
    out["x"] = _tiles(g["x"][0].T, slice(0, S))
    out["ctx"] = _tiles(g["ctx_2"][0].T, slice(0, SC))
    out.update(_constants())
    return {k: np.ascontiguousarray(v) for k, v in out.items()}


def kernel(**inputs):
    import concourse.bacc as _bacc
    from concourse.bass_utils import run_bass_kernel_spmd as _run

    nc = _bacc.Bacc("TRN2", target_bir_lowering=False, num_devices=1)
    arrays, A = {}, {}
    for name, a in _pack(inputs).items():
        arrays["in_" + name] = a
        A[name] = nc.dram_tensor("in_" + name, a.shape, F32, kind="ExternalInput").ap()
    A["out"] = nc.dram_tensor("out_t", (P, KT, S), F32, kind="ExternalOutput").ap()
    build(nc, A)
    got = _run(nc, [arrays], core_ids=[0]).results[0]["out_t"]
    return np.ascontiguousarray(got.transpose(2, 1, 0).reshape(1, S, D))
```
